# Optimizing a Trainium2 kernel written in Bass

```python
import math
import jax, jax.numpy as jnp
from jax import lax
import numpy as np

D_MODEL = 1024
BATCH = 1
SEQ = 256
DEPTH = 2

MEM_TOKENS = 256
GRID_W = 64
A_HEADS = 4
A_HEAD_DIM = D_MODEL // 8
A_WIDTH = A_HEADS * A_HEAD_DIM
A_CONV = 5
A_CHUNK = 128
B_HEADS = 8
B_HEAD_DIM = D_MODEL // 16
B_WIDTH = B_HEADS * B_HEAD_DIM
NA_ROWS = 8
NA_COLS = 16
C_HEADS = 8
C_HEAD_DIM = D_MODEL // 16
C_WIDTH = C_HEADS * 2 * C_HEAD_DIM
Q_BLOCK = 128
X_HEADS = 4
X_HEAD_DIM = D_MODEL // X_HEADS
FFN_HIDDEN = -(-8 * D_MODEL // (3 * 256)) * 256
ROPE_THETA = 10000.0
LN_EPS = 1e-5
DEEPNORM_ALPHA = (2 * DEPTH) ** 0.25
DEEPNORM_BETA = (8 * DEPTH) ** -0.25
N_EVEN = (DEPTH + 1) // 2
N_ODD = DEPTH // 2
EVEN_IN = 4 * A_WIDTH + 4 * A_HEADS + 3 * B_WIDTH
STATE_NEG = -1e30


def layer_norm(x, g, b):
    xf = x.astype(jnp.float32)
    mu = jnp.mean(xf, axis=-1, keepdims=True)
    var = jnp.mean(jnp.square(xf - mu), axis=-1, keepdims=True)
    return ((xf - mu) * lax.rsqrt(var + LN_EPS)).astype(x.dtype) * g + b

def rms_norm(x, g):
    xf = x.astype(jnp.float32)
    y = xf * lax.rsqrt(jnp.mean(jnp.square(xf), axis=-1, keepdims=True) + LN_EPS)
    return y.astype(x.dtype) * g

def split_cols(t, widths):
    offs = np.cumsum(widths)[:-1].tolist()
    return jnp.split(t, offs, axis=-1)

def centred_depthwise_conv(x, w):
    K, C = w.shape
    return lax.conv_general_dilated(
        x, w.reshape(K, 1, C).astype(x.dtype), window_strides=(1,),
        padding=[(K // 2, K // 2)], dimension_numbers=('NWC', 'WIO', 'NWC'),
        feature_group_count=C)

def rope(t):
    S, d = t.shape[1], t.shape[-1]
    inv_freq = ROPE_THETA ** (-jnp.arange(0, d, 2, dtype=jnp.float32) / d)
    ang = jnp.arange(S, dtype=jnp.float32)[:, None] * inv_freq[None, :]
    cos = jnp.cos(ang)[:, None, :]
    sin = jnp.sin(ang)[:, None, :]
    tf = t.astype(jnp.float32)
    t1, t2 = tf[..., : d // 2], tf[..., d // 2:]
    return jnp.concatenate([t1 * cos - t2 * sin, t1 * sin + t2 * cos], axis=-1).astype(t.dtype)

def mlstm_chunkwise(q, k, v, log_i, log_f):
    N, H, S, d = q.shape
    L = min(A_CHUNK, S)
    NC = S // L
    qc = q.reshape(N, H, NC, L, d)
    kc = k.reshape(N, H, NC, L, d)
    vc = v.reshape(N, H, NC, L, d)
    ai = log_i.reshape(N, H, NC, L)
    b = jnp.cumsum(log_f.reshape(N, H, NC, L), axis=-1)
    g = b[..., -1]
    w_end = g[..., None] - b + ai
    m_loc = jnp.max(w_end, axis=-1)
    p = jnp.exp(w_end - m_loc[..., None])
    kv_loc = jnp.einsum('nhcl,nhcld,nhcle->nhcde', p, kc, vc)
    k_loc = jnp.einsum('nhcl,nhcld->nhcd', p, kc)

    def step(carry, inp):
        C, nv, m = carry
        g_c, m_c, kv_c, k_c = inp
        m_new = jnp.maximum(g_c + m, m_c)
        s_old = jnp.exp(g_c + m - m_new)
        s_new = jnp.exp(m_c - m_new)
        C_new = s_old[..., None, None] * C + s_new[..., None, None] * kv_c
        n_new = s_old[..., None] * nv + s_new[..., None] * k_c
        return (C_new, n_new, m_new), (C, nv, m)

    init = (jnp.zeros((N, H, d, d), jnp.float32), jnp.zeros((N, H, d), jnp.float32),
            jnp.full((N, H), STATE_NEG, jnp.float32))
    xs = (jnp.moveaxis(g, 2, 0), jnp.moveaxis(m_loc, 2, 0),
          jnp.moveaxis(kv_loc, 2, 0), jnp.moveaxis(k_loc, 2, 0))
    _, (C_in, n_in, m_in) = lax.scan(step, init, xs)
    C_in = jnp.moveaxis(C_in, 0, 2)
    n_in = jnp.moveaxis(n_in, 0, 2)
    m_in = jnp.moveaxis(m_in, 0, 2)
    upto = jnp.tril(jnp.ones((L, L), dtype=bool))
    D = jnp.where(upto, b[..., :, None] - b[..., None, :] + ai[..., None, :], -jnp.inf)
    m_inter = b + m_in[..., None]
    m = jnp.maximum(jnp.max(D, axis=-1), m_inter)
    Smat = jnp.einsum('nhcld,nhcsd->nhcls', qc, kc) * jnp.exp(D - m[..., None])
    s_inter = jnp.exp(m_inter - m)
    num = (jnp.einsum('nhcls,nhcse->nhcle', Smat, vc)
           + s_inter[..., None] * jnp.einsum('nhcld,nhcde->nhcle', qc, C_in))
    den = jnp.sum(Smat, axis=-1) + s_inter * jnp.einsum('nhcld,nhcd->nhcl', qc, n_in)
    h = num / jnp.maximum(jnp.abs(den), jnp.exp(-m))[..., None]
    return h.reshape(N, H, S, d)

def neighbourhood_attention(q, k, v, rpb):
    B_, S, H, d = q.shape
    R = S // GRID_W
    kr = min(NA_ROWS, R)
    q = q.reshape(B_, R, GRID_W, H, d) * (d ** -0.5)
    k = k.reshape(B_, R, GRID_W, H, d)
    v = v.reshape(B_, R, GRID_W, H, d)
    rows = jnp.arange(R)
    row_start = jnp.clip(rows - NA_ROWS // 2, 0, R - kr)
    key_rows = row_start[:, None] + jnp.arange(kr)[None, :]
    k_blk = k[:, key_rows]
    v_blk = v[:, key_rows]
    cols = jnp.arange(GRID_W)
    col_start = jnp.clip(cols - NA_COLS // 2, 0, GRID_W - NA_COLS)
    in_win = (cols[None, :] >= col_start[:, None]) & (cols[None, :] < col_start[:, None] + NA_COLS)
    rel_r = key_rows - rows[:, None] + (NA_ROWS - 1)
    rel_c = jnp.clip(cols[None, :] - cols[:, None] + (NA_COLS - 1), 0, 2 * NA_COLS - 2)
    bias = rpb[:, rel_r[:, None, :, None], rel_c[None, :, None, :]]
    s = jnp.einsum('brqhd,brikhd->bhrqik', q, k_blk).astype(jnp.float32) + bias.astype(jnp.float32)
    s = jnp.where(in_win[:, None, :], s, -jnp.inf)
    p = jax.nn.softmax(s.reshape(B_, H, R, GRID_W, kr * GRID_W), axis=-1)
    p = p.reshape(B_, H, R, GRID_W, kr, GRID_W).astype(v.dtype)
    out = jnp.einsum('bhrqik,brikhd->brqhd', p, v_blk)
    return out.reshape(B_, S, H * d)

def diff_attention(q, k, v, lam):
    B_, S, H, _, d = q.shape
    nb = S // Q_BLOCK
    qb = jnp.moveaxis(q.reshape(B_, nb, Q_BLOCK, H, 2, d), 1, 0)
    scale = d ** -0.5

    def block(qi):
        s = jnp.einsum('bqhcd,bkhcd->bhcqk', qi, k).astype(jnp.float32) * scale
        p = jax.nn.softmax(s, axis=-1)
        a = p[:, :, 0] - lam * p[:, :, 1]
        return jnp.einsum('bhqk,bkhe->bqhe', a.astype(v.dtype), v)

    out = lax.map(block, qb)
    return jnp.moveaxis(out, 0, 1).reshape(B_, S, H, 2 * d)

def memory_cross_attention(x, mem, wq, wkv, wo):
    B_, S, _ = x.shape
    M = mem.shape[1]
    q = (x @ wq).reshape(B_, S, X_HEADS, X_HEAD_DIM) * (X_HEAD_DIM ** -0.5)
    k, v = jnp.split(mem @ wkv, 2, axis=-1)
    k = k.reshape(B_, M, X_HEADS, X_HEAD_DIM)
    v = v.reshape(B_, M, X_HEADS, X_HEAD_DIM)
    p = jax.nn.softmax(jnp.einsum('bshd,bmhd->bhsm', q, k).astype(jnp.float32), axis=-1)
    o = jnp.einsum('bhsm,bmhd->bshd', p.astype(v.dtype), v)
    return o.reshape(B_, S, D_MODEL) @ wo

def swiglu(x, w_gu, w_down):
    gate, up = jnp.split(x @ w_gu, 2, axis=-1)
    return (jax.nn.silu(gate) * up) @ w_down

def even_mixer(x, w_in, gate_b, conv_w, rpb, w_out):
    B_, S, _ = x.shape
    a_qk, a_v, a_o, a_g, b_q, b_k, b_v = split_cols(
        x @ w_in, [2 * A_WIDTH, A_WIDTH, A_WIDTH, 4 * A_HEADS, B_WIDTH, B_WIDTH, B_WIDTH])
    a_qk = jax.nn.silu(centred_depthwise_conv(a_qk, conv_w))
    a_q, a_k = jnp.split(a_qk, 2, axis=-1)

    def heads(t):
        return t.reshape(B_, S, A_HEADS, A_HEAD_DIM).transpose(0, 2, 1, 3).astype(jnp.float32)

    q, k, v = heads(a_q), heads(a_k) * (A_HEAD_DIM ** -0.5), heads(a_v)
    gates = (a_g.astype(jnp.float32) + gate_b.astype(jnp.float32)).reshape(B_, S, 4, A_HEADS).transpose(2, 0, 3, 1)

    def both_dirs(t):
        return jnp.concatenate([t, jnp.flip(t, axis=2)], axis=0)

    log_i = jnp.concatenate([gates[0], jnp.flip(gates[1], axis=-1)], axis=0)
    log_f = jax.nn.log_sigmoid(jnp.concatenate([gates[2], jnp.flip(gates[3], axis=-1)], axis=0))
    h2 = mlstm_chunkwise(both_dirs(q), both_dirs(k), both_dirs(v), log_i, log_f)
    h = h2[:B_] + jnp.flip(h2[B_:], axis=2)
    h = h.transpose(0, 2, 1, 3).reshape(B_, S, A_WIDTH).astype(x.dtype)
    a_out = jax.nn.sigmoid(a_o) * h
    b_out = neighbourhood_attention(b_q.reshape(B_, S, B_HEADS, B_HEAD_DIM),
                                    b_k.reshape(B_, S, B_HEADS, B_HEAD_DIM),
                                    b_v.reshape(B_, S, B_HEADS, B_HEAD_DIM), rpb)
    return jnp.concatenate([a_out, b_out], axis=-1) @ w_out

def odd_mixer(x, w_in, lam_p, subln_g, w_out, lam_init):
    B_, S, _ = x.shape
    q, k, v = jnp.split(x @ w_in, 3, axis=-1)
    q = rope(q.reshape(B_, S, 2 * C_HEADS, C_HEAD_DIM)).reshape(B_, S, C_HEADS, 2, C_HEAD_DIM)
    k = rope(k.reshape(B_, S, 2 * C_HEADS, C_HEAD_DIM)).reshape(B_, S, C_HEADS, 2, C_HEAD_DIM)
    v = v.reshape(B_, S, C_HEADS, 2 * C_HEAD_DIM)
    lp = lam_p.astype(jnp.float32)
    lam = jnp.exp(jnp.sum(lp[0] * lp[1])) - jnp.exp(jnp.sum(lp[2] * lp[3])) + lam_init
    o = diff_attention(q, k, v, lam)
    o = rms_norm(o, subln_g) * (1.0 - lam_init)
    return o.reshape(B_, S, C_WIDTH) @ w_out

def first_inputs(seed: int = 0) -> dict:
    key = jax.random.key(seed)
    ks = jax.random.split(key, 20)

    def nrm(kk, shape, scale):
        return jax.random.normal(kk, shape, jnp.float32) * scale

    x = nrm(ks[0], (BATCH, SEQ, D_MODEL), 1.0)
    mem = nrm(ks[1], (BATCH, MEM_TOKENS, D_MODEL), 1.0)
    even_w_in = nrm(ks[2], (N_EVEN, D_MODEL, EVEN_IN), D_MODEL ** -0.5)
    i_bias = nrm(ks[3], (N_EVEN, 2 * A_HEADS), 0.1)
    f_lin = jnp.linspace(3.0, 6.0, A_HEADS, dtype=jnp.float32)
    f_bias = jnp.concatenate([f_lin, f_lin])[None, :] + nrm(ks[4], (N_EVEN, 2 * A_HEADS), 0.1)
    even_gate_b = jnp.concatenate([i_bias, f_bias], axis=-1)
    even_conv_w = nrm(ks[5], (N_EVEN, A_CONV, 2 * A_WIDTH), A_CONV ** -0.5)
    even_rpb = nrm(ks[6], (N_EVEN, B_HEADS, 2 * NA_ROWS - 1, 2 * NA_COLS - 1), 0.02)
    even_w_out = nrm(ks[7], (N_EVEN, A_WIDTH + B_WIDTH, D_MODEL), (A_WIDTH + B_WIDTH) ** -0.5 * DEEPNORM_BETA)
    odd_w_in = nrm(ks[8], (N_ODD, D_MODEL, 3 * C_WIDTH), D_MODEL ** -0.5)
    odd_lambda = nrm(ks[9], (N_ODD, 4, C_HEAD_DIM), 0.1)
    odd_subln_g = 1.0 + nrm(ks[10], (N_ODD, 2 * C_HEAD_DIM), 0.02)
    odd_w_out = nrm(ks[11], (N_ODD, C_WIDTH, D_MODEL), C_WIDTH ** -0.5 * DEEPNORM_BETA)
    mem_wq = nrm(ks[12], (DEPTH, D_MODEL, D_MODEL), D_MODEL ** -0.5)
    mem_wkv = nrm(ks[13], (DEPTH, D_MODEL, 2 * D_MODEL), D_MODEL ** -0.5)
    mem_wo = nrm(ks[14], (DEPTH, D_MODEL, D_MODEL), D_MODEL ** -0.5 * DEEPNORM_BETA)
    ffn_w_gu = nrm(ks[15], (DEPTH, D_MODEL, 2 * FFN_HIDDEN), D_MODEL ** -0.5)
    ffn_w_down = nrm(ks[16], (DEPTH, FFN_HIDDEN, D_MODEL), FFN_HIDDEN ** -0.5 * DEEPNORM_BETA)
    ln_g = 1.0 + nrm(ks[17], (DEPTH, 3, D_MODEL), 0.02)
    ln_b = nrm(ks[18], (DEPTH, 3, D_MODEL), 0.02)
    return {'x': x, 'mem': mem, 'even_w_in': even_w_in, 'even_gate_b': even_gate_b,
            'even_conv_w': even_conv_w, 'even_rpb': even_rpb, 'even_w_out': even_w_out,
            'odd_w_in': odd_w_in, 'odd_lambda': odd_lambda, 'odd_subln_g': odd_subln_g,
            'odd_w_out': odd_w_out, 'mem_wq': mem_wq, 'mem_wkv': mem_wkv, 'mem_wo': mem_wo,
            'ffn_w_gu': ffn_w_gu, 'ffn_w_down': ffn_w_down, 'ln_g': ln_g, 'ln_b': ln_b}

def first_block(x, mem, even_w_in, even_gate_b, even_conv_w, even_rpb, even_w_out,
              odd_w_in, odd_lambda, odd_subln_g, odd_w_out, mem_wq, mem_wkv, mem_wo,
              ffn_w_gu, ffn_w_down, ln_g, ln_b):
    for layer in range(DEPTH):
        j = layer // 2
        if layer % 2 == 0:
            mix = even_mixer(x, even_w_in[j], even_gate_b[j], even_conv_w[j], even_rpb[j], even_w_out[j])
        else:
            lam_init = 0.8 - 0.6 * math.exp(-0.3 * layer)
            mix = odd_mixer(x, odd_w_in[j], odd_lambda[j], odd_subln_g[j], odd_w_out[j], lam_init)
        x = layer_norm(DEEPNORM_ALPHA * x + mix, ln_g[layer, 0], ln_b[layer, 0])
        xa = memory_cross_attention(x, mem, mem_wq[layer], mem_wkv[layer], mem_wo[layer])
        x = layer_norm(DEEPNORM_ALPHA * x + xa, ln_g[layer, 1], ln_b[layer, 1])
        ff = swiglu(x, ffn_w_gu[layer], ffn_w_down[layer])
        x = layer_norm(DEEPNORM_ALPHA * x + ff, ln_g[layer, 2], ln_b[layer, 2])
    return x


CTX_LEN = 256
HEAD_DIM = 64
GROUP_W = D_MODEL // 4
N_HEADS = GROUP_W // HEAD_DIM
N_KV_HEADS = N_HEADS // 2
GQ = N_HEADS // N_KV_HEADS
KV_W = N_KV_HEADS * HEAD_DIM
IN_W = 5 * GROUP_W + 2 * (GROUP_W + 2 * KV_W)
SHORT_CONV = 3
CONF_CONV = 31
WINDOW = 128
N_EXPERTS = 16
EXPERT_FF = D_MODEL
CAPACITY_FACTOR = 2
EPS = 1e-6


def rms_norm_2(x, g):
    xf = x.astype(jnp.float32)
    y = xf * lax.rsqrt(jnp.mean(xf * xf, axis=-1, keepdims=True) + EPS)
    return (y * g.astype(jnp.float32)).astype(x.dtype)

def layer_norm_2(x, g, b):
    xf = x.astype(jnp.float32)
    mu = jnp.mean(xf, axis=-1, keepdims=True)
    var = jnp.mean(jnp.square(xf - mu), axis=-1, keepdims=True)
    y = (xf - mu) * lax.rsqrt(var + EPS)
    return (y * g.astype(jnp.float32) + b.astype(jnp.float32)).astype(x.dtype)

def dwconv(x, w):
    k = w.shape[0]
    return lax.conv_general_dilated(x, w[:, None, :].astype(x.dtype), (1,), [(k // 2, k // 2)],
                                    dimension_numbers=('NWC', 'WIO', 'NWC'),
                                    feature_group_count=x.shape[-1])

def split_proj(p):
    sizes = (GROUP_W,) * 5 + (GROUP_W, KV_W, KV_W) * 2
    return jnp.split(p, np.cumsum(sizes)[:-1].tolist(), axis=-1)

def q_heads(t):
    return t.reshape(*t.shape[:-1], N_KV_HEADS, GQ, HEAD_DIM)

def kv_heads(t):
    return t.reshape(*t.shape[:-1], N_KV_HEADS, HEAD_DIM)

def short_conv_mixer(b, c, h, w):
    return b * dwconv(c * h, w)

def conformer_conv(a, g, w, bias, ln_g, ln_b):
    u = a * jax.nn.sigmoid(g)
    u = dwconv(u, w) + bias
    return jax.nn.silu(layer_norm_2(u, ln_g, ln_b))

def rope_tables(s):
    rows = s // GRID_W
    row = jnp.repeat(jnp.arange(rows), GRID_W).astype(jnp.float32)
    col = (jnp.arange(rows * GRID_W) % GRID_W).astype(jnp.float32)
    quarter = HEAD_DIM // 4
    inv = ROPE_THETA ** (-jnp.arange(quarter, dtype=jnp.float32) / quarter)
    ar = row[:, None] * inv
    ac = col[:, None] * inv
    ang = jnp.concatenate([ar, ar, ac, ac], axis=-1)
    return jnp.cos(ang), jnp.sin(ang)

def apply_rope(x, cos, sin):
    bshape = (cos.shape[0],) + (1,) * (x.ndim - 3) + (HEAD_DIM,)
    c = cos.reshape(bshape).astype(x.dtype)
    s = sin.reshape(bshape).astype(x.dtype)
    xs = x.reshape(*x.shape[:-1], 2, 2, HEAD_DIM // 4)
    rot = jnp.stack([-xs[..., 1, :], xs[..., 0, :]], axis=-2).reshape(x.shape)
    return x * c + rot * s

def gqa_attend(q, k, v, sink=None):
    s = jnp.einsum('bqkgd,bjkd->bkgqj', q, k).astype(jnp.float32) * (HEAD_DIM ** -0.5)
    if sink is not None:
        sl = jnp.broadcast_to(sink.reshape(N_KV_HEADS, GQ)[None, :, :, None, None].astype(jnp.float32),
                              s.shape[:-1] + (1,))
        s = jnp.concatenate([s, sl], axis=-1)
    p = jax.nn.softmax(s, axis=-1)
    if sink is not None:
        p = p[..., :-1]
    return jnp.einsum('bkgqj,bjkd->bqkgd', p.astype(v.dtype), v)

def window_attention(q, k, v, kc, vc, sink):
    bsz, s = q.shape[:2]
    nb = s // Q_BLOCK
    qb = q.reshape(bsz, nb, Q_BLOCK, N_KV_HEADS, GQ, HEAD_DIM)

    def bands(t):
        tp = jnp.pad(t, ((0, 0), (Q_BLOCK, Q_BLOCK), (0, 0), (0, 0)))
        tp = tp.reshape(bsz, nb + 2, Q_BLOCK, N_KV_HEADS, HEAD_DIM)
        return jnp.concatenate([tp[:, :-2], tp[:, 1:-1], tp[:, 2:]], axis=2)

    kw, vw = bands(k), bands(v)
    scale = HEAD_DIM ** -0.5
    s_loc = jnp.einsum('bnqkgd,bnjkd->bnkgqj', qb, kw).astype(jnp.float32) * scale
    s_ctx = jnp.einsum('bnqkgd,bckd->bnkgqc', qb, kc).astype(jnp.float32) * scale
    blk = jnp.arange(nb)[:, None, None] * Q_BLOCK
    qpos = blk + jnp.arange(Q_BLOCK)[None, :, None]
    kpos = blk - Q_BLOCK + jnp.arange(3 * Q_BLOCK)[None, None, :]
    valid = (kpos >= 0) & (kpos < s) & (jnp.abs(qpos - kpos) <= WINDOW)
    s_loc = jnp.where(valid[None, :, None, None], s_loc, -jnp.inf)
    sl = jnp.broadcast_to(sink.reshape(N_KV_HEADS, GQ)[None, None, :, :, None, None].astype(jnp.float32),
                          s_loc.shape[:-1] + (1,))
    p = jax.nn.softmax(jnp.concatenate([s_loc, s_ctx, sl], axis=-1), axis=-1)
    n_loc = 3 * Q_BLOCK
    p_loc = p[..., :n_loc].astype(v.dtype)
    p_ctx = p[..., n_loc:n_loc + kc.shape[1]].astype(v.dtype)
    o = (jnp.einsum('bnkgqj,bnjkd->bnqkgd', p_loc, vw)
         + jnp.einsum('bnkgqc,bckd->bnqkgd', p_ctx, vc))
    return o.reshape(bsz, s, GROUP_W)

def global_attention(q, k, v, kc, vc):
    bsz, s = q.shape[:2]
    nb = s // Q_BLOCK
    kall = jnp.concatenate([k, kc], axis=1)
    vall = jnp.concatenate([v, vc], axis=1)
    qb = jnp.moveaxis(q.reshape(bsz, nb, Q_BLOCK, N_KV_HEADS, GQ, HEAD_DIM), 1, 0)
    o = lax.map(lambda qblk: gqa_attend(qblk, kall, vall), qb)
    return jnp.moveaxis(o, 0, 1).reshape(bsz, s, GROUP_W)

def expert_choice_ffn(h, router, w_gate, w_up, w_down):
    bsz, t, d = h.shape
    cap = CAPACITY_FACTOR * t // N_EXPERTS
    aff = jax.nn.softmax((h @ router).astype(jnp.float32), axis=-1)
    gates, idx = lax.top_k(jnp.swapaxes(aff, 1, 2), cap)
    xs = jax.vmap(lambda hb, ib: hb[ib])(h, idx)
    a = jnp.einsum('becd,edf->becf', xs, w_gate)
    u = jnp.einsum('becd,edf->becf', xs, w_up)
    y = jnp.einsum('becf,efd->becd', jax.nn.silu(a) * u, w_down)
    y = y * gates[..., None].astype(y.dtype)
    return jax.vmap(lambda ib, yb: jnp.zeros((t, d), yb.dtype).at[ib.reshape(-1)].add(yb.reshape(-1, d)))(idx, y)

def layer(x, xc, mods, cmods, n1, n2, w_in, conv_a, conv_b, conv_b_bias, cln_g, cln_b, sink,
          qn_g, kn_g, w_out, router, w_gate, w_up, w_down, cos, sin, need_ctx):
    sh1, sc1, g1, sh2, sc2, g2 = [m[:, None] for m in jnp.split(mods, 6, axis=-1)]
    csh1, csc1, cg1, csh2, csc2, cg2 = [m[:, None] for m in jnp.split(cmods, 6, axis=-1)]
    bsz, s = x.shape[:2]
    lc = xc.shape[1]

    h = rms_norm_2(x, n1) * (1 + sc1) + sh1
    hc = rms_norm_2(xc, n1) * (1 + csc1) + csh1
    a_b, a_c, a_h, b_v, b_g, c_q, c_k, c_v, d_q, d_k, d_v = split_proj(h @ w_in)
    ca_b, ca_c, ca_h, cb_v, cb_g, cc_q, cc_k, cc_v, cd_q, cd_k, cd_v = split_proj(hc @ w_in)

    kc_c, vc_c = kv_heads(cc_k), kv_heads(cc_v)
    kc_d, vc_d = rms_norm_2(kv_heads(cd_k), kn_g), kv_heads(cd_v)

    ya = short_conv_mixer(a_b, a_c, a_h, conv_a)
    yb = conformer_conv(b_v, b_g, conv_b, conv_b_bias, cln_g, cln_b)
    yc = window_attention(apply_rope(q_heads(c_q), cos, sin), apply_rope(kv_heads(c_k), cos, sin),
                          kv_heads(c_v), kc_c, vc_c, sink)
    yd = global_attention(apply_rope(rms_norm_2(q_heads(d_q), qn_g), cos, sin),
                          apply_rope(rms_norm_2(kv_heads(d_k), kn_g), cos, sin),
                          kv_heads(d_v), kc_d, vc_d)
    x_new = x + g1 * (jnp.concatenate([ya, yb, yc, yd], axis=-1) @ w_out)
    h2 = rms_norm_2(x_new, n2) * (1 + sc2) + sh2
    x_new = x_new + g2 * expert_choice_ffn(h2, router, w_gate, w_up, w_down)

    if need_ctx:
        yca = short_conv_mixer(ca_b, ca_c, ca_h, conv_a)
        ycb = conformer_conv(cb_v, cb_g, conv_b, conv_b_bias, cln_g, cln_b)
        ycc = gqa_attend(q_heads(cc_q), kc_c, vc_c, sink).reshape(bsz, lc, GROUP_W)
        ycd = gqa_attend(rms_norm_2(q_heads(cd_q), qn_g), kc_d, vc_d).reshape(bsz, lc, GROUP_W)
        xc = xc + cg1 * (jnp.concatenate([yca, ycb, ycc, ycd], axis=-1) @ w_out)
        hc2 = rms_norm_2(xc, n2) * (1 + csc2) + csh2
        xc = xc + cg2 * expert_choice_ffn(hc2, router, w_gate, w_up, w_down)
    return x_new, xc

def second_inputs(seed: int = 0) -> dict:
    key = jax.random.key(seed)
    ks = jax.random.split(key, 24)
    f32 = jnp.float32
    nrm = lambda k, shape, scale: jax.random.normal(k, shape, f32) * scale
    d = D_MODEL
    return {
        "x": nrm(ks[0], (BATCH, SEQ, d), 1.0),
        "c": nrm(ks[1], (BATCH, d), 1.0),
        "ctx": nrm(ks[2], (BATCH, CTX_LEN, d), 1.0),
        "c_ctx": nrm(ks[3], (d,), 1.0),
        "ada_w": nrm(ks[4], (DEPTH, d, 6 * d), 0.5 * d ** -0.5),
        "ada_b": nrm(ks[5], (DEPTH, 6 * d), 0.01),
        "norm1_g": 1.0 + nrm(ks[6], (DEPTH, d), 0.01),
        "norm2_g": 1.0 + nrm(ks[7], (DEPTH, d), 0.01),
        "w_in": nrm(ks[8], (DEPTH, d, IN_W), d ** -0.5),
        "conv_a_w": nrm(ks[9], (DEPTH, SHORT_CONV, GROUP_W), SHORT_CONV ** -0.5),
        "conv_b_w": nrm(ks[10], (DEPTH, CONF_CONV, GROUP_W), CONF_CONV ** -0.5),
        "conv_b_b": nrm(ks[11], (DEPTH, GROUP_W), 0.01),
        "conv_ln_g": 1.0 + nrm(ks[12], (DEPTH, GROUP_W), 0.01),
        "conv_ln_b": nrm(ks[13], (DEPTH, GROUP_W), 0.01),
        "sink": nrm(ks[14], (DEPTH, N_HEADS), 1.0),
        "q_norm_g": 1.0 + nrm(ks[15], (DEPTH, HEAD_DIM), 0.01),
        "k_norm_g": 1.0 + nrm(ks[16], (DEPTH, HEAD_DIM), 0.01),
        "w_out": nrm(ks[17], (DEPTH, d, d), d ** -0.5),
        "router_w": nrm(ks[18], (DEPTH, d, N_EXPERTS), d ** -0.5),
        "w_gate": nrm(ks[19], (DEPTH, N_EXPERTS, d, EXPERT_FF), d ** -0.5),
        "w_up": nrm(ks[20], (DEPTH, N_EXPERTS, d, EXPERT_FF), d ** -0.5),
        "w_down": nrm(ks[21], (DEPTH, N_EXPERTS, EXPERT_FF, d), EXPERT_FF ** -0.5),
        "final_g": 1.0 + nrm(ks[22], (d,), 0.01),
    }

def second_block(x, c, ctx, c_ctx, ada_w, ada_b, norm1_g, norm2_g, w_in, conv_a_w, conv_b_w, conv_b_b,
              conv_ln_g, conv_ln_b, sink, q_norm_g, k_norm_g, w_out, router_w, w_gate, w_up, w_down,
              final_g):
    cos, sin = rope_tables(x.shape[1])
    sc = jax.nn.silu(c)
    scc = jax.nn.silu(c_ctx)[None]
    xc = ctx
    for i in range(DEPTH):
        mods = sc @ ada_w[i] + ada_b[i]
        cmods = scc @ ada_w[i] + ada_b[i]
        x, xc = layer(x, xc, mods, cmods, norm1_g[i], norm2_g[i], w_in[i], conv_a_w[i], conv_b_w[i],
                      conv_b_b[i], conv_ln_g[i], conv_ln_b[i], sink[i], q_norm_g[i], k_norm_g[i],
                      w_out[i], router_w[i], w_gate[i], w_up[i], w_down[i], cos, sin,
                      i < DEPTH - 1)
    return rms_norm_2(x, final_g)


def setup_inputs(seed=0):
    out = dict(first_inputs(seed))
    for name, value in second_inputs(seed + 1).items():
        if name != "x":
            out[name + "_2"] = value
    return out


def reference(
    x, mem, even_w_in, even_gate_b, even_conv_w, even_rpb, even_w_out, odd_w_in, odd_lambda,
    odd_subln_g, odd_w_out, mem_wq, mem_wkv, mem_wo, ffn_w_gu, ffn_w_down, ln_g, ln_b, c_2,
    ctx_2, c_ctx_2, ada_w_2, ada_b_2, norm1_g_2, norm2_g_2, w_in_2, conv_a_w_2, conv_b_w_2,
    conv_b_b_2, conv_ln_g_2, conv_ln_b_2, sink_2, q_norm_g_2, k_norm_g_2, w_out_2, router_w_2,
    w_gate_2, w_up_2, w_down_2, final_g_2,
):
    x = first_block(
        x, mem, even_w_in, even_gate_b, even_conv_w, even_rpb, even_w_out, odd_w_in, odd_lambda,
        odd_subln_g, odd_w_out, mem_wq, mem_wkv, mem_wo, ffn_w_gu, ffn_w_down, ln_g, ln_b,
    )
    return second_block(
        x, c_2, ctx_2, c_ctx_2, ada_w_2, ada_b_2, norm1_g_2, norm2_g_2, w_in_2, conv_a_w_2,
        conv_b_w_2, conv_b_b_2, conv_ln_g_2, conv_ln_b_2, sink_2, q_norm_g_2, k_norm_g_2,
        w_out_2, router_w_2, w_gate_2, w_up_2, w_down_2, final_g_2,
    )


_drawn_inputs = setup_inputs


def setup_inputs(seed=0):
    import zlib

    import numpy as np

    out = dict(_drawn_inputs(seed))
    spreads = {}
    factors = {'even_rpb': 8.0,
     'odd_lambda': 7.376,
     'odd_subln_g': 7.491,
     'ada_b_2': 3.68,
     'norm1_g_2': 8.0,
     'norm2_g_2': 45.183,
     'conv_b_b_2': 64.0,
     'conv_ln_g_2': 200.0,
     'conv_ln_b_2': 200.0,
     'sink_2': 8.0,
     'q_norm_g_2': 189.024,
     'k_norm_g_2': 64.0,
     'final_g_2': 200.0,
     'conv_b_w_2': 3.478}
    for name, (base, spread) in spreads.items():
        noise = np.random.default_rng([zlib.crc32(name.encode()), seed]).standard_normal(out[name].shape)
        drawn = base * np.exp(spread * noise) if base else spread * noise
        out[name] = __import__('jax').numpy.asarray(drawn.astype(out[name].dtype))
    for name, factor in factors.items():
        out[name] = (out[name] * factor).astype(out[name].dtype)
    return out
```

```python
import math
from contextlib import ExitStack

import numpy as np

import concourse.bass as bass
from concourse import mybir

F32 = mybir.dt.float32
ALU = mybir.AluOpType
ACT = mybir.ActivationFunctionType
AX = mybir.AxisListType

P = 128
D = 1024
KC = D // P
SEQ = 256
T2 = SEQ // P
DEPTH = 2
A_HEADS, A_CONV = 4, 5
A_W = 512
B_HEADS, B_W = 8, 512
GRID_W, NA_ROWS, NA_COLS = 64, 8, 16
ROWS = SEQ // GRID_W
C_HEADS = 8
X_HEADS, X_HD = 4, 256
FFN = 2816
FC = FFN // P
ALPHA = (2 * DEPTH) ** 0.25
LN_EPS = 1e-5
LAM_INIT = 0.8 - 0.6 * math.exp(-0.3)
NEG = -1e30
EPS = 1e-6
HD = 64
N_HEADS = 4
NE = 16
CAP = 32
CONV_B = 31
PAD_B = CONV_B // 2
IN_W = 2304
UK, UN = 4, 512
RING = 12

COLS = {}
_at = 0
for _name, _n in (("conv", 40), ("subln", 1), ("n1", 16), ("n2", 16), ("cc", 16), ("conv_a", 12),
                  ("conv_b", 124), ("conv_bb", 4), ("cln_g", 4), ("cln_b", 4), ("qn", 2), ("kn", 2), ("ada_b", 96)):
    COLS[_name] = (_at, _n)
    _at += _n
NCOLS = _at
CONSTS = {}
_at = 0
for _name, _n in (("ident", 128), ("rot32", 128), ("rot16", 128), ("blk64", 128), ("ones", 128), ("cos1", 256),
                  ("sin1", 256), ("cos2", 256), ("sin2", 256), ("mlmask", 1024), ("winmask", 512),
                  ("namask", 64), ("iota", 32), ("sel4", 512)):
    CONSTS[_name] = (_at, _n)
    _at += _n
NCONST = _at

EVENTS = ("const_in", "param_in", "x_in", "mem_in", "ctx_in", "nab_in", "ln_row_in", "final_row_in", "xT", "proj",
          "var", "rstd", "x_ready", "x2", "conv", "silu", "gate_abs", "gate_exp", "gate_ln1", "gate_ln",
          "gate_rows", "gate_cols", "decay", "decay_exp", "nmax", "probs", "probs_exp",
          "probsT", "oT", "rope_out", "sq", "rms", "hid", "lam_in", "lam_sums", "lam_exps", "zero", "ssq", "sc_silu",
          "mods_rows", "mods", "diag", "gates_bc", "u_in", "uconv", "u_norm", "yb", "xhat", "hT", "aff_exp",
          "aff", "top", "out_dma", "ab_in", "logit_max", "router_in", "gbc_free", "u_in2", "uvar", "ssq2")


def weight_plan(w):
    units = []

    def block(key, mat, n0, n1, kc=KC):
        m = mat.rearrange("(c p) n -> p c n", p=P)
        for h in range(0, kc, UK):
            units.append((key + (h // UK,), m[:, h:min(h + UK, kc), n0:n1]))

    def matrix(key, mat, kc=KC):
        n = mat.shape[1]
        for b in range(0, n, UN):
            block(key + (b // UN,), mat, b, min(b + UN, n), kc)

    e = w["even_w_in"][0]
    for b, n0 in enumerate((0, 512, 1024, 1536, 2064, 2576, 3088)):
        block(("even_in", b), e, n0, n0 + 512)
    matrix(("even_out",), w["even_w_out"][0])
    for layer in range(DEPTH):
        if layer == 1:
            matrix(("odd_in",), w["odd_w_in"][0])
            matrix(("odd_out",), w["odd_w_out"][0])
        matrix(("mem_kv", layer), w["mem_wkv"][layer])
        matrix(("mem_q", layer), w["mem_wq"][layer])
        matrix(("mem_o", layer), w["mem_wo"][layer])
        for b in range(0, FFN, UN):
            n = min(UN, FFN - b)
            block(("gate", layer, b // UN), w["ffn_w_gu"][layer], b, b + n)
            block(("up", layer, b // UN), w["ffn_w_gu"][layer], FFN + b, FFN + b + n)
        matrix(("down", layer), w["ffn_w_down"][layer], FC)
    for layer in range(DEPTH):
        ada = w["ada_w_2"][layer].rearrange("(c p) n -> p c n", p=P)
        for g in range(3):
            for h in range(2):
                for j in range(4):
                    b = 4 * g + j
                    units.append((("ada", layer, g, h, j), ada[:, UK * h:UK * h + UK, UN * b:UN * b + UN]))
        matrix(("in2", layer), w["w_in_2"][layer])
        matrix(("out2", layer), w["w_out_2"][layer])
        units.append((("experts", layer), None))
    return units


def experts_per_group(layer):
    return 2 if layer == 0 else 4


def moe_units(layer):
    g = experts_per_group(layer)
    order = []
    for b in range(2):
        for name in ("w_gate_2", "w_up_2"):
            order += [(name, b, h, j) for h in range(2) for j in range(g)]
    for b in range(2):
        order += [("w_down_2", b, h, j) for h in range(2) for j in range(g)]
    return order


class Marks:

    def __init__(self, table):
        self.table, self.seen, self.count = table, {}, {}

    def mark(self, kind, key, n=1):
        self.count[kind] = self.count.get(kind, 0) + n
        assert (kind, key) not in self.seen, (kind, key)
        self.seen[(kind, key)] = self.count[kind]

    def value(self, kind, key):
        return 1 if self.table is None else self.table[(kind, key)]


def build(nc, w, out, table, stop=None):
    marks = Marks(table)
    units = weight_plan(w)
    unit_at, n = {}, 0
    for key, _ in units:
        unit_at[key] = n
        n += 1 if key[0] != "experts" else len(moe_units(key[1])) * (NE // experts_per_group(key[1]))

    with ExitStack() as ctx:
        def sb(name, shape):
            return ctx.enter_context(nc.sbuf_tensor(name, shape, F32))

        def sem(name):
            return ctx.enter_context(nc.semaphore(name))

        ring = sb("ring", [P, RING, UK, UN])
        const = sb("const", [P, NCONST])
        cols = sb("cols", [P, NCOLS])
        router = sb("router", [P, DEPTH, KC, NE])
        gate_b = sb("gate_b", [4, 4])
        sink = sb("sink", [P, DEPTH, N_HEADS])
        x = sb("x", [P, 4, D])
        xT = sb("xT", [P, KC, 2 * SEQ])
        arena = sb("arena", [P, 15488])
        stats = sb("stats", [P, 4, 2, 6])
        mv = sb("mv", [P, 4, 2])
        std = sb("std", [P, 4])
        rstd = sb("rstd", [P, 4])
        small = sb("small", [P, 2, 16])
        lam = sb("lam", [P, 8])
        modsT = sb("modsT", [P, 48, 2])
        aff = sb("aff", [P, 4, NE])
        posT = sb("posT", [P, 4, NE])
        bank = [ctx.enter_context(nc.psum_tensor(f"bank{i}", [P, 512], F32)) for i in range(8)]

        def con(name):
            at, n = CONSTS[name]
            return const[:, at:at + n]

        def col(name, i=0, n=1):
            return cols[:, COLS[name][0] + i:COLS[name][0] + i + n]

        def area(at, *shape):
            n = int(np.prod(shape))
            v = arena[:, at:at + n]
            if len(shape) == 1:
                return v
            names = "abcd"[:len(shape)]
            return v.rearrange(f"p ({' '.join(names)}) -> p {' '.join(names)}", **dict(zip(names, shape)))

        ident = con("ident")
        decay = [area(1024, 2, 2, 256), area(3072, 2, 2, 256)]
        nab = area(4096, T2, B_HEADS, 256)
        ln_row = area(4096, 2, D)
        qk_pad = area(8192, 8, SEQ + 4)
        b_qkT = area(8192, 8, SEQ)
        qkT = area(10272, 8, SEQ)
        a_v = area(12320, T2, 512)
        a_oT = area(13344, 4, SEQ)
        b_v = area(14368, T2, 512)
        y1T = x[:, 2:4, :].rearrange("p a (b c) -> p (a b) c", c=SEQ)
        mem_rows = x[:, 2:4, :]
        qT = area(8192, 8, SEQ)
        kT = area(10240, 8, SEQ)
        v_rows = area(12288, T2, D)
        raw = area(14336, 2, SEQ)
        rcos = area(14848, 2, SEQ)
        hT = area(8192, FC, SEQ)
        hsilu = area(13824, 2, 512)
        g2, g3 = (x[0:4, t, :].rearrange("p (s k) -> p s k", k=SEQ) for t in (2, 3))
        g_in, g_forget, g_c, g_tmp = g2[:, 0:2], g2[:, 2:4], g3[:, 0:2], g3[:, 2:4]
        g_max = area(0, 4, SEQ)[0:4]
        lam_raw = area(6144, 4, 64)
        dvar = area(6144, C_HEADS, SEQ)
        gate_w = area(2304, KC, 16)
        g_one = area(2048, SEQ)[0:4]

        gcols = sb("gcols", [P, 2, 2, 2, 4])

        g_row = area(4096, 2, D)
        y_lo = area(6144, 4, 2 * SEQ)
        y_hi = xT[:, 4:8, :]
        qk = area(8192, 8, 2 * SEQ)
        xhat = area(8192, 4, D)
        v2 = area(12288, 4, 2, P)
        z_pad = area(13312, 2, 2, SEQ + 2)
        u_pad = area(14344, 2, 2, SEQ + 2 * PAD_B)
        u_rows = area(13312, 4, SEQ)
        sq = area(0, 2, 2 * SEQ)
        qvar = area(1024, 2, 2 * SEQ)
        rtmp = area(2048, 2, SEQ)
        btmp = area(2048, 2, 512)
        mods_rows = area(0, 3, 512)
        scT = area(1536, KC, 32)
        diag = area(2048, KC, P)
        sig = area(3072, 2, 2 * SEQ)
        gain = sb("gain", [P, 2, KC, 2])
        lmax = sb("lmax", [P, 2, 4])
        top8 = sb("top8", [NE, 8])
        affT, left, picked, ones_row = (area(512 * i, 2 * SEQ)[0:NE] for i in range(4))
        moe_x, moe_tmp = area(0, KC, P), area(1024, KC, P)
        moe_h, moe_hT = area(2048, D), area(3072, KC, P)
        moe_y, moe_g = area(6144, D), area(7168, 4 * P)
        moe_pick, moe_pick_g = area(7680, 4, P), area(12288, 4, P)
        moe_silu = area(12800, 2, 512)
        acc = xT[:, :, :].rearrange("p a (b c) -> p (a b) c", c=512)

        def shift(k):
            return modsT[:, 24 * k:24 * k + 8, :]

        LO, HI = 0, 1
        S = {k: sem(k) for k in EVENTS}
        MOE = ("pick", "xg_full", "xt", "g_full", "g_sb", "blocks", "halves", "silu", "hid", "ht_full", "ht_sb", "y_sb",
               "sum_full", "sum_free", "one", "one2", "loads")
        M = [{k: sem(f"moe{layer}_{k}") for k in MOE} for layer in range(DEPTH)]
        bank_full = [sem(f"bank_full{i}") for i in range(8)]
        bank_free = [sem(f"bank_free{i}") for i in range(8)]
        ring_in = [sem(f"ring_in{i}") for i in range(RING)]
        dve_step = sem("dve_step")
        act_step = sem("act_step")
        pool_step = sem("pool_step")

        def signal(kind, key, n=1):
            marks.mark(kind, key, n)
            return S[kind], n

        def after(kind, key):
            return S[kind], marks.value(kind, key)

        fills, filled = {}, [0] * 8
        last_fill, last_reader = [None], {}

        def full(key):
            b, n = fills[key]
            return bank_full[b], n

        def freed(key):
            return bank_free[fills[key][0]], 1

        def bank_of(key):
            return bank[fills[key][0]]

        block = ctx.enter_context(nc.Block())

        def unit(stage, i, q, k, scale, v, y, keys=256, bias=None, sink_at=None):
            return dict(key=(stage, i), n=i, q=q, k=k, scale=scale, v=v, y=y, keys=keys, bias=bias, sink=sink_at)

        def half(t, c, j, n0=0, n=SEQ):
            return t[64 * j:64 * j + 64, c, n0:n0 + n]

        na_units = [unit("na", h, [half(b_qkT, h // 2, h % 2)], [[half(b_qkT, 4 + h // 2, h % 2)]], 64 ** -0.5,
                         [b_v[:, kb, 64 * h:64 * h + 64] for kb in range(2)],
                         [(y1T[64 * (h % 2):64 * (h % 2) + 64, 4 + h // 2, :], 64 * (h % 2))],
                         bias=nab[:, :, h, :]) for h in range(B_HEADS)]

        def probs_of(u):
            return area(u["n"] % 2 * 2 * u["keys"], 2, u["keys"])

        def probsT_of(u):
            return area(2048 + u["n"] % 2 * 2 * u["keys"], u["keys"] // P, 256)

        ml_units = [unit("ml", h, None, None, P ** -0.5, [a_v[:, kb, P * h:P * h + P] for kb in range(2)],
                         [(y1T[:, h, :], 0)]) for h in range(A_HEADS)]
        diff_units = [unit("diff", h, None, None, 64 ** -0.5, [v_rows[:, kb, P * h:P * h + P] for kb in range(2)],
                           [(y1T[:, h, :], 0)]) for h in range(C_HEADS)]

        def diff_probs(u, m):
            return area(1024 * m + 512 * (u["n"] % 2), 2, SEQ)

        def block2_units(layer):
            us = []
            for s in range(2 if layer == 0 else 1):
                for kind, name in enumerate(("win", "glob")):
                    for h in range(N_HEADS):
                        kv = h // 2
                        tok = [0, SEQ] if s == 0 else [SEQ]
                        us.append(unit(f"{name}{layer}{s}", h, [half(qk, 4 * kind + h // 2, h % 2, SEQ * s)],
                                       [[half(qk, 4 * kind + 2 + kv, h % 2, t)] for t in tok], HD ** -0.5,
                                       [v2[:, t // P + i, kind, 64 * kv:64 * kv + 64] for t in tok for i in range(2)],
                                       [(y_hi[64 * (h % 2):64 * (h % 2) + 64, 2 * kind + h // 2, SEQ * s:SEQ * s + SEQ], 64 * (h % 2))],
                                       keys=256 * len(tok), bias=con("winmask").rearrange("p (t k) -> p t k", t=2)
                                       if (kind, s) == (0, 0) else None, sink_at=sink[:, layer, h:h + 1] if kind == 0 else None))
            return us

        def by_stage(us):
            names = []
            for u in us:
                if u["key"][0] not in names:
                    names.append(u["key"][0])
            return [[u for u in us if u["key"][0] == n] for n in names]

        CHUNKS = dict(ab0=0, ab1=128, ac0=256, ac1=384, ah0=512, ah1=640, bv0=768, bv1=896, bg0=1024, bg1=1152,
                      cq0=1280, cq1=1408, dq0=1792, dq1=1920)
        KV_COLS = dict(ck=1536, cv=1664, dk=2048, dv=2176)
        QK_AT = dict(cq0=0, cq1=1, ck0=2, ck1=3, dq0=4, dq1=5, dk0=6, dk1=7)

        def mem_units(layer):
            return [unit(f"mem{layer}", h, [qT[:, 2 * h, :], qT[:, 2 * h + 1, :]],
                         [[kT[:, 2 * h, :], kT[:, 2 * h + 1, :]]], X_HD ** -0.5,
                         [v_rows[:, kb, X_HD * h:X_HD * h + X_HD] for kb in range(2)],
                         [(y1T[:, 2 * h, :], 0), (y1T[:, 2 * h + 1, :], 0)]) for h in range(X_HEADS)]

        @block.tensor
        def _(pe):
            def open_bank(key, b):
                fills[key] = (b, filled[b] + 1)
                if filled[b]:
                    pe.wait_ge(bank_free[b], filled[b])
                filled[b] += 1
                return bank[b]

            dense = [0]

            def dense_bank(key):
                dense[0] += 1
                return open_bank(key, dense[0] % 4)

            def weights(key):
                u = unit_at[key]
                pe.wait_ge(ring_in[u % RING], 16 * (u // RING + 1))
                return ring[:, u % RING]

            def w_block(key, kc=KC):
                halves = [weights(key + (h,)) for h in range(-(-kc // UK))]
                return lambda c: halves[c // UK][:, c % UK]

            def filled_now(key):
                last_fill[0] = fills[key]
                return bank_full[fills[key][0]], 1

            def read(key, n):
                for h in range(n):
                    last_reader[unit_at[key + (h,)]] = last_fill[0]

            def project_T(key, src, n_tok, width=512):
                wb = w_block(key)
                per = 512 // n_tok
                for j in range(width // P // per):
                    b = dense_bank(key + ("out", j))
                    for m in range(per):
                        c0 = (per * j + m) * P
                        for c in range(KC):
                            mm = pe.matmul(b[:, n_tok * m:n_tok * m + n_tok], wb(c)[:, c0:c0 + P], src(c),
                                           start=(c == 0), stop=(c == KC - 1))
                    mm.then_inc(*filled_now(key + ("out", j)))
                read(key, 2)

            def project_rows(key, src, tiles, kc=KC):
                wb = w_block(key, kc)
                for t in tiles:
                    b = dense_bank(key + ("out", t))
                    for c in range(kc):
                        mm = pe.matmul(b[:, :], src(c, t), wb(c), start=(c == 0), stop=(c == kc - 1))
                    mm.then_inc(*filled_now(key + ("out", t)))
                read(key, -(-kc // UK))

            def to_T(key, rows, tiles):
                for t in tiles:
                    for h in range(2):
                        b = dense_bank(key + (t, h))
                        for c in range(4):
                            mm = pe.transpose(b[:, P * c:P * c + P], rows(t)[:, (4 * h + c) * P:(4 * h + c + 1) * P], ident)
                        mm.then_inc(*filled_now(key + (t, h)))

            def x_chunks(c):
                return xT[:, c, 0:SEQ]

            def m_chunks(c):
                return xT[:, c, SEQ:2 * SEQ]

            def x_tile(c, t):
                return xT[:, c, t * P:t * P + P]

            def scores(u):
                parts = 1 if u["keys"] == 256 else 2
                for part in range(parts):
                    b = open_bank(("s",) + u["key"] + (part,), 4 + (u["n"] + part) % 2 if parts == 1 else 4 + part)
                    for t in (range(2) if parts == 1 else [part]):
                        for kb in range(len(u["k"])):
                            at = 256 * (t if parts == 1 else kb)
                            nk = len(u["k"][kb])
                            for c in range(nk):
                                mm = pe.matmul(b[:, at:at + 256], u["q"][c][:, t * P:t * P + P], u["k"][kb][c],
                                               start=(c == 0), stop=(c == nk - 1))
                    mm.then_inc(bank_full[fills[("s",) + u["key"] + (part,)][0]], 1)

            def turn(u):
                pe.wait_ge(*after("probs", u["key"]))
                pr = probs_of(u)
                for part in range(u["keys"] // 256):
                    key = ("pT",) + u["key"] + (part,)
                    b = open_bank(key, 6)
                    for kb in range(2):
                        for t in range(2):
                            mm = pe.transpose(b[:, 256 * kb + P * t:256 * kb + P * t + P],
                                              pr[:, t, (2 * part + kb) * P:(2 * part + kb + 1) * P], ident)
                    mm.then_inc(bank_full[6], 1)

            def values(u):
                pe.wait_ge(*after("probsT", u["key"]))
                b = open_bank(("o",) + u["key"], 7)
                n = u["keys"] // P
                for i, (_, p0) in enumerate(u["y"]):
                    dv = 64 if u["y"][i][0].shape[0] == 64 else P
                    for kb in range(n):
                        mm = pe.matmul(b[p0:p0 + dv, 256 * i:256 * i + 256], u["v"][kb][:, i * dv:(i + 1) * dv],
                                       probsT_of(u)[:, kb, :], start=(kb == 0), stop=(kb == n - 1))
                mm.then_inc(bank_full[7], 1)

            def attend(us, score=scores):
                for i in range(len(us) + 2):
                    if i < len(us):
                        score(us[i])
                    if 0 <= i - 1 < len(us):
                        turn(us[i - 1])
                    if 0 <= i - 2:
                        values(us[i - 2])

            pe.wait_ge(*after("const_in", "const"))
            pe.wait_ge(*after("param_in", "all"))
            pe.wait_ge(*after("x_in", 0))
            to_T(("xT", "in"), lambda t: x[:, t, :], range(T2))
            pe.wait_ge(*after("mem_in", 0))
            to_T(("memT",), lambda t: mem_rows[:, t, :], range(T2))
            pe.wait_ge(*after("xT", ("in", T2 - 1, 1)))

            for b in (0, 1):
                project_T(("even_in", b), x_chunks, SEQ)
            for kind in range(2):
                g = dense_bank(("gates", kind))
                for d in range(2):
                    for c in range(KC):
                        mm = pe.matmul(g[0:4, 256 * d:256 * d + 256], gate_w[:, c, 8 * kind + 4 * d:8 * kind + 4 * d + 4],
                                       x_chunks(c), start=(c == 0), stop=(c == KC - 1))
                mm.then_inc(bank_full[fills[("gates", kind)][0]], 1)
            project_rows(("even_in", 2), x_tile, range(T2))
            project_T(("even_in", 3), x_chunks, SEQ)
            pe.wait_ge(*after("gate_rows", 0))
            g = open_bank(("gate_cols",), 7)
            for kind in range(2):
                for d in range(2):
                    for t in range(2):
                        at = 4 * (4 * kind + 2 * d + t)
                        mm = pe.transpose(g[:, at:at + 4], g_max[:, 2 * kind + d, t * P:t * P + P], ident[0:4, 0:4])
            mm.then_inc(bank_full[7], 1)
            project_T(("even_in", 4), x_chunks, SEQ)
            project_T(("even_in", 5), x_chunks, SEQ)
            project_rows(("even_in", 6), x_tile, range(T2))

            for h in range(A_HEADS):
                b = open_bank(("cb", h), 6)
                for d in range(2):
                    mm = pe.matmul(b[:, 256 * d:256 * d + 256], con("sel4")[0:4, P * h:P * h + P], g_c[:, d, :],
                                   start=True, stop=True)
                mm.then_inc(bank_full[6], 1)
                if h == 0:
                    pe.wait_ge(*after("silu", 7))
                b = open_bank(("s", "ml", h, 0), 4 + h % 2)
                for t in range(2):
                    mm = pe.matmul(b[:, 256 * t:256 * t + 256], qkT[:, h, t * P:t * P + P], qkT[:, 4 + h, :], start=True, stop=True)
                mm.then_inc(bank_full[4 + h % 2], 1)
                if h:
                    turn(ml_units[h - 1])
                    values(ml_units[h - 1])
            turn(ml_units[-1])
            pe.wait_ge(*after("proj", ("even_in", 6, "out", 1)))
            values(ml_units[-1])
            attend(na_units)
            pe.wait_ge(*after("oT", ("na", B_HEADS - 1)))

            def out_proj(key, kc=KC, src=None):
                for nb in range(2):
                    project_rows(key + (nb,), src or (lambda c, t: y1T[:, c, t * P:t * P + P]), range(T2), kc)

            def norm_T(i):
                for t in range(T2):
                    pe.wait_ge(*after("x_ready", (i, t)))
                    to_T(("xT", i), lambda t: x[:, t, :], [t])

            out_proj(("even_out",))
            for layer in range(DEPTH):
                if layer == 1:
                    pe.wait_ge(*after("xT", (2, T2 - 1, 1)))
                    for b in range(4):
                        project_T(("odd_in", b), x_chunks, SEQ)
                        for j in range(2):
                            for m in range(2):
                                c = 4 * b + 2 * j + m
                                pe.wait_ge(*after("proj", ("raw", c)))
                                r = open_bank(("rot", c), 4 + c % 2)
                                pe.matmul(r[:, 0:SEQ], con("rot32"), raw[:, c % 2, :], start=True, stop=True)\
                                  .then_inc(bank_full[4 + c % 2], 1)
                    for b in (4, 5):
                        project_rows(("odd_in", b), x_tile, range(T2))
                    pe.wait_ge(*after("rope_out", 15))
                    pe.wait_ge(*after("proj", ("odd_in", 5, "out", 1)))

                    def diff_scores(u):
                        for m in range(2):
                            h = u["n"]
                            b = open_bank(("s",) + u["key"] + (m,), 4 + m)
                            for t in range(2):
                                mm = pe.matmul(b[:, 256 * t:256 * t + 256], half(qT, h, m)[:, t * P:t * P + P],
                                               half(kT, h, m), start=True, stop=True)
                            mm.then_inc(bank_full[4 + m], 1)

                    def diff_values(u):
                        values(u)
                        pe.wait_ge(*after("ssq", u["n"]))
                        b = open_bank(("ss", u["n"]), 7)
                        pe.matmul(b[:, 0:SEQ], con("ones"), raw[:, u["n"] % 2, :], start=True, stop=True)\
                          .then_inc(bank_full[7], 1)
                    for i in range(C_HEADS + 2):
                        if i < C_HEADS:
                            diff_scores(diff_units[i])
                        if 0 <= i - 1 < C_HEADS:
                            turn(diff_units[i - 1])
                        if 0 <= i - 2:
                            diff_values(diff_units[i - 2])
                    pe.wait_ge(*after("oT", ("diff", C_HEADS - 1)))
                    out_proj(("odd_out",))
                n0 = 3 * layer
                if layer == 0:
                    pe.wait_ge(*after("xT", ("mem", T2 - 1, 1)))
                for b in range(2):
                    project_T(("mem_kv", layer, b), m_chunks, SEQ)
                for b in range(2, 4):
                    project_rows(("mem_kv", layer, b), lambda c, t: xT[:, c, SEQ + t * P:SEQ + t * P + P], range(T2))
                norm_T(n0)
                pe.wait_ge(*after("xT", (n0, T2 - 1, 1)))
                for b in range(2):
                    project_T(("mem_q", layer, b), x_chunks, SEQ)
                pe.wait_ge(*after("proj", ("mem_q", layer, 1, "out", 1)))
                attend(mem_units(layer))
                pe.wait_ge(*after("oT", (f"mem{layer}", X_HEADS - 1)))
                out_proj(("mem_o", layer))
                norm_T(n0 + 1)
                pe.wait_ge(*after("xT", (n0 + 1, T2 - 1, 1)))
                for b in range(-(-FFN // UN)):
                    width = min(UN, FFN - b * UN)
                    project_T(("gate", layer, b), x_chunks, SEQ, width)
                    project_T(("up", layer, b), x_chunks, SEQ, width)
                pe.wait_ge(*after("hid", (layer, FC // 2 - 1)))
                out_proj(("down", layer), FC, lambda c, t: hT[:, c, t * P:t * P + P])
                if layer == 0:
                    norm_T(n0 + 2)

            if stop:
                return
            for layer in range(DEPTH):
                seqs = 2 if layer == 0 else 1
                n_tok = SEQ * seqs
                tiles = range(2 * seqs)
                pe.wait_ge(*after("sc_silu", layer))
                for g in range(3):
                    b = dense_bank(("ada", layer, g))
                    for h in range(2):
                        ws = [weights(("ada", layer, g, h, j)) for j in range(4)]
                        for k in range(UK):
                            for j in range(4):
                                mm = pe.matmul(b[32 * j:32 * j + 32, :], scT[:, UK * h + k, :], ws[j][:, k],
                                               start=(h == 0 and k == 0), stop=(h == 1 and k == UK - 1))
                    mm.then_inc(*filled_now(("ada", layer, g)))
                    for j in range(4):
                        for h in range(2):
                            last_reader[unit_at[("ada", layer, g, h, j)]] = last_fill[0]
                for g in range(3):
                    pe.wait_ge(*after("mods_rows", (layer, g)))
                    b = dense_bank(("modsT", layer, g))
                    for q in range(4):
                        mm = pe.transpose(b[:, P * q:P * q + P], mods_rows[:, g, P * q:P * q + P], ident)
                    mm.then_inc(*filled_now(("modsT", layer, g)))

                def gate_rows_of(kind):
                    for s in range(seqs):
                        pe.wait_ge(*after("diag", (layer, kind, s)))
                        for h in range(2):
                            b = dense_bank(("gbc", layer, kind, s, h))
                            pe.matmul(b[:, :], con("ones"), diag[:, 4 * h:4 * h + 4, :].rearrange("p a b -> p (a b)"),
                                      start=True, stop=True).then_inc(*filled_now(("gbc", layer, kind, s, h)))

                def hidden_T(kind, ts):
                    for t in ts:
                        pe.wait_ge(*after("xhat", (layer, kind, t)))
                    for c in range(KC):
                        b = dense_bank(("h", layer, kind, c))
                        for t in ts:
                            mm = pe.transpose(b[:, P * t:P * t + P], xhat[:, t, P * c:P * c + P], ident)
                        mm.then_inc(*filled_now(("h", layer, kind, c)))

                gate_rows_of(0)
                hidden_T(0, range(4))
                pe.wait_ge(*after("hT", (layer, 0, KC - 1)))

                def chunk(name, wb, at):
                    b = dense_bank(("c", layer, name))
                    for c in range(KC):
                        mm = pe.matmul(b[:, 0:n_tok], wb(c)[:, at:at + P], xT[:, c, 0:n_tok], start=(c == 0), stop=(c == KC - 1))
                    mm.then_inc(*filled_now(("c", layer, name)))

                def keys(name, wb, at):
                    for kv in range(2):
                        b = dense_bank(("c", layer, f"{name}{kv}"))
                        for i in range(2):
                            for c in range(KC):
                                mm = pe.matmul(b[64 * i:64 * i + 64, :], wb(c)[:, at + 64 * kv:at + 64 * kv + 64], xT[:, c, :],
                                               start=(c == 0), stop=(c == KC - 1))
                        mm.then_inc(*filled_now(("c", layer, f"{name}{kv}")))

                def values2(name, wb, at):
                    b = dense_bank(("c", layer, name))
                    for t in range(4):
                        for c in range(KC):
                            mm = pe.matmul(b[:, P * t:P * t + P], xT[:, c, P * t:P * t + P], wb(c)[:, at:at + P],
                                           start=(c == 0), stop=(c == KC - 1))
                    mm.then_inc(*filled_now(("c", layer, name)))

                for blk in range(-(-IN_W // UN)):
                    wb = w_block(("in2", layer, blk))
                    for name, at in [*CHUNKS.items()]:
                        if at // UN == blk:
                            chunk(name, wb, at % UN)
                    if blk == 3:
                        keys("ck", wb, KV_COLS["ck"] % UN)
                        values2("cv", wb, KV_COLS["cv"] % UN)
                    if blk == 4:
                        keys("dk", wb, KV_COLS["dk"] % UN)
                        values2("dv", wb, KV_COLS["dv"] % UN)
                    read(("in2", layer, blk), 2)
                for i, name in enumerate(("dq0", "dq1", "dk0", "dk1")):
                    n = n_tok if name[1] == "q" else 2 * SEQ
                    pe.wait_ge(*after("sq", (layer, name)))
                    b = open_bank(("qss", layer, name), 4 + i % 2)
                    pe.matmul(b[:, 0:n], con("blk64"), sq[:, i % 2, 0:n], start=True, stop=True).then_inc(*filled_now(("qss", layer, name)))
                for i, name in enumerate(QK_AT):
                    if name[0] == "c":
                        pe.wait_ge(*after("proj", ("qk", layer, name)))
                    else:
                        pe.wait_ge(*after("rms", ("qk", layer, name)))
                    b = open_bank(("rot2", layer, name), 6 + i % 2)
                    pe.matmul(b[:, 0:SEQ], con("rot16"), qk[:, QK_AT[name], 0:SEQ], start=True, stop=True)\
                      .then_inc(*filled_now(("rot2", layer, name)))
                for c in range(2):
                    pe.wait_ge(*after("uconv", (layer, c)))
                for tp in range(seqs):
                    b = dense_bank(("u", layer, tp))
                    for t in range(2):
                        for c in range(2):
                            mm = pe.transpose(b[:, 256 * t + P * c:256 * t + P * c + P],
                                              y_lo[:, 2 + c, (2 * tp + t) * P:(2 * tp + t + 1) * P], ident)
                    mm.then_inc(*filled_now(("u", layer, tp)))
                pe.wait_ge(*after("u_norm", (layer, seqs - 1)))
                for c in range(2):
                    b = dense_bank(("ub", layer, c))
                    for t in tiles:
                        mm = pe.transpose(b[:, P * t:P * t + P], u_rows[:, t, P * c:P * c + P], ident)
                    mm.then_inc(*filled_now(("ub", layer, c)))
                pe.wait_ge(*after("rope_out", ("qk", layer, "dk1")))
                pe.wait_ge(*after("proj", ("v2", layer, "dv")))
                for us in by_stage(block2_units(layer)):
                    attend(us)
                    pe.wait_ge(*after("oT", us[-1]["key"]))
                pe.wait_ge(*after("yb", (layer, 1)))
                for nb in range(2):
                    project_rows(("out2", layer, nb), lambda c, t: (y_lo[:, c, t * P:t * P + P] if c < 4 else y_hi[:, c - 4, t * P:t * P + P]), tiles)
                gate_rows_of(1)
                hidden_T(1, tiles)
                pe.wait_ge(*after("hT", (layer, 1, KC - 1)))
                b = dense_bank(("logits", layer))
                for t in tiles:
                    for c in range(KC):
                        mm = pe.matmul(b[:, NE * t:NE * t + NE], xT[:, c, P * t:P * t + P], router[:, layer, c, :], start=(c == 0), stop=(c == KC - 1))
                mm.then_inc(*filled_now(("logits", layer)))
                pe.wait_ge(*after("aff", layer))
                b = dense_bank(("affT", layer))
                for t in tiles:
                    mm = pe.transpose(b[0:NE, P * t:P * t + P], aff[:, t, :], ident)
                mm.then_inc(*filled_now(("affT", layer)))
                pe.wait_ge(*after("top", layer))
                b = dense_bank(("posT", layer))
                for t in tiles:
                    mm = pe.transpose(b[:, NE * t:NE * t + NE], picked[:, P * t:P * t + P], ident[0:NE, 0:NE])
                mm.then_inc(*filled_now(("posT", layer)))

                m, G, order = M[layer], experts_per_group(layer), moe_units(layer)
                W = P // G
                u0, U = unit_at[("experts", layer)], len(order)
                n_sum = 2 * len(tiles)
                for b8 in range(8):
                    if filled[b8]:
                        pe.wait_ge(bank_free[b8], filled[b8])
                with pe.Fori(0, NE // G) as i:
                    pe.wait_ge(m["pick"], i + 1)
                    for h in range(2):
                        pe.wait_ge(m["y_sb"], 2 * i + 1 + h)
                        for c in range(4):
                            for n, t in enumerate(tiles):
                                mm = pe.matmul(bank[4 + h][:, P * c:P * c + P], xhat[:, t, P * (4 * h + c):P * (4 * h + c) + P],
                                               moe_pick[:, t, :], start=(n == 0), stop=(n == len(tiles) - 1))
                        mm.then_inc(m["xg_full"], 1)
                    pe.wait_ge(m["sum_free"], n_sum * i + n_sum)
                    for t in tiles:
                        mm = pe.transpose(bank[6][:, P * t:P * t + P], moe_pick_g[:, t, :], ident)
                    mm.then_inc(m["g_full"], 1)
                    pe.wait_ge(m["xt"], i + 1)

                    def product(bi, dst, src):
                        for h in range(2):
                            for j in range(G):
                                k = (2 * bi + h) * G + j
                                pe.wait_ge(ring_in[(u0 + k) % RING], i * (16 * U // RING) + 16 * ((u0 + k) // RING + 1))
                            for c in range(UK):
                                for j in range(G):
                                    k = (2 * bi + h) * G + j
                                    mm = pe.matmul(dst[W * j:W * j + W, :], src[:, UK * h + c, W * j:W * j + W],
                                                   ring[:, (u0 + k) % RING, c, :], start=(h == 0 and c == 0),
                                                   stop=(h == 1 and c == UK - 1))
                            if h == 0:
                                mm.then_inc(m["halves"], 1)
                        mm.then_inc(m["blocks"], 1)
                    for nb in range(2):
                        pe.wait_ge(m["hid"], 2 * i + 1 + nb)
                        product(2 * nb, bank[2 * nb], moe_x)
                        product(2 * nb + 1, bank[2 * nb + 1], moe_x)
                    for nb in range(2):
                        pe.wait_ge(m["hid"], 2 * i + 3 + nb)
                        if nb:
                            pe.wait_ge(m["ht_sb"], 2 * i + 1)
                        for q in range(4):
                            mm = pe.transpose(bank[7][:, P * q:P * q + P], moe_h[:, 512 * nb + P * q:512 * nb + P * q + P], ident)
                        mm.then_inc(m["ht_full"], 1)
                    pe.wait_ge(m["ht_sb"], 2 * i + 2)
                    for nb in range(2):
                        product(4 + nb, bank[4 + nb], moe_hT)
                    pe.wait_ge(m["g_sb"], i + 1)
                    pe.wait_ge(m["y_sb"], 2 * i + 4)
                    for n in range(n_sum):
                        if n >= 2:
                            pe.wait_ge(m["sum_free"], n_sum * i + n_sum + n - 1)
                        pe.matmul(bank[6 + n % 2][:, :], moe_g[:, P * (n // 2):P * (n // 2) + P], moe_y[:, 512 * (n % 2):512 * (n % 2) + 512],
                                  start=True, stop=True).then_inc(m["sum_full"], 1)

        @block.sync
        def _(sp):
            sp.dma_start(const[:, :], w["consts"]).then_inc(*signal("const_in", "const", 16))
            sp.dma_start(x[:, 0:2, :], w["x"][0].rearrange("(t p) d -> p t d", p=P)).then_inc(*signal("x_in", 0, 16))
            sp.dma_start(mem_rows, w["mem"][0].rearrange("(t p) d -> p t d", p=P)).then_inc(*signal("mem_in", 0, 16))
            u, moe_last = 0, {}
            for key, view in units:
                if key[0] == "experts":
                    layer = key[1]
                    m, G, order = M[layer], experts_per_group(layer), moe_units(layer)
                    U, groups = len(order), NE // G

                    def load(k, expert):
                        name, nb, h, j = order[k % U]
                        view = w[name][layer, expert(j + (G if k >= U else 0))].rearrange("(c p) n -> p c n", p=P)
                        sp.dma_start(ring[:, (u + k) % RING], view[:, UK * h:UK * h + UK, UN * nb:UN * nb + UN])\
                          .then_inc(ring_in[(u + k) % RING], 16)

                    def slot_free(k, i):
                        bi, h = (k - RING) // (2 * G), (k - RING) // G % 2
                        sp.wait_ge(m["blocks" if h else "halves"], i * 6 + bi + 1)
                        sp.sem_inc(m["loads"], 1)
                    for k in range(RING):
                        b, n = last_reader[u + k - RING]
                        sp.wait_ge(bank_full[b], n)
                        load(k, lambda e: e)
                    with sp.Fori(0, groups - 1) as i:
                        for k in range(RING, U + RING):
                            slot_free(k, i)
                            load(k, lambda e: i * G + e)
                    for k in range(RING, U):
                        slot_free(k, groups - 1)
                        load(k, lambda e: (groups - 1) * G + e)
                    for k in range(U - RING, U):
                        moe_last[u + U * (groups - 1) + k] = (m["blocks" if k // G % 2 else "halves"], (groups - 1) * 6 + k // (2 * G) + 1)
                    u += U * groups
                    continue
                if (stop and key[0] == stop):
                    break
                if u - RING in moe_last:
                    sp.wait_ge(*moe_last[u - RING])
                elif u >= RING:
                    b, n = last_reader[u - RING]
                    sp.wait_ge(bank_full[b], n)
                sp.dma_start(ring[:, u % RING, 0:view.shape[1], 0:view.shape[2]], view).then_inc(ring_in[u % RING], 16)
                u += 1
            for t in range(T2):
                sp.wait_ge(*after("x_ready", (5 if stop else "final", t)))
            sp.dma_start(out[0].rearrange("(t p) d -> p t d", p=P), x[:, 0:2, :]).then_inc(*signal("out_dma", 0, 16))
            sp.wait_ge(*after("out_dma", 0))

        @block.gpsimd
        def _(pool):
            pool.dma_start(cols[:, :], w["cols"]).then_inc(*signal("param_in", "cols", 16))
            pool.dma_start(gate_b[:, :], w["gate_b"]).then_inc(*signal("param_in", "gate_b", 16))
            pool.dma_start(gate_w[:, :, :], w["even_w_in"][0][:, 2048:2064].rearrange("(c p) n -> p c n", p=P))\
                .then_inc(*signal("param_in", "gate_w", 16))
            pool.dma_start(sink[:, :, :], w["sink_2"].partition_broadcast(P)).then_inc(*signal("param_in", "all", 16))
            pool.dma_start(router[:, :, :, :].rearrange("p l c e -> p (l c) e"), w["router_w_2"].rearrange("l (c p) e -> p (l c) e", p=P))\
                .then_inc(*signal("router_in", 0, 16))
            pool.wait_ge(*after("xT", ("in", 0, 0)))
            for r in range(ROWS):
                pool.dma_start(nab[64 * (r % 2):64 * (r % 2) + 64, r // 2, :, :].rearrange("p h (i k) -> p h i k", k=GRID_W),
                               w["rpb_windows"][:, :, ROWS - 1 - r:2 * ROWS - 1 - r, :]).then_inc(*signal("nab_in", r, 16))
            for i in range(3 * DEPTH):
                if i == 0:
                    pool.wait_ge(*after("oT", ("na", B_HEADS - 1)))
                else:
                    for t in range(T2):
                        pool.wait_ge(*after("x_ready", (i - 1, t)))
                for k, name in enumerate(("ln_g", "ln_b")):
                    pool.dma_start(ln_row[:, k, :], w[name][i // 3, i % 3].partition_broadcast(P))\
                        .then_inc(*signal("ln_row_in", (i, k), 16))
                if i == 2:
                    pool.dma_start(lam_raw.rearrange("p a b -> p (a b)"), w["odd_lambda"][0].rearrange("a b -> (a b)").partition_broadcast(P))\
                        .then_inc(*signal("lam_in", 0, 16))
            if stop:
                return
            for t in range(T2):
                pool.wait_ge(*after("x_ready", (4, t)))
            pool.dma_start(x[:, 2:4, :], w["ctx_2"][0].rearrange("(t p) d -> p t d", p=P)).then_inc(*signal("ctx_in", 0, 16))
            for t in range(T2):
                pool.wait_ge(*after("x2", (DEPTH - 1, 1, t)))
            pool.dma_start(g_row[:, 1, :], w["final_g_2"].partition_broadcast(P)).then_inc(*signal("final_row_in", 0, 16))

        @block.scalar
        def _(act):
            steps = [0]

            def link(ins):
                steps[0] += 1
                ins.then_inc(act_step, 1)
                act.wait_ge(act_step, steps[0])

            def copy_T(key, dst, func=ACT.Copy):
                act.wait_ge(*full(key))
                n = dst.shape[1]
                act.activation(dst, bank_of(key)[:, :].rearrange("p (a b) -> p a b", a=n), func)\
                   .then_inc(*freed(key))

            def evac(key, dst, func=ACT.Copy, a=None):
                act.wait_ge(*full(key))
                src = bank_of(key)[:, 0:int(np.prod(dst.shape[1:]))]
                if len(dst.shape) == 3:
                    src = src.rearrange("p (a b) -> p a b", a=dst.shape[1])
                link(act.activation(dst, src, func))
                act.sem_inc(*freed(key))

            def done(kind, key):
                act.sem_inc(*signal(kind, key))

            def to_T(key, event, off):
                for h in range(2):
                    evac(key + (h,), xT[:, 4 * h:4 * h + 4, off:off + P])
                    done("xT", event + (h,))

            def norm_T(i):
                for t in range(T2):
                    act.wait_ge(*after("var", (i, t)))
                    act.activation(std[:, t:t + 1], mv[:, t, 1:2], ACT.Sqrt).then_inc(*signal("rstd", (i, t)))
                for t in range(T2):
                    if i < 5:
                        to_T(("xT", i, t), (i, t), t * P)

            def exps(u, scale_in=True):
                parts = 1 if u["keys"] == 256 else 2
                act.wait_ge(*after("nmax", u["key"]))
                if u["n"] >= 2:
                    act.wait_ge(*full(("pT", u["key"][0], u["n"] - 2, parts - 1)))
                pr, m = probs_of(u), u["n"] % 2
                for t in range(2):
                    if u["bias"] is None:
                        key = ("s",) + u["key"] + (0 if parts == 1 else t,)
                        act.wait_ge(*full(key))
                        src = bank_of(key)[:, 0:512] if parts == 2 else bank_of(key)[:, 256 * t:256 * t + 256]
                        scale = u["scale"]
                    else:
                        src, scale = pr[:, t, :], 1.0
                    link(act.activation(pr[:, t, :], src, ACT.Exp, bias=small[:, m, t:t + 1], scale=scale,
                                        accum_out=small[:, m, 2 + t:3 + t]))
                    if u["bias"] is None and (parts == 2 or t == 1):
                        act.sem_inc(*freed(key))
                if u["sink"] is not None:
                    for t in range(2):
                        link(act.activation(small[:, m, 4 + t:5 + t], u["sink"], ACT.Exp, bias=small[:, m, t:t + 1]))
                done("probs_exp", u["key"])

            def evac_T(u):
                if u["n"] >= 2:
                    act.wait_ge(*full(("o", u["key"][0], u["n"] - 2)))
                for part in range(u["keys"] // 256):
                    key = ("pT",) + u["key"] + (part,)
                    evac(key, probsT_of(u)[:, 2 * part:2 * part + 2, :])
                done("probsT", u["key"])

            def attend(us):
                for i in range(len(us) + 1):
                    if i < len(us):
                        exps(us[i])
                    if i:
                        evac_T(us[i - 1])

            for t in range(T2):
                to_T(("xT", "in", t), ("in", t), t * P)
            for t in range(T2):
                to_T(("memT", t), ("mem", t), SEQ + t * P)
            for b in (0, 1):
                for j in range(2):
                    c = 4 * b + 2 * j
                    evac(("even_in", b, "out", j), qk_pad[:, c:c + 2, 2:2 + SEQ])
                    done("proj", ("even_in", b, "out", j))
            act.wait_ge(*after("gate_abs", 0))
            act.activation(g_tmp, g_tmp, ACT.Exp, scale=-1.0).then_inc(*signal("gate_exp", 0))
            act.wait_ge(*after("gate_ln1", 0))
            act.activation(g_tmp, g_tmp, ACT.Ln).then_inc(*signal("gate_ln", 0))
            for t in range(T2):
                evac(("even_in", 2, "out", t), a_v[:, t, :])
            for j in range(2):
                evac(("even_in", 3, "out", j), a_oT[:, 2 * j:2 * j + 2, :], ACT.Sigmoid)
            done("proj", "a_o")
            act.wait_ge(*full(("gate_cols",)))
            g = bank_of(("gate_cols",))
            link(act.activation(gcols[:, 0].rearrange("p a b c -> p (a b c)"), g[:, 0:16], ACT.Copy))
            link(act.activation(gcols[:, 1].rearrange("p a b c -> p (a b c)"), g[:, 16:32], ACT.Exp))
            act.sem_inc(*freed(("gate_cols",)))
            done("gate_cols", 0)
            for c in range(8):
                act.wait_ge(*after("conv", c))
                act.activation(qkT[:, c, :], qkT[:, c, :], ACT.Silu).then_inc(*signal("silu", c))
            for b in (4, 5):
                for j in range(2):
                    c = 4 * (b - 4) + 2 * j
                    evac(("even_in", b, "out", j), b_qkT[:, c:c + 2, :])
            for t in range(T2):
                evac(("even_in", 6, "out", t), b_v[:, t, :])
                done("proj", ("even_in", 6, "out", t))
            for h in range(A_HEADS + 1):
                if h < A_HEADS:
                    act.wait_ge(*after("decay", h))
                    for d in range(2):
                        for t in range(2):
                            e = decay[h % 2][:, d, t, :]
                            ins = act.activation(e, e, ACT.Exp, bias=gcols[:, 0, d, t, h:h + 1])
                    ins.then_inc(*signal("decay_exp", h))
                if h:
                    evac_T(ml_units[h - 1])
            attend(na_units)

            for layer in range(DEPTH):
                if layer == 1:
                    act.wait_ge(*after("lam_sums", 0))
                    link(act.activation(lam[:, 2:4], lam[:, 0:2], ACT.Exp))
                    done("lam_exps", 0)
                    for b in range(4):
                        for j in range(2):
                            for m in range(2):
                                c = 4 * b + 2 * j + m
                                if m == 0:
                                    act.wait_ge(*full(("odd_in", b, "out", j)))
                                if c >= 2:
                                    act.wait_ge(*after("rope_out", c - 2))
                                else:
                                    act.wait_ge(*after("lam_sums", 0))
                                link(act.activation(raw[:, c % 2, :], bank_of(("odd_in", b, "out", j))[:, 256 * m:256 * m + 256], ACT.Copy))
                                done("proj", ("raw", c))
                            act.sem_inc(*freed(("odd_in", b, "out", j)))
                    for b in (4, 5):
                        for t in range(T2):
                            evac(("odd_in", b, "out", t), v_rows[:, t, 512 * (b - 4):512 * (b - 4) + 512])
                            done("proj", ("odd_in", b, "out", t))

                    def diff_exps(u):
                        act.wait_ge(*after("nmax", u["key"]))
                        for m in range(2):
                            for t in range(2):
                                key = ("s",) + u["key"] + (m,)
                                link(act.activation(diff_probs(u, m)[:, t, :], bank_of(key)[:, 256 * t:256 * t + 256], ACT.Exp,
                                                    bias=small[:, u["n"] % 2, 2 * m + t:2 * m + t + 1], scale=u["scale"],
                                                    accum_out=small[:, u["n"] % 2, 4 + 2 * m + t:5 + 2 * m + t]))
                            act.sem_inc(*freed(key))
                        done("probs_exp", u["key"])

                    def diff_out(u):
                        key = ("o",) + u["key"]
                        act.wait_ge(*full(key))
                        act.activation(u["y"][0][0], bank_of(key)[:, 0:SEQ], ACT.Copy)
                        if u["n"] >= 2:
                            act.wait_ge(*full(("ss", u["n"] - 2)))
                        link(act.activation(raw[:, u["n"] % 2, :], bank_of(key)[:, 0:SEQ], ACT.Square))
                        act.sem_inc(*freed(key))
                        done("ssq", u["n"])
                    for i in range(C_HEADS + 2):
                        if i < C_HEADS:
                            diff_exps(diff_units[i])
                        if 0 <= i - 1 < C_HEADS:
                            evac_T(diff_units[i - 1])
                        if 0 <= i - 2:
                            diff_out(diff_units[i - 2])
                    act.wait_ge(*after("rms", "diff"))
                    act.activation(dvar, dvar, ACT.Sqrt).then_inc(*signal("rstd", "diff"))
                n0 = 3 * layer
                for b in range(2):
                    for j in range(2):
                        c = 4 * b + 2 * j
                        evac(("mem_kv", layer, b, "out", j), kT[:, c:c + 2, :])
                for b in range(2, 4):
                    for t in range(T2):
                        evac(("mem_kv", layer, b, "out", t), v_rows[:, t, 512 * (b - 2):512 * (b - 2) + 512])
                norm_T(n0)
                for b in range(2):
                    for j in range(2):
                        c = 4 * b + 2 * j
                        evac(("mem_q", layer, b, "out", j), qT[:, c:c + 2, :])
                        done("proj", ("mem_q", layer, b, "out", j))
                attend(mem_units(layer))
                norm_T(n0 + 1)
                for k in range(FC // 2):
                    b, j = k // 2, k % 2
                    key = ("gate", layer, b, "out", j)
                    act.wait_ge(*full(key))
                    if k >= 2:
                        act.wait_ge(*after("hid", (layer, k - 2)))
                    link(act.activation(hsilu[:, k % 2, :], bank_of(key)[:, :], ACT.Silu))
                    act.sem_inc(*freed(key))
                    done("silu", (layer, k))
                norm_T(n0 + 2)
            if stop:
                return
            for layer in range(DEPTH):
                seqs = 2 if layer == 0 else 1
                n_tok = SEQ * seqs
                tiles = range(2 * seqs)
                act.wait_ge(*after("zero", (layer, "scT")))
                act.activation(scT[:, :, 0:2], col("cc", 0, 16).rearrange("p (c s) -> p c s", s=2), ACT.Silu)\
                   .then_inc(*signal("sc_silu", layer))
                for g in range(3):
                    evac(("ada", layer, g), mods_rows[:, g, :])
                    done("mods_rows", (layer, g))

                def gate_rows_of(kind):
                    for s in range(seqs):
                        for h in range(2):
                            if kind == 1 and s == 0 and h == 0:
                                for t in tiles:
                                    act.wait_ge(*after("x2", (layer, 0, t)))
                            evac(("gbc", layer, kind, s, h), g_row[:, s, 512 * h:512 * h + 512])
                    done("gates_bc", (layer, kind))

                def norm_rows(kind, ts):
                    act.wait_ge(*after("ssq2", (layer, kind)))
                    act.activation(std[:, 0:len(ts)], mv[:, 0:len(ts), 1], ACT.Sqrt).then_inc(*signal("rstd", ("n2", layer, kind)))

                def hidden_T(kind, ns):
                    for c in range(KC):
                        act.wait_ge(*full(("h", layer, kind, c)))
                        for s in range(ns):
                            ins = act.activation(xT[:, c, SEQ * s:SEQ * s + SEQ], bank_of(("h", layer, kind, c))[:, SEQ * s:SEQ * s + SEQ],
                                                 ACT.Identity, bias=shift(kind)[:, c, s:s + 1], scale=gain[:, kind, c, s:s + 1])
                        link(ins)
                        act.sem_inc(*freed(("h", layer, kind, c)))
                        done("hT", (layer, kind, c))

                norm_rows(0, range(4))
                gate_rows_of(0)
                act.wait_ge(*after("mods", layer))
                hidden_T(0, 2)
                for name in CHUNKS:
                    if name in ("cq0", "cq1", "dq0", "dq1"):
                        continue
                    key, i = ("c", layer, name), int(name[2])
                    if name[:2] == "ab":
                        evac(key, y_lo[:, i, 0:n_tok])
                        done("ab_in", (layer, i))
                    elif name[:2] == "ac":
                        evac(key, y_lo[:, 2 + i, 0:n_tok])
                        done("ab_in", (layer, 2 + i))
                    elif name[:2] == "bv":
                        evac(key, sig[:, i, 0:n_tok])
                        done("u_in", (layer, "v", i))
                    elif name[:2] == "bg":
                        act.wait_ge(*full(key))
                        act.wait_ge(*after("gbc_free", (layer, i)))
                        link(act.activation(sq[:, i, 0:n_tok], bank_of(key)[:, 0:n_tok], ACT.Sigmoid))
                        act.sem_inc(*freed(key))
                        done("u_in", (layer, "g", i))

                def qk_evac(name):
                    n = n_tok if name[1] == "q" else 2 * SEQ
                    evac(("c", layer, name), qk[:, QK_AT[name], 0:n])
                    done("proj", ("qk", layer, name))

                for name in ("cq0", "cq1", "dq0", "dq1", "ck0", "ck1"):
                    qk_evac(name)
                evac(("c", layer, "cv"), v2[:, :, 0, :])
                for name in ("dk0", "dk1"):
                    qk_evac(name)
                evac(("c", layer, "dv"), v2[:, :, 1, :])
                done("proj", ("v2", layer, "dv"))
                act.wait_ge(*after("u_in2", (layer, 1)))
                for i, name in enumerate(("dq0", "dq1", "dk0", "dk1")):
                    n = n_tok if name[1] == "q" else 2 * SEQ
                    if i >= 2:
                        act.wait_ge(*full(("qss", layer, ("dq0", "dq1")[i - 2])))
                    act.activation(sq[:, i % 2, 0:n], qk[:, QK_AT[name], 0:n], ACT.Square).then_inc(*signal("sq", (layer, name)))
                for i, name in enumerate(("dq0", "dq1", "dk0", "dk1")):
                    n = n_tok if name[1] == "q" else 2 * SEQ
                    act.wait_ge(*after("ssq", ("qk", layer, name)))
                    act.activation(qvar[:, i % 2, 0:n], qvar[:, i % 2, 0:n], ACT.Sqrt).then_inc(*signal("rstd", ("qk", layer, name)))
                act.wait_ge(*after("uvar", layer))
                act.activation(std[:, 0:len(tiles)], mv[:, 0:len(tiles), 1], ACT.Sqrt).then_inc(*signal("rstd", ("u", layer)))
                for c in range(2):
                    key = ("ub", layer, c)
                    act.wait_ge(*full(key))
                    at = 2 * layer + c
                    link(act.activation(y_lo[:, 2 + c, 0:n_tok], bank_of(key)[:, 0:n_tok], ACT.Silu, bias=col("cln_b", at), scale=col("cln_g", at)))
                    act.sem_inc(*freed(key))
                    done("yb", (layer, c))
                for us in by_stage(block2_units(layer)):
                    attend(us)
                norm_rows(1, tiles)
                gate_rows_of(1)
                hidden_T(1, seqs)
                act.wait_ge(*after("logit_max", layer))
                act.activation(aff[:, 0:len(tiles), :], aff[:, 0:len(tiles), :], ACT.Exp).then_inc(*signal("aff_exp", layer))

                m, G = M[layer], experts_per_group(layer)
                act.sem_inc(m["y_sb"], 2)
                with act.Fori(0, NE // G) as i:
                    act.wait_ge(m["g_full"], i + 1)
                    n = P * len(tiles)
                    act.activation(moe_g[:, 0:n], bank[6][:, 0:n], ACT.Copy).then_inc(m["g_sb"], 1)
                    for nb in range(2):
                        act.wait_ge(m["blocks"], 6 * i + 2 * nb + 1)
                        act.activation(moe_silu[:, nb, :], bank[2 * nb][:, :], ACT.Silu).then_inc(m["silu"], 1)
                    for nb in range(2):
                        act.wait_ge(m["ht_full"], 2 * i + nb + 1)
                        act.activation(moe_hT[:, 4 * nb:4 * nb + 4, :].rearrange("p a b -> p (a b)"), bank[7][:, :], ACT.Copy)\
                           .then_inc(m["ht_sb"], 1)
                    for nb in range(2):
                        act.wait_ge(m["blocks"], 6 * i + 5 + nb)
                        act.activation(moe_y[:, 512 * nb:512 * nb + 512], bank[4 + nb][:, :], ACT.Copy).then_inc(m["y_sb"], 1)
            act.wait_ge(*after("ssq2", ("final", 0)))
            act.activation(std[:, 0:2], mv[:, 0:2, 1], ACT.Sqrt).then_inc(*signal("rstd", "final"))

        @block.vector
        def _(dve):
            steps = [0]

            def link(ins):
                steps[0] += 1
                ins.then_inc(dve_step, 1)
                dve.wait_ge(dve_step, steps[0])

            def done(kind, key):
                dve.sem_inc(*signal(kind, key))

            def drop(key):
                dve.sem_inc(*freed(key))

            def residual_norm(i, key):
                for nb in range(2):
                    for t in range(T2):
                        k = key + (nb, "out", t)
                        dve.wait_ge(*full(k))
                        xs = x[:, t, 512 * nb:512 * nb + 512]
                        link(dve.scalar_tensor_tensor(xs, xs, ALPHA, bank_of(k)[:, :], ALU.mult, ALU.add))
                        drop(k)
                        link(dve.bn_stats(stats[:, t, nb, :], xs))
                for t in range(T2):
                    link(dve.bn_aggr(mv[:, t, :], stats[:, t, :, :].rearrange("p a b -> p (a b)")))
                    dve.tensor_scalar(mv[:, t, 1:2], mv[:, t, 1:2], LN_EPS, None, ALU.add).then_inc(*signal("var", (i, t)))
                for t in range(T2):
                    dve.wait_ge(*after("rstd", (i, t)))
                    link(dve.reciprocal(rstd[:, t:t + 1], std[:, t:t + 1]))
                    link(dve.tensor_scalar(x[:, t, :], x[:, t, :], mv[:, t, 0:1], rstd[:, t:t + 1], ALU.subtract, ALU.mult))
                    dve.wait_ge(*after("ln_row_in", (i, 1)))
                    link(dve.tensor_tensor(x[:, t, :], x[:, t, :], ln_row[:, 0, :], ALU.mult))
                    dve.tensor_tensor(x[:, t, :], x[:, t, :], ln_row[:, 1, :], ALU.add).then_inc(*signal("x_ready", (i, t)))

            def maxima(u):
                parts = 1 if u["keys"] == 256 else 2
                m, pr = u["n"] % 2, probs_of(u)
                if u["n"] >= 2:
                    dve.wait_ge(*full(("pT", u["key"][0], u["n"] - 2, parts - 1)))
                for part in range(parts):
                    key = ("s",) + u["key"] + (part,)
                    dve.wait_ge(*full(key))
                    ts = slice(0, 2) if parts == 1 else slice(part, part + 1)
                    src = bank_of(key)[:, :].rearrange("p (t k) -> p t k", k=u["keys"])
                    if u["bias"] is not None:
                        n = u["bias"].shape[2]
                        link(dve.scalar_tensor_tensor(pr[:, ts, 0:n], src[:, :, 0:n], u["scale"], u["bias"][:, ts, :], ALU.mult, ALU.add))
                        if n < u["keys"]:
                            link(dve.tensor_scalar(pr[:, ts, n:], src[:, :, n:], u["scale"], None, ALU.mult))
                        drop(key)
                        src = pr[:, ts, :]
                    link(dve.tensor_reduce(small[:, m, 6:8][:, ts], src, AX.X, ALU.max))
                scale = u["scale"] if u["bias"] is None else 1.0
                if u["sink"] is not None:
                    if scale != 1.0:
                        link(dve.tensor_scalar(small[:, m, 6:8], small[:, m, 6:8], scale, None, ALU.mult))
                        scale = 1.0
                    link(dve.tensor_scalar(small[:, m, 6:8], small[:, m, 6:8], u["sink"], None, ALU.max))
                link(dve.tensor_scalar(small[:, m, 0:2], small[:, m, 6:8], -scale, None, ALU.mult))
                done("nmax", u["key"])

            def normalise(u):
                m, pr = u["n"] % 2, probs_of(u)
                dve.wait_ge(*after("probs_exp", u["key"]))
                if u["sink"] is not None:
                    link(dve.tensor_tensor(small[:, m, 2:4], small[:, m, 2:4], small[:, m, 4:6], ALU.add))
                link(dve.reciprocal(small[:, m, 8:10], small[:, m, 2:4]))
                for t in range(2):
                    ins = dve.tensor_scalar(pr[:, t, :], pr[:, t, :], small[:, m, 8 + t:9 + t], None, ALU.mult)
                ins.then_inc(*signal("probs", u["key"]))

            def output(u, gate=None):
                key = ("o",) + u["key"]
                dve.wait_ge(*full(key))
                for i, (y, p0) in enumerate(u["y"]):
                    src = bank_of(key)[p0:p0 + y.shape[0], 256 * i:256 * i + 256]
                    if gate is None:
                        ins = dve.tensor_copy(y, src)
                    else:
                        ins = dve.tensor_tensor(y, src, gate, ALU.mult)
                link(ins)
                drop(key)
                done("oT", u["key"])

            def attend(us):
                maxima(us[0])
                for i in range(len(us) + 2):
                    if i + 1 < len(us):
                        maxima(us[i + 1])
                    if i < len(us):
                        normalise(us[i])
                    if i >= 2:
                        output(us[i - 2])

            def gates():
                for kind, dst in ((0, g_in), (1, g_forget)):
                    dve.wait_ge(*full(("gates", kind)))
                    src = bank_of(("gates", kind))[0:4, :].rearrange("p (d k) -> p d k", d=2)
                    for d in range(2):
                        ins = dve.tensor_scalar(dst[:, d, :], src[:, d, :], gate_b[:, 2 * kind + d:2 * kind + d + 1], None, ALU.add)
                    link(ins)
                    drop(("gates", kind))
                dve.scalar_tensor_tensor(g_tmp, g_forget, -1.0, g_forget, ALU.mult, ALU.max).then_inc(*signal("gate_abs", 0))
                dve.wait_ge(*after("gate_exp", 0))
                dve.tensor_scalar(g_tmp, g_tmp, 1.0, None, ALU.add).then_inc(*signal("gate_ln1", 0))
                dve.wait_ge(*after("gate_ln", 0))
                link(dve.scalar_tensor_tensor(g_forget, g_forget, 0.0, g_tmp, ALU.min, ALU.subtract))

                def along(v, d):
                    return v[:, d, :] if d == 0 else v[:, d, ::-1]
                for d in range(2):
                    ins = dve.tensor_tensor_scan(along(g_tmp, d), g_one[:, :], along(g_forget, d), 0.0, ALU.mult, ALU.add)
                link(ins)
                link(dve.tensor_tensor(g_c, g_in, g_tmp, ALU.subtract))
                for d in range(2):
                    ins = dve.tensor_tensor_scan(along(g_in, d), along(g_c, d), along(g_c, d), NEG, ALU.max, ALU.max)
                link(ins)
                link(dve.tensor_scalar(g_max[:, 0:2, :], g_in, -1.0, None, ALU.mult))
                dve.tensor_tensor(g_max[:, 2:4, :], g_max[:, 0:2, :], g_tmp, ALU.subtract).then_inc(*signal("gate_rows", 0))

            dve.memset(qk_pad[:, :, 0:2], 0.0)
            link(dve.memset(qk_pad[:, :, SEQ + 2:SEQ + 4], 0.0))
            link(dve.memset(g_one[:, :], 1.0))
            dve.wait_ge(*after("const_in", "const"))
            dve.wait_ge(*after("param_in", "all"))
            for c in range(8):
                dve.wait_ge(*after("proj", ("even_in", c // 4, "out", c // 2 % 2)))
                link(dve.tensor_scalar(qkT[:, c, :], qk_pad[:, c, 0:SEQ], col("conv", c), None, ALU.mult))
                for j in range(1, A_CONV):
                    ins = dve.scalar_tensor_tensor(qkT[:, c, :], qk_pad[:, c, j:j + SEQ], col("conv", 8 * j + c), qkT[:, c, :],
                                                   ALU.mult, ALU.add)
                    if j < A_CONV - 1:
                        link(ins)
                ins.then_inc(*signal("conv", c))
                if c == 3:
                    gates()

            mlmask = con("mlmask").rearrange("p (d t k) -> p d t k", d=2, t=2)

            def decays(h):
                if h >= 2:
                    dve.wait_ge(*after("probs", ("ml", h - 2)))
                dve.wait_ge(*full(("cb", h)))
                for d in range(2):
                    cb = bank_of(("cb", h))[:, 256 * d:256 * d + 256].unsqueeze(1).to_broadcast([P, 2, SEQ])
                    ins = dve.tensor_tensor(decay[h % 2][:, d], cb, mlmask[:, d], ALU.add)
                link(ins)
                drop(("cb", h))
                done("decay", h)

            def mixes(h):
                u = ml_units[h]
                m, pr, key = h % 2, probs_of(u), ("s", "ml", h, 0)
                dve.wait_ge(*after("decay_exp", h))
                dve.wait_ge(*full(key))
                for d in range(2):
                    for t in range(2):
                        e = decay[h % 2][:, d, t, :]
                        ins = dve.scalar_tensor_tensor(e, bank_of(key)[:, 256 * t:256 * t + 256], P ** -0.5, e, ALU.mult, ALU.mult,
                                                       accum_out=small[:, m, 2 * d + t:2 * d + t + 1])
                link(ins)
                drop(key)
                dve.wait_ge(*after("gate_cols", 0))
                den, big = small[:, m, 0:4], small[:, m, 4:8]
                link(dve.scalar_tensor_tensor(big, den, -1.0, den, ALU.mult, ALU.max))
                floor = gcols[:, 1, :, :, h]
                big2 = big.rearrange("p (d t) -> p d t", d=2)
                link(dve.tensor_tensor(big2, big2, floor, ALU.max))
                link(dve.reciprocal(small[:, m, 8:12], big))
                if h >= 2:
                    dve.wait_ge(*full(("pT", "ml", h - 2, 0)))
                for t in range(2):
                    ins = dve.tensor_scalar(pr[:, t, :], decay[h % 2][:, 0, t, :], small[:, m, 8 + t:9 + t], None, ALU.mult)
                link(ins)
                for t in range(2):
                    ins = dve.scalar_tensor_tensor(pr[:, t, :], decay[h % 2][:, 1, t, :], small[:, m, 10 + t:11 + t], pr[:, t, :],
                                                   ALU.mult, ALU.add)
                ins.then_inc(*signal("probs", ("ml", h)))

            dve.wait_ge(*after("proj", "a_o"))
            for h in range(A_HEADS):
                decays(h)
                mixes(h)
                if h:
                    output(ml_units[h - 1], a_oT[:, h - 1, :])
            output(ml_units[-1], a_oT[:, A_HEADS - 1, :])
            dve.wait_ge(*after("nab_in", ROWS - 1))
            keep = con("namask").unsqueeze(1).to_broadcast([P, T2 * B_HEADS * ROWS, GRID_W])
            nab_rows = nab.rearrange("p t h (i k) -> p (t h i) k", k=GRID_W)
            link(dve.tensor_tensor(nab_rows, nab_rows, keep, ALU.add))
            attend(na_units)
            residual_norm(0, ("even_out",))
            for layer in range(DEPTH):
                n0 = 3 * layer
                if layer == 1:
                    lp = lam_raw
                    dve.wait_ge(*after("lam_in", 0))
                    for i in range(2):
                        ins = dve.scalar_tensor_tensor(rcos[:, 0, 64 * i:64 * i + 64], lp[:, 2 * i, :], 1.0, lp[:, 2 * i + 1, :], ALU.mult,
                                                       ALU.mult, accum_out=lam[:, i:i + 1])
                    link(ins)
                    done("lam_sums", 0)
                    dve.wait_ge(*after("lam_exps", 0))
                    link(dve.tensor_tensor(lam[:, 4:5], lam[:, 3:4], lam[:, 2:3], ALU.subtract))
                    link(dve.tensor_scalar(lam[:, 5:6], lam[:, 4:5], -LAM_INIT, None, ALU.add))
                    link(dve.tensor_scalar(lam[:, 6:7], col("subln"), 1.0 - LAM_INIT, None, ALU.mult))
                    for c in range(16):
                        dst = (qT if c < 8 else kT)[:, c % 8, :]
                        dve.wait_ge(*after("proj", ("raw", c)))
                        dve.tensor_tensor(rcos[:, c % 2, :], raw[:, c % 2, :], con("cos1"), ALU.mult)
                        dve.wait_ge(*full(("rot", c)))
                        link(dve.tensor_tensor(dst, bank_of(("rot", c))[:, 0:SEQ], con("sin1"), ALU.mult))
                        drop(("rot", c))
                        dve.tensor_tensor(dst, dst, rcos[:, c % 2, :], ALU.add).then_inc(*signal("rope_out", c))

                    def diff_maxima(u):
                        m = u["n"] % 2
                        for k in range(2):
                            key = ("s",) + u["key"] + (k,)
                            dve.wait_ge(*full(key))
                            link(dve.tensor_reduce(small[:, m, 12 + 2 * k:14 + 2 * k],
                                                   bank_of(key)[:, :].rearrange("p (t k) -> p t k", t=2), AX.X, ALU.max))
                        link(dve.tensor_scalar(small[:, m, 0:4], small[:, m, 12:16], -u["scale"], None, ALU.mult))
                        done("nmax", u["key"])

                    def diff_normalise(u):
                        m = u["n"] % 2
                        dve.wait_ge(*after("probs_exp", u["key"]))
                        link(dve.reciprocal(small[:, m, 8:12], small[:, m, 4:8]))
                        link(dve.tensor_scalar(small[:, m, 10:12], small[:, m, 10:12], lam[:, 5:6], None, ALU.mult))
                        for t in range(2):
                            ins = dve.tensor_scalar(diff_probs(u, 0)[:, t, :], diff_probs(u, 0)[:, t, :], small[:, m, 8 + t:9 + t], None, ALU.mult)
                        link(ins)
                        for t in range(2):
                            ins = dve.scalar_tensor_tensor(diff_probs(u, 0)[:, t, :], diff_probs(u, 1)[:, t, :], small[:, m, 10 + t:11 + t],
                                                           diff_probs(u, 0)[:, t, :], ALU.mult, ALU.add)
                        ins.then_inc(*signal("probs", u["key"]))

                    diff_maxima(diff_units[0])
                    for i in range(C_HEADS + 2):
                        if i + 1 < C_HEADS:
                            diff_maxima(diff_units[i + 1])
                        if i < C_HEADS:
                            diff_normalise(diff_units[i])
                        if i >= 2:
                            dve.wait_ge(*full(("ss", i - 2)))
                            link(dve.tensor_scalar(dvar[:, i - 2, :], bank_of(("ss", i - 2))[:, 0:SEQ], 1.0 / P, LN_EPS, ALU.mult, ALU.add))
                            drop(("ss", i - 2))
                    done("rms", "diff")
                    dve.wait_ge(*after("rstd", "diff"))
                    link(dve.reciprocal(dvar, dvar))
                    for h in range(C_HEADS):
                        y = y1T[:, h, :]
                        dve.scalar_tensor_tensor(y, y, lam[:, 6:7], dvar[:, h, :], ALU.mult, ALU.mult)\
                           .then_inc(*signal("oT", ("diff", h)))
                    residual_norm(n0, ("odd_out",))
                attend(mem_units(layer))
                residual_norm(n0 + 1, ("mem_o", layer))
                for k in range(FC // 2):
                    key = ("up", layer, k // 2, "out", k % 2)
                    dve.wait_ge(*after("silu", (layer, k)))
                    dve.wait_ge(*full(key))
                    link(dve.tensor_tensor(hT[:, 2 * k:2 * k + 2, :].rearrange("p a b -> p (a b)"), bank_of(key)[:, :], hsilu[:, k % 2, :], ALU.mult))
                    drop(key)
                    done("hid", (layer, k))
                residual_norm(n0 + 2, ("down", layer))
            if stop:
                return

            def gate_diag(layer, kind, seqs):
                for s in range(seqs):
                    if s:
                        dve.wait_ge(*full(("gbc", layer, kind, 0, 1)))
                    g = modsT[:, 16 + 24 * kind:24 + 24 * kind, s:s + 1].to_broadcast([P, KC, P])
                    dve.tensor_tensor(diag, ident.unsqueeze(1).to_broadcast([P, KC, P]), g, ALU.mult)\
                       .then_inc(*signal("diag", (layer, kind, s)))

            def norm_rows(layer, kind, ts):
                for t in ts:
                    ins = dve.scalar_tensor_tensor(xhat[:, t, :], x[:, t, :], 1.0, x[:, t, :], ALU.mult, ALU.mult,
                                                   accum_out=mv[:, t, 0:1])
                link(ins)
                dve.tensor_scalar(mv[:, 0:len(ts), 1], mv[:, 0:len(ts), 0], 1.0 / D, EPS, ALU.mult, ALU.add)\
                   .then_inc(*signal("ssq2", (layer, kind)))
                dve.wait_ge(*after("rstd", ("n2", layer, kind) if layer != "final" else "final"))
                link(dve.reciprocal(rstd[:, 0:len(ts)], std[:, 0:len(ts)]))
                if layer != "final":
                    for t in ts:
                        dve.tensor_scalar(xhat[:, t, :], x[:, t, :], rstd[:, t:t + 1], None, ALU.mult)\
                           .then_inc(*signal("xhat", (layer, kind, t)))

            dve.wait_ge(*after("x_ready", (5, 1)))
            dve.wait_ge(*after("ctx_in", 0))
            for layer in range(DEPTH):
                seqs = 2 if layer == 0 else 1
                n_tok = SEQ * seqs
                tiles = range(2 * seqs)
                dve.memset(scT, 0.0).then_inc(*signal("zero", (layer, "scT")))
                norm_rows(layer, 0, range(4))
                for g in range(3):
                    key = ("modsT", layer, g)
                    dve.wait_ge(*full(key))
                    src = bank_of(key)[:, :].rearrange("p (q j r) -> p j q r", q=4, j=4)[:, :, :, 0:2]
                    at = COLS["ada_b"][0] + 48 * layer + 16 * g
                    bias = cols[:, at:at + 16].rearrange("p (j q) -> p j q", j=4).unsqueeze(3).to_broadcast([P, 4, 4, 2])
                    dst = modsT[:, 16 * g:16 * g + 16, :].rearrange("p (j q) s -> p j q s", j=4)
                    link(dve.tensor_tensor(dst, src, bias, ALU.add))
                    drop(key)
                for kind, name in enumerate(("n1", "n2")):
                    sc = modsT[:, 24 * kind + 8:24 * kind + 16, :]
                    n = col(name, 8 * layer, 8).unsqueeze(2).to_broadcast([P, KC, 2])
                    ins = dve.scalar_tensor_tensor(gain[:, kind], sc, 1.0, n, ALU.add, ALU.mult)
                link(ins)
                done("mods", layer)
                gate_diag(layer, 0, seqs)
                dve.memset(z_pad[:, :, :, 0:1], 0.0)
                dve.memset(z_pad[:, :, :, SEQ + 1:SEQ + 2], 0.0)
                dve.memset(u_pad[:, :, :, 0:PAD_B], 0.0)
                link(dve.memset(u_pad[:, :, :, SEQ + PAD_B:SEQ + 2 * PAD_B], 0.0))
                dve.wait_ge(*full(("gbc", layer, 0, seqs - 1, 1)))
                for i in range(2):
                    done("gbc_free", (layer, i))
                for i in range(2):
                    key = ("c", layer, f"ah{i}")
                    dve.wait_ge(*after("ab_in", (layer, 2 + i)))
                    dve.wait_ge(*full(key))
                    seq = [v.rearrange("p (s k) -> p s k", k=SEQ) for v in (y_lo[:, 2 + i, 0:n_tok], bank_of(key)[:, 0:n_tok])]
                    link(dve.tensor_tensor(z_pad[:, i, 0:seqs, 1:1 + SEQ], seq[0], seq[1], ALU.mult))
                    drop(key)
                    y = y_lo[:, 2 + i, 0:n_tok].rearrange("p (s k) -> p s k", k=SEQ)
                    at = 6 * layer + i
                    link(dve.tensor_scalar(y, z_pad[:, i, 0:seqs, 0:SEQ], col("conv_a", at), None, ALU.mult))
                    for j in (1, 2):
                        link(dve.scalar_tensor_tensor(y, z_pad[:, i, 0:seqs, j:j + SEQ], col("conv_a", at + 2 * j), y, ALU.mult, ALU.add))
                    link(dve.tensor_tensor(y_lo[:, i, 0:n_tok], y_lo[:, i, 0:n_tok], y_lo[:, 2 + i, 0:n_tok], ALU.mult))
                for i in range(2):
                    dve.wait_ge(*after("u_in", (layer, "v", i)))
                    dve.wait_ge(*after("u_in", (layer, "g", i)))
                    a, b = (v[:, i, 0:n_tok].rearrange("p (s k) -> p s k", k=SEQ) for v in (sig, sq))
                    link(dve.tensor_tensor(u_pad[:, i, 0:seqs, PAD_B:PAD_B + SEQ], a, b, ALU.mult))
                    done("u_in2", (layer, i))

                def long_conv(i):
                    y = y_lo[:, 2 + i, 0:n_tok].rearrange("p (s k) -> p s k", k=SEQ)
                    at = 62 * layer + i
                    link(dve.tensor_scalar(y, u_pad[:, i, 0:seqs, 0:SEQ], col("conv_b", at), col("conv_bb", 2 * layer + i), ALU.mult, ALU.add))
                    for j in range(1, CONV_B):
                        link(dve.scalar_tensor_tensor(y, u_pad[:, i, 0:seqs, j:j + SEQ], col("conv_b", at + 2 * j), y, ALU.mult, ALU.add))
                    done("uconv", (layer, i))

                for i, name in enumerate(("dq0", "dq1", "dk0", "dk1")):
                    n = n_tok if name[1] == "q" else 2 * SEQ
                    key = ("qss", layer, name)
                    dve.wait_ge(*full(key))
                    link(dve.tensor_scalar(qvar[:, i % 2, 0:n], bank_of(key)[:, 0:n], 1.0 / HD, EPS, ALU.mult, ALU.add))
                    drop(key)
                    done("ssq", ("qk", layer, name))
                    dve.wait_ge(*after("rstd", ("qk", layer, name)))
                    link(dve.reciprocal(qvar[:, i % 2, 0:n], qvar[:, i % 2, 0:n]))
                    v = qk[:, QK_AT[name], 0:n]
                    link(dve.scalar_tensor_tensor(v, v, col("qn" if name[1] == "q" else "kn", layer), qvar[:, i % 2, 0:n], ALU.mult, ALU.mult))
                    done("rms", ("qk", layer, name))
                for i, name in enumerate(QK_AT):
                    v = qk[:, QK_AT[name], 0:SEQ]
                    key = ("rot2", layer, name)
                    dve.wait_ge(*full(key))
                    dve.tensor_tensor(rtmp[:, 0, :], bank_of(key)[:, 0:SEQ], con("sin2"), ALU.mult)
                    link(dve.tensor_tensor(v, v, con("cos2"), ALU.mult))
                    drop(key)
                    link(dve.tensor_tensor(v, v, rtmp[:, 0, :], ALU.add))
                    done("rope_out", ("qk", layer, name))
                for i in range(2):
                    long_conv(i)
                for tp in range(seqs):
                    key = ("u", layer, tp)
                    dve.wait_ge(*full(key))
                    for t in range(2):
                        link(dve.bn_stats(stats[:, 2 * tp + t, 0, :], bank_of(key)[:, 256 * t:256 * t + 256]))
                        link(dve.bn_aggr(mv[:, 2 * tp + t, :], stats[:, 2 * tp + t, 0, :]))
                dve.tensor_scalar(mv[:, 0:len(tiles), 1], mv[:, 0:len(tiles), 1], EPS, None, ALU.add).then_inc(*signal("uvar", layer))
                dve.wait_ge(*after("rstd", ("u", layer)))
                link(dve.reciprocal(rstd[:, 0:len(tiles)], std[:, 0:len(tiles)]))
                for tp in range(seqs):
                    key = ("u", layer, tp)
                    for t in range(2):
                        tt = 2 * tp + t
                        ins = dve.tensor_scalar(u_rows[:, tt, :], bank_of(key)[:, 256 * t:256 * t + 256], mv[:, tt, 0:1], rstd[:, tt:tt + 1],
                                                ALU.subtract, ALU.mult)
                    link(ins)
                    drop(key)
                    done("u_norm", (layer, tp))
                for us in by_stage(block2_units(layer)):
                    attend(us)
                dve.wait_ge(*after("gates_bc", (layer, 0)))
                n = 0
                for nb in range(2):
                    for t in tiles:
                        key = ("out2", layer, nb, "out", t)
                        dve.wait_ge(*full(key))
                        link(dve.tensor_tensor(btmp[:, n % 2, :], bank_of(key)[:, :], g_row[:, t // 2, 512 * nb:512 * nb + 512], ALU.mult))
                        drop(key)
                        xs = x[:, t, 512 * nb:512 * nb + 512]
                        link(dve.tensor_tensor(xs, xs, btmp[:, n % 2, :], ALU.add))
                        n += 1
                        if nb:
                            done("x2", (layer, 0, t))
                norm_rows(layer, 1, tiles)
                gate_diag(layer, 1, seqs)
                L = len(tiles)
                key = ("logits", layer)
                dve.wait_ge(*full(key))
                lg = bank_of(key)[:, 0:NE * L].rearrange("p (t e) -> p t e", e=NE)
                link(dve.tensor_reduce(lmax[:, 0, 0:L], lg, AX.X, ALU.max))
                link(dve.tensor_tensor(aff[:, 0:L, :], lg, lmax[:, 0, 0:L].unsqueeze(2).to_broadcast([P, L, NE]), ALU.subtract))
                drop(key)
                done("logit_max", layer)
                dve.wait_ge(*after("aff_exp", layer))
                link(dve.tensor_reduce(lmax[:, 0, 0:L], aff[:, 0:L, :], AX.X, ALU.add))
                link(dve.reciprocal(lmax[:, 1, 0:L], lmax[:, 0, 0:L]))
                dve.tensor_tensor(aff[:, 0:L, :], aff[:, 0:L, :], lmax[:, 1, 0:L].unsqueeze(2).to_broadcast([P, L, NE]), ALU.mult)\
                   .then_inc(*signal("aff", layer))
                key = ("affT", layer)
                dve.wait_ge(*full(key))
                link(dve.memset(ones_row[:, 0:SEQ], 1.0))
                link(dve.tensor_copy(left[:, 0:n_tok], bank_of(key)[0:NE, 0:n_tok]))
                drop(key)
                for s in range(seqs):
                    span = slice(SEQ * s, SEQ * s + SEQ)
                    for _ in range(CAP // 8):
                        link(dve.max(top8[:, :], left[:, span]))
                        link(dve.match_replace(left[:, span], top8[:, :], left[:, span], -1.0))
                    link(dve.tensor_scalar(left[:, span], left[:, span], 0.0, None, ALU.is_lt))
                    link(dve.tensor_tensor_scan(affT[:, span], ones_row[:, 0:SEQ], left[:, span], 0.0, ALU.mult, ALU.add))
                    link(dve.tensor_tensor(picked[:, span], affT[:, span], left[:, span], ALU.mult))
                done("top", layer)
                key = ("posT", layer)
                dve.wait_ge(*full(key))
                link(dve.tensor_copy(posT[:, 0:L, :], bank_of(key)[:, 0:NE * L].rearrange("p (t e) -> p t e", e=NE)))
                drop(key)

                m, G = M[layer], experts_per_group(layer)
                W, n_sum = P // G, 2 * L
                link(dve.memset(moe_pick, 0.0))
                link(dve.memset(moe_pick_g, 0.0))
                link(dve.memset(acc[:, 0:n_sum, :], 0.0))
                dve.sem_inc(m["hid"], 2)
                dve.sem_inc(m["sum_free"], n_sum)
                with dve.Fori(0, NE // G) as i:
                    for s in range(seqs):
                        ts = slice(2 * s, 2 * s + 2)
                        full4 = [P, 2, G, CAP]
                        pos = posT[:, ts, bass.ds(i * G, G)].unsqueeze(3).to_broadcast(full4)
                        gts = aff[:, ts, bass.ds(i * G, G)].unsqueeze(3).to_broadcast(full4)
                        it = con("iota").unsqueeze(1).unsqueeze(1).to_broadcast(full4)
                        one = moe_pick[:, ts, :].rearrange("p t (e s k) -> p t e s k", e=G, s=seqs)[:, :, :, s, :]
                        oneg = moe_pick_g[:, ts, :].rearrange("p t (e s k) -> p t e s k", e=G, s=seqs)[:, :, :, s, :]
                        dve.tensor_tensor(one, pos, it, ALU.is_equal).then_inc(m["one"], 1)
                        dve.wait_ge(m["one"], seqs * i + s + 1)
                        ins = dve.tensor_tensor(oneg, one, gts, ALU.mult)
                    ins.then_inc(m["pick"], 1)
                    for h in range(2):
                        dve.wait_ge(m["xg_full"], 2 * i + h + 1)
                        for s in range(seqs):
                            shape = [P, 4, G, CAP]
                            src = bank[4 + h][:, :].rearrange("p (c e s k) -> p c e s k", c=4, e=G, s=seqs)[:, :, :, s, :]
                            tmp, dst = (v[:, 4 * h:4 * h + 4, :].rearrange("p c (e s k) -> p c e s k", e=G, s=seqs)[:, :, :, s, :] for v in (moe_tmp, moe_x))
                            a = gain[:, 1, 4 * h:4 * h + 4, s:s + 1].unsqueeze(3).to_broadcast(shape)
                            b = shift(1)[:, 4 * h:4 * h + 4, s:s + 1].unsqueeze(3).to_broadcast(shape)
                            dve.tensor_tensor(tmp, src, a, ALU.mult).then_inc(m["one2"], 1)
                            dve.wait_ge(m["one2"], 2 * seqs * i + seqs * h + s + 1)
                            ins = dve.tensor_tensor(dst, tmp, b, ALU.add)
                    ins.then_inc(m["xt"], 1)
                    for nb in range(2):
                        dve.wait_ge(m["silu"], 2 * i + nb + 1)
                        dve.wait_ge(m["blocks"], 6 * i + 2 * nb + 2)
                        dve.tensor_tensor(moe_h[:, 512 * nb:512 * nb + 512], bank[2 * nb + 1][:, :], moe_silu[:, nb, :], ALU.mult)\
                           .then_inc(m["hid"], 1)
                    for n in range(n_sum):
                        dve.wait_ge(m["sum_full"], n_sum * i + n + 1)
                        dve.tensor_tensor(acc[:, n, :], acc[:, n, :], bank[6 + n % 2][:, :], ALU.add).then_inc(m["sum_free"], 1)
                dve.wait_ge(*after("gates_bc", (layer, 1)))
                dve.wait_ge(m["sum_free"], n_sum * (NE // G + 1))
                for t in tiles:
                    a = acc[:, 2 * t:2 * t + 2, :].rearrange("p a b -> p (a b)")
                    link(dve.tensor_tensor(a, a, g_row[:, t // 2, :], ALU.mult))
                    dve.tensor_tensor(x[:, t, :], x[:, t, :], a, ALU.add).then_inc(*signal("x2", (layer, 1, t)))
                dve.wait_ge(*after("x2", (layer, 1, tiles[-1])))
            norm_rows("final", 0, range(T2))
            dve.wait_ge(*after("final_row_in", 0))
            for t in range(T2):
                link(dve.tensor_scalar(x[:, t, :], x[:, t, :], rstd[:, t:t + 1], None, ALU.mult))
                dve.tensor_tensor(x[:, t, :], x[:, t, :], g_row[:, 1, :], ALU.mult).then_inc(*signal("x_ready", ("final", t)))
    return marks.seen


def consts():
    c = np.zeros((P, NCONST), np.float32)

    def put(name, v):
        at, n = CONSTS[name]
        c[:v.shape[0], at:at + n] = v.reshape(v.shape[0], n)
    p = np.arange(P)
    put("ident", np.eye(P, dtype=np.float32))
    for name, r in (("rot32", 32), ("rot16", 16)):
        m = np.zeros((P, P), np.float32)
        lo = p[(p // r) % 2 == 0]
        m[lo + r, lo] = -1.0
        m[lo, lo + r] = 1.0
        put(name, m)
    put("blk64", (p[:, None] // 64 == p[None] // 64).astype(np.float32))
    put("ones", np.ones((P, P), np.float32))
    pos = np.arange(SEQ, dtype=np.float32)
    inv = np.float32(10000.0) ** (-np.arange(0, 64, 2, dtype=np.float32) / np.float32(64))
    ang = (pos[:, None] * inv[None]).astype(np.float32)
    ang = np.concatenate([ang, ang, ang, ang], 1).T
    put("cos1", np.cos(ang))
    put("sin1", np.sin(ang))
    inv = np.float32(10000.0) ** (-np.arange(16, dtype=np.float32) / np.float32(16))
    ar = (pos // GRID_W)[:, None] * inv
    ac = (pos % GRID_W)[:, None] * inv
    ang = np.concatenate([ar, ar, ac, ac] * 2, 1).astype(np.float32).T
    put("cos2", np.cos(ang))
    put("sin2", np.sin(ang))
    q, k = np.arange(SEQ).reshape(T2, P).T[:, :, None], np.arange(SEQ)[None, None]
    put("mlmask", np.stack([np.where(k <= q, 0, NEG), np.where(k >= q, 0, NEG)], 1).astype(np.float32))
    put("winmask", np.where(abs(q - k) <= 128, 0, NEG).astype(np.float32))
    start = np.clip(p % GRID_W - NA_COLS // 2, 0, GRID_W - NA_COLS)[:, None]
    kc = np.arange(GRID_W)[None]
    put("namask", np.where((kc >= start) & (kc < start + NA_COLS), 0, NEG).astype(np.float32))
    put("iota", np.tile(np.arange(1, 33, dtype=np.float32), (P, 1)))
    put("sel4", np.repeat(np.eye(4, dtype=np.float32), P, 1))
    return c


WEIGHTS = ("x", "mem", "even_w_in", "even_w_out", "odd_w_in", "odd_lambda", "odd_w_out", "mem_wq", "mem_wkv", "mem_wo",
           "ffn_w_gu", "ffn_w_down", "ln_g", "ln_b", "ctx_2", "ada_w_2", "w_in_2", "sink_2", "w_out_2", "router_w_2",
           "w_gate_2", "w_up_2", "w_down_2", "final_g_2")


def layout(a):
    def chunks(v):
        v = np.asarray(v)
        v = v.reshape(v.shape[:-1] + (-1, P))
        return np.moveaxis(v, -1, 0).reshape(P, -1)
    parts = {
        "conv": chunks(a["even_conv_w"][0]), "subln": chunks(a["odd_subln_g"]),
        "n1": chunks(a["norm1_g_2"]), "n2": chunks(a["norm2_g_2"]),
        "cc": np.stack([chunks(a["c_2"][0]), chunks(a["c_ctx_2"])], -1).reshape(P, 16),
        "conv_a": chunks(a["conv_a_w_2"]), "conv_b": chunks(a["conv_b_w_2"]), "conv_bb": chunks(a["conv_b_b_2"]),
        "cln_g": chunks(a["conv_ln_g_2"]), "cln_b": chunks(a["conv_ln_b_2"]),
        "qn": np.tile(a["q_norm_g_2"], (1, 2)).T, "kn": np.tile(a["k_norm_g_2"], (1, 2)).T,
        "ada_b": chunks(a["ada_b_2"]),
    }
    first = NA_ROWS - ROWS
    rpb = np.pad(np.asarray(a["even_rpb"][0])[:, first:first + 2 * ROWS - 1], ((0, 0), (0, 0), (GRID_W - NA_COLS, GRID_W - NA_COLS)))
    windows = np.stack([rpb[:, :, GRID_W - 1 - q:2 * GRID_W - 1 - q] for q in range(GRID_W)])
    return {"cols": np.ascontiguousarray(np.concatenate([parts[k] for k in COLS], 1)),
            "gate_b": np.ascontiguousarray(np.asarray(a["even_gate_b"]).reshape(4, 4).T),
            "rpb_windows": windows, "consts": consts()}


def program(nc, shapes, table, stop=None):
    w = {n: nc.dram_tensor(f"in_{n}", s, F32, kind="ExternalInput").ap() for n, s in shapes.items()}
    out = nc.dram_tensor("out", (1, SEQ, D), F32, kind="ExternalOutput").ap()
    return build(nc, w, out, table, stop)


def kernel(stop=None, **inputs):
    import concourse.bacc as bacc
    from concourse.bass_utils import run_bass_kernel_spmd
    arrays = {n: np.ascontiguousarray(inputs[n]) for n in WEIGHTS}
    arrays.update(layout(inputs))
    shapes = {n: v.shape for n, v in arrays.items()}
    table = program(bacc.Bacc("TRN2", target_bir_lowering=False, num_devices=1), shapes, None, stop)
    nc = bacc.Bacc("TRN2", target_bir_lowering=False, num_devices=1)
    program(nc, shapes, table, stop)
    r = run_bass_kernel_spmd(nc, [{f"in_{n}": v for n, v in arrays.items()}], core_ids=[0])
    return r.results[0]["out"]
```

```python
import math
from contextlib import ExitStack

import numpy as np

import concourse.bass as bass
from concourse import mybir

F32 = mybir.dt.float32
F32R = mybir.dt.float32r
ALU = mybir.AluOpType
ACT = mybir.ActivationFunctionType
AX = mybir.AxisListType

P = 128
D = 1024
KC = D // P
SEQ = 256
T2 = SEQ // P
DEPTH = 2
A_HEADS, A_CONV = 4, 5
B_HEADS = 8
GRID_W, NA_ROWS, NA_COLS = 64, 8, 16
ROWS = SEQ // GRID_W
C_HEADS = 8
X_HEADS, X_HD = 4, 256
FFN = 2816
FC = FFN // P
ALPHA = (2 * DEPTH) ** 0.25
LN_EPS = 1e-5
LAM_INIT = 0.8 - 0.6 * math.exp(-0.3)
NEG = -1e30
EPS = 1e-6
HD = 64
N_HEADS = 4
NE = 16
CAP = 32
CONV_B = 31
PAD_B = CONV_B // 2
IN2_BLOCKS = (("b", 768, 1280), ("d", 1792, 2304), ("c", 1280, 1792), ("ab", 0, 512), ("ah", 512, 768))
UK, UN = 4, 512
RING = 12
MEM_HI, X_HI, HI_AT, HI_SLOTS, RAW_AT, RAW_SLOTS = 0, 1, 2, 4, 6, 6

COLS = {}
_at = 0
for _name, _n in (("conv", 40), ("subln", 1), ("n1", 16), ("n2", 16), ("cc", 16), ("conv_a", 12),
                  ("conv_b", 124), ("conv_bb", 4), ("cln_g", 4), ("cln_b", 4), ("qn", 2), ("kn", 2), ("ada_b", 96)):
    COLS[_name] = (_at, _n)
    _at += _n
NCOLS = _at
CONSTS = {}
_at = 0
for _name, _n in (("ident", 128), ("rot32", 128), ("rot16", 128), ("blk64", 128), ("ones", 128), ("cos1", 256),
                  ("sin1", 256), ("cos2", 256), ("sin2", 256), ("mlmask", 1024), ("winmask", 512),
                  ("namask", 64), ("iota", 32), ("sel4", 512)):
    CONSTS[_name] = (_at, _n)
    _at += _n
NCONST = _at

EVENTS = ("const_in", "ident_in", "cols_in", "gate_b_in", "gate_w_in", "sink_in", "x_in", "mem_in", "ctx_in", "nab_in", "ln_row_in", "final_row_in", "xT", "proj",
          "var", "rstd", "x_ready", "x2", "conv", "silu", "gate_abs", "gate_exp", "gate_ln1", "gate_ln",
          "gate_rows", "gate_cols", "decay", "decay_exp", "nmax", "probs", "probs_exp",
          "probsT", "oT", "rope_out", "sq", "rms", "hid", "lam_in", "lam_sums", "lam_exps", "zero", "ssq", "sc_silu",
          "mods_rows", "mods", "diag", "gates_bc", "u_in", "uconv", "u_norm", "yb", "xhat", "hT", "hT_odd", "aff_exp", "w_hi", "w_lo", "xT_hi", "y_hi", "y_lo", "h_full", "h_hi", "gate_w_hi",
          "aff", "top", "out_dma", "ab_in", "logit_max", "router_in", "u_in2", "uvar", "ssq2", "short", "ssq_act", "cleared")


def weight_plan(w):
    units = []

    def block(key, mat, n0, n1, kc=KC):
        m = mat.rearrange("(c p) n -> p c n", p=P)
        for h in range(0, kc, UK):
            units.append((key + (h // UK,), m[:, h:min(h + UK, kc), n0:n1]))

    def matrix(key, mat, kc=KC):
        n = mat.shape[1]
        for b in range(0, n, UN):
            block(key + (b // UN,), mat, b, min(b + UN, n), kc)

    def ada_half(layer, g, h):
        ada = w["ada_w_2"][layer].rearrange("(c p) n -> p c n", p=P)
        for j in range(4):
            c = 4 * g + j
            units.append((("ada", layer, g, h, j), ada[:, UK * h:UK * h + UK, UN * c:UN * c + UN]))

    e = w["even_w_in"][0]
    for b, n0 in enumerate((0, 512, 1024, 1536, 2064, 2576, 3088)):
        block(("even_in", b), e, n0, n0 + 512)
    matrix(("even_out",), w["even_w_out"][0])
    for layer in range(DEPTH):
        if layer == 1:
            matrix(("odd_in",), w["odd_w_in"][0])
            matrix(("odd_out",), w["odd_w_out"][0])
        matrix(("mem_kv", layer), w["mem_wkv"][layer])
        matrix(("mem_q", layer), w["mem_wq"][layer])
        for h in range(2):
            ada_half(layer, 0, h)
        matrix(("mem_o", layer), w["mem_wo"][layer])
        for b in range(0, FFN, UN):
            n = min(UN, FFN - b)
            block(("gate", layer, b // UN), w["ffn_w_gu"][layer], b, b + n)
            block(("up", layer, b // UN), w["ffn_w_gu"][layer], FFN + b, FFN + b + n)
            if b // UN < 4:
                ada_half(layer, 1 + b // UN // 2, b // UN % 2)
        matrix(("down", layer), w["ffn_w_down"][layer], FC)
    for layer in range(DEPTH):
        for b, n0, n1 in IN2_BLOCKS:
            block(("in2", layer, b), w["w_in_2"][layer], n0, n1)
        matrix(("out2", layer), w["w_out_2"][layer])
        units.append((("experts", layer), None))
    return units


def experts_per_group(layer):
    return 2 if layer == 0 else 4


def moe_units(layer):
    g = experts_per_group(layer)
    order = []
    for b in range(2):
        for name in ("w_gate_2", "w_up_2"):
            order += [(name, b, h, j) for h in range(2) for j in range(g)]
    for b in range(2):
        order += [("w_down_2", b, h, j) for h in range(2) for j in range(g)]
    return order


class Marks:

    def __init__(self, table):
        self.table, self.seen, self.count = table, {}, {}

    def mark(self, kind, key, n=1):
        self.count[kind] = self.count.get(kind, 0) + n
        assert (kind, key) not in self.seen, (kind, key)
        self.seen[(kind, key)] = self.count[kind]

    def value(self, kind, key):
        return 1 if self.table is None else self.table[(kind, key)]


def build(nc, w, out, table, stop=None):
    marks = Marks(table)
    units = weight_plan(w)
    first2 = [key[0] for key, _ in units].index("in2")
    split_units = [u for u in range(first2) if units[u][0][0] != "ada"]
    place = {u: i for i, u in enumerate(split_units)}
    unit_at, n = {}, 0
    for key, _ in units:
        unit_at[key] = n
        n += 1 if key[0] != "experts" else len(moe_units(key[1])) * (NE // experts_per_group(key[1]))

    with ExitStack() as ctx:
        def sb(name, shape):
            return ctx.enter_context(nc.sbuf_tensor(name, shape, F32))

        def sem(name):
            return ctx.enter_context(nc.semaphore(name))

        def both(name, shape):
            with nc.sbuf_tensor(name, shape, F32) as plain:
                pass
            return plain, ctx.enter_context(nc.sbuf_tensor(name + "_r", shape, F32R))

        ring, ring_r = both("ring", [P, RING, UK, UN])
        const = sb("const", [P, NCONST])
        cols = sb("cols", [P, NCOLS])
        router = sb("router", [P, DEPTH, KC, NE])
        gate_b = sb("gate_b", [4, 4])
        sink = sb("sink", [P, DEPTH, N_HEADS])
        x, x_r = both("x", [P, 4, D])
        xT, xT_r = both("xT", [P, KC, 2 * SEQ])
        arena, arena_r = both("arena", [P, 15488])
        stats = sb("stats", [P, 4, 2, 6])
        mv = sb("mv", [P, 4, 2])
        std = sb("std", [P, 4])
        rstd = sb("rstd", [P, 4])
        small = sb("small", [P, 2, 16])
        lam = sb("lam", [P, 8])
        aff = sb("aff", [P, T2, 2, 32])
        posT = sb("posT", [P, T2, 2, 32])
        bank = [ctx.enter_context(nc.psum_tensor(f"bank{i}", [P, 512], F32)) for i in range(8)]

        def aff_of(seqs):
            return aff[:, :, 0:seqs, 0:NE].rearrange("p t s e -> p s t e")

        def con(name):
            at, n = CONSTS[name]
            return const[:, at:at + n]

        def col(name, i=0, n=1):
            return cols[:, COLS[name][0] + i:COLS[name][0] + i + n]

        def area(at, *shape, of=arena):
            n = int(np.prod(shape))
            v = of[:, at:at + n]
            if len(shape) == 1:
                return v
            names = "abcd"[:len(shape)]
            return v.rearrange(f"p ({' '.join(names)}) -> p {' '.join(names)}", **dict(zip(names, shape)))

        ident = con("ident")
        decay = [area(1024, 2, 2, 256), area(3072, 2, 2, 256)]
        nab = area(4096, T2, B_HEADS, 256)
        ln_row = area(4096, 2, D)
        qk_pad = area(8192, 8, SEQ + 4)
        b_qkT = area(8192, 8, SEQ)
        qkT = area(10272, 8, SEQ)
        a_v = area(12320, T2, 512)
        a_oT = area(13344, 4, SEQ)
        b_v = area(14368, T2, 512)
        y1T = x[:, 2:4, :].rearrange("p a (b c) -> p (a b) c", c=SEQ)
        mem_rows = x[:, 2:4, :]
        def real(slot):
            return ring_r[:, slot].rearrange("p a b -> p (a b)").rearrange("p (c n) -> p c n", c=KC)
        m_hi, x_hi = real(MEM_HI), real(X_HI)
        x_lo, m_lo = xT_r[:, :, 0:SEQ], xT_r[:, :, SEQ:2 * SEQ]
        y1_lo = x_r[:, 2:4, :].rearrange("p a (b c) -> p (a b) c", c=SEQ)
        qT = area(8192, 8, SEQ)
        kT = area(10240, 8, SEQ)
        v_rows = area(12288, T2, D)
        raw = area(14336, 2, SEQ)
        rcos = area(14848, 2, SEQ)
        hT = area(8192, FC, SEQ)
        hT_lo = area(8192, FC, SEQ, of=arena_r)
        hT_hi = [area(0, 16, SEQ, of=arena_r), area(6144, FC - 16, SEQ, of=arena_r)]
        hsilu = area(13824, 2, 512)
        g2, g3 = (x[0:4, t, :].rearrange("p (s k) -> p s k", k=SEQ) for t in (2, 3))
        g_in, g_forget, g_c, g_tmp = g2[:, 0:2], g2[:, 2:4], g3[:, 0:2], g3[:, 2:4]
        g_max = area(0, 4, SEQ)[0:4]
        lam_raw = area(7680, 4, 64)
        dvar = area(6144, C_HEADS, SEQ)
        gate_w = area(2304, KC, 16)
        gate_w_lo, gate_w_hi = (area(at, KC, 16, of=arena_r) for at in (2304, 2432))
        g_one = area(2048, SEQ)[0:4]

        gcols = sb("gcols", [P, 2, 2, 2, 4])

        g_row = area(4096, 2, D)
        y_lo = area(6144, 4, 2 * SEQ)
        y_hi = xT[:, 4:8, :]
        qk = area(8192, 8, 2 * SEQ)
        xhat = area(8192, 4, D)
        v2 = area(12288, 4, 2, P)
        z_pad = area(13312, 2, 2, SEQ + 2)
        u_pad = area(14344, 2, 2, SEQ + 2 * PAD_B)
        u_rows = area(14344, 4, SEQ)
        yb = area(14344, 2, 2 * SEQ)
        sq = area(0, 2, 2 * SEQ)
        qvar = area(1024, 2, 2 * SEQ)
        rtmp = area(2048, 2, SEQ)
        btmp = area(2048, 2, 512)
        scT = con("mlmask")[:, 0:256].rearrange("p (c s) -> p c s", c=KC)
        mods_rows = [con("mlmask")[:, 256:768], con("sel4")]
        mods_all = con("mlmask")[:, 768:960].rearrange("p (l k s) -> p l k s", l=DEPTH, k=48)
        diag = area(2048, KC, P)
        sig = area(3072, 2, 2 * SEQ)
        gain = sb("gain", [P, 2, KC, 2])
        lmax = sb("lmax", [P, 2, 4])
        top8 = sb("top8", [64, 8])
        affT, left, picked, ones_row = (area(SEQ * i, SEQ)[0:64] for i in range(4))
        moe_x, moe_tmp = area(0, KC, P), area(1024, KC, P)
        moe_h, moe_hT = area(2048, D), area(3072, KC, P)
        moe_y, moe_g = area(6144, D), area(7168, 4 * P)
        moe_pick, moe_pick_g = area(7680, 4, P), area(12288, 4, P)
        moe_silu = area(12800, 2, 512)
        acc = xT[:, :, :].rearrange("p a (b c) -> p (a b) c", c=512)

        def scalar_tiles(layer, kind, ts):
            return (2, 3, 0) if (layer, kind) == (0, 0) else ts[:len(ts) // 2]

        def shift(layer, k):
            return mods_all[:, layer, 24 * k:24 * k + 8, :]

        LO, HI = 0, 1
        S = {k: sem(k) for k in EVENTS}
        MOE = ("pick", "xg_full", "xt", "g_full", "g_sb", "blocks", "halves", "silu", "hid", "ht_full", "ht_sb", "y_sb",
               "sum_full", "sum_free", "one", "one2", "loads")
        M = [{k: sem(f"moe{layer}_{k}") for k in MOE} for layer in range(DEPTH)]
        bank_full = [sem(f"bank_full{i}") for i in range(8)]
        bank_free = [sem(f"bank_free{i}") for i in range(8)]
        ring_in = [sem(f"ring_in{i}") for i in range(RING)]
        raw_in = [sem(f"raw_in{i}") for i in range(RAW_SLOTS)]
        half_read = sem("half_read")
        dve_step = sem("dve_step")
        act_step = sem("act_step")
        pool_step = sem("pool_step")

        def signal(kind, key, n=1):
            marks.mark(kind, key, n)
            return S[kind], n

        def after(kind, key):
            return S[kind], marks.value(kind, key)

        def slot_of(u):
            if u < first2:
                return RAW_AT + u % RAW_SLOTS, raw_in[u % RAW_SLOTS], 16 * (u // RAW_SLOTS + 1)
            v = u - first2
            return v % RING, ring_in[v % RING], 16 * (v // RING + 1)

        def hi_of(u):
            return ring_r[:, HI_AT + place[u] % HI_SLOTS]

        def hid_T(c):
            return (hT_hi[0][:, c] if c < 16 else hT_hi[1][:, c - 16]), hT_lo[:, c]

        fills, filled, halves_read = {}, [0] * 8, [0]
        last_fill, last_reader, last_out = [None], {}, {}

        def full(key):
            b, n = fills[key]
            return bank_full[b], n

        def freed(key):
            return bank_free[fills[key][0]], 1

        def bank_of(key):
            return bank[fills[key][0]]

        block = ctx.enter_context(nc.Block())

        def unit(stage, i, q, k, scale, v, y, keys=256, bias=None, sink_at=None, size=512, parts=None):
            return dict(key=(stage, i), n=i, q=q, k=k, scale=scale, v=v, y=y, keys=keys, bias=bias, sink=sink_at, size=size, parts=parts)

        def half(t, c, j, n0=0, n=SEQ):
            return t[64 * j:64 * j + 64, c, n0:n0 + n]

        na_units = [unit("na", h, [half(b_qkT, h // 2, h % 2)], [[half(b_qkT, 4 + h // 2, h % 2)]], 64 ** -0.5,
                         [b_v[:, kb, 64 * h:64 * h + 64] for kb in range(2)],
                         [(y1T[64 * (h % 2):64 * (h % 2) + 64, 4 + h // 2, :], 64 * (h % 2))],
                         bias=nab[:, :, h, :], parts=[tuple(v[64 * (h % 2):64 * (h % 2) + 64, 4 + h // 2] for v in (x_hi, y1_lo))]) for h in range(B_HEADS)]

        def probs_of(u):
            return area(u["n"] % 2 * u["size"], 2, u["keys"])

        def probsT_of(u):
            return area(2048 + u["n"] % 2 * u["size"], u["keys"] // P, 256)

        ml_units = [unit("ml", h, None, None, P ** -0.5, [a_v[:, kb, P * h:P * h + P] for kb in range(2)],
                         [(y1T[:, h, :], 0)], parts=[(x_hi[:, h], y1_lo[:, h])]) for h in range(A_HEADS)]
        diff_units = [unit("diff", h, None, None, 64 ** -0.5, [v_rows[:, kb, P * h:P * h + P] for kb in range(2)],
                           [(y1T[:, h, :], 0)]) for h in range(C_HEADS)]

        def diff_probs(u, m):
            return area(1024 * m + 512 * (u["n"] % 2), 2, SEQ)

        def block2_units(layer):
            us = []
            for s in range(2 if layer == 0 else 1):
                for kind in range(2):
                    for h in range(N_HEADS):
                        kv = h // 2
                        tok = [0, SEQ] if s == 0 else [SEQ]
                        us.append(unit(f"mix{layer}", len(us), [half(qk, 4 * kind + h % 2, kv, SEQ * s)],
                                       [[half(qk, 4 * kind + 2, kv, t)] for t in tok], HD ** -0.5,
                                       [v2[:, t // P + i, kind, 64 * kv:64 * kv + 64] for t in tok for i in range(2)],
                                       [(y_hi[64 * (h % 2):64 * (h % 2) + 64, 2 * kind + h // 2, SEQ * s:SEQ * s + SEQ], 64 * (h % 2))],
                                       keys=256 * len(tok), size=1024, bias=con("winmask").rearrange("p (t k) -> p t k", t=2)
                                       if (kind, s) == (0, 0) else None, sink_at=sink[:, layer, h:h + 1] if kind == 0 else None))
            return us

        def turned(u):
            stage, n = u["key"][0], u["n"] - 2
            wide = stage[:3] == "mix" and n < 2 * N_HEADS
            return ("pT", stage, n, 1 if wide else 0)

        CHUNKS = dict(ab0=0, ab1=128, ac0=256, ac1=384, ah0=512, ah1=640, bv0=768, bv1=896, bg0=1024, bg1=1152)
        QK_AT = dict(cq0=0, cq1=1, ck0=2, dq0=4, dq1=5, dk0=6)

        def mem_units(layer):
            return [unit(f"mem{layer}", h, [qT[:, 2 * h, :], qT[:, 2 * h + 1, :]],
                         [[kT[:, 2 * h, :], kT[:, 2 * h + 1, :]]], X_HD ** -0.5,
                         [v_rows[:, kb, X_HD * h:X_HD * h + X_HD] for kb in range(2)],
                         [(y1T[:, 2 * h, :], 0), (y1T[:, 2 * h + 1, :], 0)], parts=[(x_hi[:, c], y1_lo[:, c]) for c in (2 * h, 2 * h + 1)]) for h in range(X_HEADS)]

        @block.tensor
        def _(pe):
            def open_bank(key, b):
                fills[key] = (b, filled[b] + 1)
                if filled[b]:
                    pe.wait_ge(bank_free[b], filled[b])
                filled[b] += 1
                return bank[b]

            dense = [0]

            def dense_bank(key):
                dense[0] += 1
                return open_bank(key, dense[0] % 4)

            def weights(key):
                slot, loaded, n = slot_of(unit_at[key])
                pe.wait_ge(loaded, n)
                return ring[:, slot]

            def w_block(key, kc=KC):
                halves = [weights(key + (h,)) for h in range(-(-kc // UK))]
                return lambda c: halves[c // UK][:, c % UK]

            def filled_now(key):
                b, n = fills[key]
                last_fill[0] = (bank_full[b], n)
                return bank_full[b], 1

            def read(key, n):
                for h in range(n):
                    last_reader[unit_at[key + (h,)]] = last_fill[0]

            def split_weights(key, h):
                u = unit_at[key + (h,)]
                pe.wait_ge(*after("w_lo", u))
                return hi_of(u), ring_r[:, slot_of(u)[0]]

            def passes(dst, w_parts, x_parts, first, last):
                (w_hi, w_lo), (v_hi, v_lo) = w_parts, x_parts
                pe.matmul(dst, w_hi, v_hi, start=first, stop=False)
                pe.matmul(dst, w_lo, v_hi, start=False, stop=False)
                return pe.matmul(dst, w_hi, v_lo, start=False, stop=last)

            def half_through(key, h, mm):
                halves_read[0] += 1
                last_reader[unit_at[key + (h,)]] = (half_read, halves_read[0])
                mm.then_inc(half_read, 1)

            def project_T(key, src, width=512):
                out_banks = [dense_bank(key + ("out", j)) for j in range(width // 256)]
                last_out[key] = key + ("out", len(out_banks) - 1)
                for h in range(2):
                    hi, lo = split_weights(key, h)
                    for j, b in enumerate(out_banks):
                        for m in range(2):
                            c0 = (2 * j + m) * P
                            for c in range(UK):
                                mm = passes(b[:, SEQ * m:SEQ * m + SEQ], (hi[:, c, c0:c0 + P], lo[:, c, c0:c0 + P]), src(UK * h + c),
                                            h == m == c == 0, h == m == 1 and c == UK - 1)
                        if h == 1:
                            mm.then_inc(*filled_now(key + ("out", j)))
                    if h == 0:
                        half_through(key, 0, mm)
                last_reader[unit_at[key + (1,)]] = last_fill[0]

            def project_rows(key, src, kc=KC):
                out_banks = [dense_bank(key + ("out", t)) for t in range(T2)]
                last_out[key] = key + ("out", T2 - 1)
                for h in range(-(-kc // UK)):
                    hi, lo = split_weights(key, h)
                    for t, b in enumerate(out_banks):
                        for c in range(UK * h, min(UK * h + UK, kc)):
                            mm = passes(b[:, :], tuple(v[:, t * P:t * P + P] for v in src(c)), (hi[:, c - UK * h], lo[:, c - UK * h]),
                                        c == 0, c == kc - 1)
                        if c == kc - 1:
                            mm.then_inc(*filled_now(key + ("out", t)))
                    if c < kc - 1:
                        half_through(key, h, mm)
                last_reader[unit_at[key + (h,)]] = last_fill[0]

            def project_rows2(key, src, tiles):
                wb = w_block(key)
                for t in tiles:
                    b = dense_bank(key + ("out", t))
                    for c in range(KC):
                        mm = pe.matmul(b[:, :], src(c, t), wb(c), start=(c == 0), stop=(c == KC - 1))
                    mm.then_inc(*filled_now(key + ("out", t)))
                read(key, 2)

            def to_T(key, rows, tiles):
                for t in tiles:
                    for h in range(2):
                        b = dense_bank(key + (t, h))
                        for c in range(4):
                            mm = pe.transpose(b[:, P * c:P * c + P], rows(t)[:, (4 * h + c) * P:(4 * h + c + 1) * P], ident)
                        mm.then_inc(*filled_now(key + (t, h)))

            def x_parts(c):
                return x_hi[:, c], x_lo[:, c]

            def m_parts(c):
                return m_hi[:, c], m_lo[:, c]

            def y_parts(c):
                return x_hi[:, c], y1_lo[:, c]

            def scores(u):
                parts = 1 if u["keys"] == 256 else 2
                for part in range(parts):
                    b = open_bank(("s",) + u["key"] + (part,), 4 + u["n"] % 2 if parts == 1 else (4, 2)[u["n"] % 2] + part)
                    for t in (range(2) if parts == 1 else [part]):
                        for kb in range(len(u["k"])):
                            at = 256 * (t if parts == 1 else kb)
                            nk = len(u["k"][kb])
                            for c in range(nk):
                                mm = pe.matmul(b[:, at:at + 256], u["q"][c][:, t * P:t * P + P], u["k"][kb][c],
                                               start=(c == 0), stop=(c == nk - 1))
                    mm.then_inc(bank_full[fills[("s",) + u["key"] + (part,)][0]], 1)

            def turn(u):
                pe.wait_ge(*after("probs", u["key"]))
                pr = probs_of(u)
                for part in range(u["keys"] // 256):
                    key = ("pT",) + u["key"] + (part,)
                    b = open_bank(key, (6, 1)[part])
                    for kb in range(2):
                        for t in range(2):
                            mm = pe.transpose(b[:, 256 * kb + P * t:256 * kb + P * t + P],
                                              pr[:, t, (2 * part + kb) * P:(2 * part + kb + 1) * P], ident)
                    mm.then_inc(*filled_now(key))

            def values(u):
                pe.wait_ge(*after("probsT", u["key"]))
                b = open_bank(("o",) + u["key"], 7)
                n = u["keys"] // P
                for i, (_, p0) in enumerate(u["y"]):
                    dv = 64 if u["y"][i][0].shape[0] == 64 else P
                    for kb in range(n):
                        mm = pe.matmul(b[p0:p0 + dv, 256 * i:256 * i + 256], u["v"][kb][:, i * dv:(i + 1) * dv],
                                       probsT_of(u)[:, kb, :], start=(kb == 0), stop=(kb == n - 1))
                mm.then_inc(bank_full[7], 1)

            def attend(us, score=scores):
                for u in us[:2]:
                    score(u)
                for i in range(len(us) + 1):
                    if i + 2 < len(us):
                        score(us[i + 2])
                    if i < len(us):
                        turn(us[i])
                    if i:
                        values(us[i - 1])

            pe.wait_ge(*after("ident_in", 0))
            pe.wait_ge(*after("x_in", 0))
            to_T(("xT", "in"), lambda t: x[:, t, :], range(T2))
            pe.wait_ge(*after("xT", ("in", T2 - 1, 1)))

            for b in (0, 1):
                project_T(("even_in", b), x_parts)
                if b == 0:
                    pe.wait_ge(*after("mem_in", 0))
                    to_T(("memT",), lambda t: mem_rows[:, t, :], range(T2))
            pe.wait_ge(*after("gate_w_hi", 0))
            for kind in range(2):
                g = dense_bank(("gates", kind))
                for d in range(2):
                    for c in range(KC):
                        at = slice(8 * kind + 4 * d, 8 * kind + 4 * d + 4)
                        mm = passes(g[0:4, 256 * d:256 * d + 256], (gate_w_hi[:, c, at], gate_w_lo[:, c, at]), x_parts(c),
                                    c == 0, c == KC - 1)
                mm.then_inc(bank_full[fills[("gates", kind)][0]], 1)
            project_rows(("even_in", 2), x_parts)
            project_T(("even_in", 3), x_parts)
            pe.wait_ge(*after("gate_rows", 0))
            g = open_bank(("gate_cols",), 7)
            for kind in range(2):
                for d in range(2):
                    for t in range(2):
                        at = 4 * (4 * kind + 2 * d + t)
                        mm = pe.transpose(g[:, at:at + 4], g_max[:, 2 * kind + d, t * P:t * P + P], ident[0:4, 0:4])
            mm.then_inc(bank_full[7], 1)
            def mlstm_scores(h):
                b = open_bank(("cb", h), 6)
                for d in range(2):
                    mm = pe.matmul(b[:, 256 * d:256 * d + 256], con("sel4")[0:4, P * h:P * h + P], g_c[:, d, :],
                                   start=True, stop=True)
                mm.then_inc(bank_full[6], 1)
                if h == 0:
                    pe.wait_ge(*after("silu", 7))
                b = open_bank(("s", "ml", h, 0), 4 + h % 2)
                for t in range(2):
                    mm = pe.matmul(b[:, 256 * t:256 * t + 256], qkT[:, h, t * P:t * P + P], qkT[:, 4 + h, :], start=True, stop=True)
                mm.then_inc(bank_full[4 + h % 2], 1)

            project_T(("even_in", 4), x_parts)
            pe.wait_ge(*after("const_in", 0))
            mlstm_scores(0)
            mlstm_scores(1)
            project_T(("even_in", 5), x_parts)
            turn(ml_units[0])
            mlstm_scores(2)
            project_rows(("even_in", 6), x_parts)
            values(ml_units[0])
            turn(ml_units[1])
            mlstm_scores(3)
            values(ml_units[1])
            for u in ml_units[2:]:
                turn(u)
                values(u)
            pe.wait_ge(*after("proj", ("even_in", 6, "out", 1)))
            attend(na_units)
            pe.wait_ge(*after("oT", ("na", B_HEADS - 1)))

            def out_proj(key, kc=KC, src=y_parts):
                for nb in range(2):
                    project_rows(key + (nb,), src, kc)

            def norm_T(i):
                for t in range(T2):
                    pe.wait_ge(*after("x_ready", (i, t)))
                    to_T(("xT", i), lambda t: x[:, t, :], [t])

            def ada_rows(l, g, h):
                key = ("ada", l, g)
                if h == 1:
                    b = bank_of(key)
                else:
                    b = open_bank(key, 5 + g) if g else dense_bank(key)
                ws = [weights(key + (h, j)) for j in range(4)]
                for k in range(UK):
                    for j in range(4):
                        mm = pe.matmul(b[32 * j:32 * j + 32, :], scT[:, UK * h + k, :], ws[j][:, k],
                                       start=(h == 0 and k == 0), stop=(h == 1 and k == UK - 1))
                if h == 0:
                    half_through(("ada", l, g, 0), 3, mm)
                else:
                    mm.then_inc(*filled_now(key))
                for j in range(4):
                    last_reader[unit_at[key + (h, j)]] = last_fill[0] if h else (half_read, halves_read[0])

            def ada_T(l, g):
                pe.wait_ge(*after("mods_rows", (l, g)))
                b = dense_bank(("modsT", l, g))
                for q in range(4):
                    mm = pe.transpose(b[:, P * q:P * q + P], mods_rows[g % 2][:, P * q:P * q + P], ident)
                mm.then_inc(*filled_now(("modsT", l, g)))

            out_proj(("even_out",))
            for layer in range(DEPTH):
                if layer == 1:
                    pe.wait_ge(*after("xT", (2, T2 - 1, 1)))
                    for b in range(4):
                        project_T(("odd_in", b), x_parts)
                        for j in range(2):
                            for m in range(2):
                                c = 4 * b + 2 * j + m
                                pe.wait_ge(*after("proj", ("raw", c)))
                                r = open_bank(("rot", c), 4 + c % 2)
                                pe.matmul(r[:, 0:SEQ], con("rot32"), raw[:, c % 2, :], start=True, stop=True)\
                                  .then_inc(bank_full[4 + c % 2], 1)
                    for b in (4, 5):
                        project_rows(("odd_in", b), x_parts)
                    pe.wait_ge(*after("rope_out", 15))
                    pe.wait_ge(*after("proj", ("odd_in", 5, "out", 1)))

                    def diff_scores(u):
                        for m in range(2):
                            h = u["n"]
                            b = open_bank(("s",) + u["key"] + (m,), (4, 2)[h % 2] + m)
                            for t in range(2):
                                mm = pe.matmul(b[:, 256 * t:256 * t + 256], half(qT, h, m)[:, t * P:t * P + P],
                                               half(kT, h, m), start=True, stop=True)
                            mm.then_inc(*filled_now(("s",) + u["key"] + (m,)))

                    def square_sums(u):
                        pe.wait_ge(*after("ssq", u["n"]))
                        b = open_bank(("ss", u["n"]), u["n"] % 2)
                        pe.matmul(b[:, 0:SEQ], con("ones"), raw[:, u["n"] % 2, :], start=True, stop=True)\
                          .then_inc(*filled_now(("ss", u["n"])))
                    for u in diff_units[:2]:
                        diff_scores(u)
                    for i in range(C_HEADS + 2):
                        if i + 2 < C_HEADS:
                            diff_scores(diff_units[i + 2])
                        if i < C_HEADS:
                            turn(diff_units[i])
                        if i >= 2:
                            square_sums(diff_units[i - 2])
                        if 0 <= i - 1 < C_HEADS:
                            values(diff_units[i - 1])
                    pe.wait_ge(*after("y_lo", ("diff", C_HEADS - 1)))
                    out_proj(("odd_out",))
                n0 = 3 * layer
                if layer == 0:
                    pe.wait_ge(*after("xT", ("mem", T2 - 1, 1)))
                for b in range(2):
                    project_T(("mem_kv", layer, b), m_parts)
                for b in range(2, 4):
                    project_rows(("mem_kv", layer, b), m_parts)
                norm_T(n0)
                pe.wait_ge(*after("xT", (n0, T2 - 1, 1)))
                for b in range(2):
                    project_T(("mem_q", layer, b), x_parts)
                if layer == 0:
                    pe.wait_ge(*after("sc_silu", 0))
                ada_rows(layer, 0, 0)
                pe.wait_ge(*after("proj", ("mem_q", layer, 1, "out", 1)))
                attend(mem_units(layer))
                ada_rows(layer, 0, 1)
                pe.wait_ge(*after("oT", (f"mem{layer}", X_HEADS - 1)))
                out_proj(("mem_o", layer))
                norm_T(n0 + 1)
                pe.wait_ge(*after("xT", (n0 + 1, T2 - 1, 1)))
                for b in range(-(-FFN // UN)):
                    width = min(UN, FFN - b * UN)
                    project_T(("gate", layer, b), x_parts, width)
                    project_T(("up", layer, b), x_parts, width)
                    if b < 4:
                        ada_rows(layer, 1 + b // 2, b % 2)
                    if b in (0, 2):
                        ada_T(layer, b // 2)
                pe.wait_ge(*after("hid", (layer, FC // 2 - 1)))
                ada_T(layer, 2)
                out_proj(("down", layer), FC, hid_T)
                if layer == 0:
                    norm_T(n0 + 2)

            if stop:
                return
            for layer in range(DEPTH):
                seqs = 2 if layer == 0 else 1
                n_tok = SEQ * seqs
                tiles = range(2 * seqs)

                def gate_rows_of(kind):
                    for s in range(seqs):
                        pe.wait_ge(*after("diag", (layer, kind, s)))
                        for h in range(2):
                            b = dense_bank(("gbc", layer, kind, s, h))
                            pe.matmul(b[:, :], con("ones"), diag[:, 4 * h:4 * h + 4, :].rearrange("p a b -> p (a b)"),
                                      start=True, stop=True).then_inc(*filled_now(("gbc", layer, kind, s, h)))

                def hidden_T(kind, ts, use=None):
                    for t in ts:
                        pe.wait_ge(*after("xhat", (layer, kind, t)))
                    for c in range(KC):
                        b = dense_bank(("h", layer, kind, c))
                        for t in ts:
                            mm = pe.transpose(b[:, P * t:P * t + P], xhat[:, t, P * c:P * c + P], ident)
                        mm.then_inc(*filled_now(("h", layer, kind, c)))
                        if use and c >= 3:
                            use(c - 3)
                    if use:
                        for c in range(KC - 3, KC):
                            mm = use(c)
                        mm.then_inc(*filled_now(("logits", layer)))

                hidden_T(0, range(4))
                pe.wait_ge(*after("hT", (layer, 0, KC - 2)))
                pe.wait_ge(*after("hT_odd", (layer, 0, KC - 1)))

                def chunk(name, wb, at, n=n_tok):
                    b = dense_bank(("c", layer, name))
                    for c in range(KC):
                        mm = pe.matmul(b[:, 0:n], wb(c)[:, at:at + P], xT[:, c, 0:n], start=(c == 0), stop=(c == KC - 1))
                    mm.then_inc(*filled_now(("c", layer, name)))

                def queries(name, wb, j):
                    b = dense_bank(("c", layer, name))
                    for c in range(KC):
                        for v in range(2):
                            at = HD * (2 * v + j)
                            mm = pe.matmul(b[HD * v:HD * v + HD, 0:n_tok], wb(c)[:, at:at + HD], xT[:, c, 0:n_tok],
                                           start=(c == 0), stop=(c == KC - 1))
                    mm.then_inc(*filled_now(("c", layer, name)))

                def values2(name, wb, at):
                    b = dense_bank(("c", layer, name))
                    for t in range(4):
                        for c in range(KC):
                            mm = pe.matmul(b[:, P * t:P * t + P], xT[:, c, P * t:P * t + P], wb(c)[:, at:at + P],
                                           start=(c == 0), stop=(c == KC - 1))
                    mm.then_inc(*filled_now(("c", layer, name)))

                def square_sums2(names):
                    for name in names:
                        n = n_tok if name[1] == "q" else 2 * SEQ
                        pe.wait_ge(*after("sq", (layer, name)))
                        i = int(name[2])
                        b = open_bank(("qss", layer, name), 4 + i)
                        pe.matmul(b[:, 0:n], con("blk64"), sq[:, i, 0:n], start=True, stop=True).then_inc(*filled_now(("qss", layer, name)))

                def rotations(names):
                    for name in names:
                        pe.wait_ge(*(after("proj", ("qk", layer, name)) if name[0] == "c" else after("rms", ("qk", layer, name))))
                        b = open_bank(("rot2", layer, name), 6 + int(name[2]))
                        pe.matmul(b[:, 0:SEQ], con("rot16"), qk[:, QK_AT[name], 0:SEQ], start=True, stop=True)\
                          .then_inc(*filled_now(("rot2", layer, name)))

                for blk, n0, n1 in IN2_BLOCKS:
                    wb = w_block(("in2", layer, blk))
                    if blk in "dc":
                        for i in range(2):
                            queries(f"{blk}q{i}", wb, i)
                        if blk == "c":
                            square_sums2(("dq0", "dq1"))
                        chunk(blk + "k0", wb, 2 * P, 2 * SEQ)
                        values2(blk + "v", wb, 3 * P)
                        if blk == "c":
                            square_sums2(("dk0",))
                            rotations(("cq0", "cq1"))
                    else:
                        for name, at in CHUNKS.items():
                            if n0 <= at < n1:
                                chunk(name, wb, at - n0)
                        if blk == "b":
                            gate_rows_of(0)
                        if blk == "ab":
                            rotations(("ck0", "dq0", "dq1"))
                    read(("in2", layer, blk), 2)
                rotations(("dk0",))
                for c in range(2):
                    pe.wait_ge(*after("uconv", (layer, c)))
                for tp in range(seqs):
                    b = dense_bank(("u", layer, tp))
                    for t in range(2):
                        for c in range(2):
                            mm = pe.transpose(b[:, 256 * t + P * c:256 * t + P * c + P],
                                              sig[:, c, (2 * tp + t) * P:(2 * tp + t + 1) * P], ident)
                    mm.then_inc(*filled_now(("u", layer, tp)))
                pe.wait_ge(*after("u_norm", (layer, seqs - 1)))
                for c in range(2):
                    b = dense_bank(("ub", layer, c))
                    for t in tiles:
                        mm = pe.transpose(b[:, P * t:P * t + P], u_rows[:, t, P * c:P * c + P], ident)
                    mm.then_inc(*filled_now(("ub", layer, c)))
                pe.wait_ge(*after("rope_out", ("qk", layer, "dk0")))
                pe.wait_ge(*after("proj", ("v2", layer, "cv")))
                us = block2_units(layer)
                attend(us)
                pe.wait_ge(*after("oT", us[-1]["key"]))
                pe.wait_ge(*after("yb", (layer, 1)))
                pe.wait_ge(*after("short", layer))
                for nb in range(2):
                    project_rows2(("out2", layer, nb), lambda c, t: (y_lo if c < 2 else yb if c < 4 else y_hi)[:, (c, c - 2, c - 4)[(c >= 2) + (c >= 4)], t * P:t * P + P], tiles)
                logits = open_bank(("logits", layer), 6)

                def router_chunk(c):
                    pe.wait_ge(*after("hT_odd" if c % 2 else "hT", (layer, 1, c)))
                    for t in tiles:
                        mm = pe.matmul(logits[:, NE * t:NE * t + NE], xT[:, c, P * t:P * t + P], router[:, layer, c, :],
                                       start=(c == t == 0), stop=(c == KC - 1 and t == tiles[-1]))
                    return mm
                pe.wait_ge(*after("router_in", 0))
                hidden_T(1, tiles, router_chunk)
                pe.wait_ge(*after("aff", layer))
                R = 32 * (seqs - 1) + NE
                b = dense_bank(("affT", layer))
                for t in range(T2):
                    mm = pe.transpose(b[0:R, P * t:P * t + P], aff[:, t].rearrange("p s e -> p (s e)")[:, 0:R], ident)
                mm.then_inc(*filled_now(("affT", layer)))
                gate_rows_of(1)
                pe.wait_ge(*after("top", layer))
                b = dense_bank(("posT", layer))
                for t in range(T2):
                    mm = pe.transpose(b[:, 64 * t:64 * t + R], picked[0:R, P * t:P * t + P], ident[0:R, 0:R])
                mm.then_inc(*filled_now(("posT", layer)))

                m, G, order = M[layer], experts_per_group(layer), moe_units(layer)
                W = P // G
                u0, U = unit_at[("experts", layer)] - first2, len(order)
                n_sum = 2 * len(tiles)
                for b8 in range(8):
                    if filled[b8]:
                        pe.wait_ge(bank_free[b8], filled[b8])
                with pe.Fori(0, NE // G) as i:
                    pe.wait_ge(m["pick"], i + 1)
                    for h in range(2):
                        pe.wait_ge(m["y_sb"], 2 * i + 1 + h)
                        for c in range(4):
                            for n, t in enumerate(tiles):
                                mm = pe.matmul(bank[4 + h][:, P * c:P * c + P], xhat[:, t, P * (4 * h + c):P * (4 * h + c) + P],
                                               moe_pick[:, t, :], start=(n == 0), stop=(n == len(tiles) - 1))
                        mm.then_inc(m["xg_full"], 1)
                    pe.wait_ge(m["sum_free"], n_sum * i + n_sum)
                    for t in tiles:
                        mm = pe.transpose(bank[6][:, P * t:P * t + P], moe_pick_g[:, t, :], ident)
                    mm.then_inc(m["g_full"], 1)
                    pe.wait_ge(m["xt"], i + 1)

                    def product(bi, dst, src):
                        for h in range(2):
                            for j in range(G):
                                k = (2 * bi + h) * G + j
                                pe.wait_ge(ring_in[(u0 + k) % RING], i * (16 * U // RING) + 16 * ((u0 + k) // RING + 1))
                            for c in range(UK):
                                for j in range(G):
                                    k = (2 * bi + h) * G + j
                                    mm = pe.matmul(dst[W * j:W * j + W, :], src[:, UK * h + c, W * j:W * j + W],
                                                   ring[:, (u0 + k) % RING, c, :], start=(h == 0 and c == 0),
                                                   stop=(h == 1 and c == UK - 1))
                            if h == 0:
                                mm.then_inc(m["halves"], 1)
                        mm.then_inc(m["blocks"], 1)
                    for nb in range(2):
                        pe.wait_ge(m["hid"], 2 * i + 1 + nb)
                        product(2 * nb, bank[2 * nb], moe_x)
                        product(2 * nb + 1, bank[2 * nb + 1], moe_x)
                    for nb in range(2):
                        pe.wait_ge(m["hid"], 2 * i + 3 + nb)
                        if nb:
                            pe.wait_ge(m["ht_sb"], 2 * i + 1)
                        for q in range(4):
                            mm = pe.transpose(bank[7][:, P * q:P * q + P], moe_h[:, 512 * nb + P * q:512 * nb + P * q + P], ident)
                        mm.then_inc(m["ht_full"], 1)
                    pe.wait_ge(m["ht_sb"], 2 * i + 2)
                    for nb in range(2):
                        product(4 + nb, bank[4 + nb], moe_hT)
                    pe.wait_ge(m["g_sb"], i + 1)
                    pe.wait_ge(m["y_sb"], 2 * i + 4)
                    for n in range(n_sum):
                        if n >= 2:
                            pe.wait_ge(m["sum_free"], n_sum * i + n_sum + n - 1)
                        pe.matmul(bank[6 + n % 2][:, :], moe_g[:, P * (n // 2):P * (n // 2) + P], moe_y[:, 512 * (n % 2):512 * (n % 2) + 512],
                                  start=True, stop=True).then_inc(m["sum_full"], 1)

        @block.sync
        def _(sp):
            sp.dma_start(const[:, 0:P], w["consts"][:, 0:P]).then_inc(*signal("ident_in", 0, 16))
            sp.dma_start(x[:, 0:2, :], w["x"][0].rearrange("(t p) d -> p t d", p=P)).then_inc(*signal("x_in", 0, 16))
            def slot_before(u):
                if u < first2:
                    return u - RAW_SLOTS if u >= RAW_SLOTS else None
                slot = u - first2
                if slot >= RING:
                    return u - RING
                if slot >= RAW_AT:
                    return max(b for b in range(first2) if RAW_AT + b % RAW_SLOTS == slot)
                if slot >= HI_AT:
                    return max(b for b in split_units if HI_AT + place[b] % HI_SLOTS == slot)
                return unit_at[("mem_kv", DEPTH - 1, 3, 1)] if slot == MEM_HI else unit_at[("up", DEPTH - 1, FFN // UN, 1)]

            u, moe_last = 0, {}
            for key, view in units:
                if u == 2:
                    sp.dma_start(mem_rows, w["mem"][0].rearrange("(t p) d -> p t d", p=P)).then_inc(*signal("mem_in", 0, 16))
                if u == 6:
                    sp.dma_start(const[:, P:], w["consts"][:, P:]).then_inc(*signal("const_in", 0, 16))
                if key[0] == "experts":
                    layer = key[1]
                    m, G, order = M[layer], experts_per_group(layer), moe_units(layer)
                    U, groups, v = len(order), NE // G, u - first2

                    def load(k, expert):
                        name, nb, h, j = order[k % U]
                        view = w[name][layer, expert(j + (G if k >= U else 0))].rearrange("(c p) n -> p c n", p=P)
                        sp.dma_start(ring[:, (v + k) % RING], view[:, UK * h:UK * h + UK, UN * nb:UN * nb + UN])\
                          .then_inc(ring_in[(v + k) % RING], 16)

                    def slot_free(k, i):
                        bi, h = (k - RING) // (2 * G), (k - RING) // G % 2
                        sp.wait_ge(m["blocks" if h else "halves"], i * 6 + bi + 1)
                        sp.sem_inc(m["loads"], 1)
                    for k in range(RING):
                        sp.wait_ge(*last_reader[u + k - RING])
                        load(k, lambda e: e)
                    with sp.Fori(0, groups - 1) as i:
                        for k in range(RING, U + RING):
                            slot_free(k, i)
                            load(k, lambda e: i * G + e)
                    for k in range(RING, U):
                        slot_free(k, groups - 1)
                        load(k, lambda e: (groups - 1) * G + e)
                    for k in range(U - RING, U):
                        moe_last[u + U * (groups - 1) + k] = (m["blocks" if k // G % 2 else "halves"], (groups - 1) * 6 + k // (2 * G) + 1)
                    u += U * groups
                    continue
                if (stop and key[0] == stop):
                    break
                slot, loaded, _ = slot_of(u)
                before = slot_before(u)
                if before in moe_last:
                    sp.wait_ge(*moe_last[before])
                elif before is not None:
                    sp.wait_ge(*last_reader[before])
                sp.dma_start(ring[:, slot, 0:view.shape[1], 0:view.shape[2]], view).then_inc(loaded, 16)
                u += 1
            for t in range(T2):
                sp.wait_ge(*after("x_ready", (5 if stop else "final", t)))
            sp.dma_start(out[0].rearrange("(t p) d -> p t d", p=P), x[:, 0:2, :]).then_inc(*signal("out_dma", 0, 16))
            sp.wait_ge(*after("out_dma", 0))

        @block.gpsimd
        def _(pool):
            pool.dma_start(gate_w[:, :, :], w["even_w_in"][0][:, 2048:2064].rearrange("(c p) n -> p c n", p=P))\
                .then_inc(*signal("gate_w_in", 0, 16))
            pool.dma_start(sink[:, :, :], w["sink_2"].partition_broadcast(P)).then_inc(*signal("sink_in", 0, 16))
            pool.dma_start(router[:, :, :, :].rearrange("p l c e -> p (l c) e"), w["router_w_2"].rearrange("l (c p) e -> p (l c) e", p=P))\
                .then_inc(*signal("router_in", 0, 16))

            def norm_rows_in(i):
                if i == 0:
                    pool.wait_ge(*after("oT", ("na", B_HEADS - 1)))
                else:
                    for t in range(T2):
                        pool.wait_ge(*after("x_ready", (i - 1, t)))
                for k, name in enumerate(("ln_g", "ln_b")):
                    pool.dma_start(ln_row[:, k, :], w[name][i // 3, i % 3].partition_broadcast(P))\
                        .then_inc(*signal("ln_row_in", (i, k), 16))

            def place_of(*key):
                return place[unit_at[key]] + HI_SLOTS - 1
            at = {place_of("even_out", 0, 0): 0, place_of("mem_q", 0, 0, 0): 1, place_of("gate", 0, 0, 0): 2,
                  place_of("odd_in", 0, 0): 3, place_of("mem_q", 1, 0, 0): 4, place_of("gate", 1, 0, 0): 5}
            for i, u in enumerate(split_units):
                kc, n = units[u][1].shape[1:]
                whole, lo = (r[:, slot_of(u)[0], 0:kc, 0:n] for r in (ring, ring_r))
                pool.wait_ge(*after("w_hi", u))
                pool.tensor_tensor(lo, whole, hi_of(u)[:, 0:kc, 0:n], ALU.subtract).then_inc(*signal("w_lo", u))
                if i == HI_SLOTS:
                    for r in range(ROWS):
                        pool.dma_start(nab[64 * (r % 2):64 * (r % 2) + 64, r // 2, :, :].rearrange("p h (i k) -> p h i k", k=GRID_W),
                                       w["rpb_windows"][:, :, ROWS - 1 - r:2 * ROWS - 1 - r, :]).then_inc(*signal("nab_in", r, 16))
                if i in at:
                    norm_rows_in(at[i])
                if i == place_of("gate", 0, 0, 0):
                    pool.dma_start(lam_raw.rearrange("p a b -> p (a b)"), w["odd_lambda"][0].rearrange("a b -> (a b)").partition_broadcast(P))\
                        .then_inc(*signal("lam_in", 0, 16))
            if stop:
                return
            for t in range(T2):
                pool.wait_ge(*after("x_ready", (4, t)))
            pool.dma_start(x[:, 2:4, :], w["ctx_2"][0].rearrange("(t p) d -> p t d", p=P)).then_inc(*signal("ctx_in", 0, 16))
            steps = [0]

            def link(ins):
                steps[0] += 1
                ins.then_inc(pool_step, 1)
                pool.wait_ge(pool_step, steps[0])

            def gate_diag(layer, kind, seqs):
                for s in range(seqs):
                    if s:
                        pool.wait_ge(*full(("gbc", layer, kind, 0, 1)))
                    g = mods_all[:, layer, 16 + 24 * kind:24 + 24 * kind, s:s + 1].to_broadcast([P, KC, P])
                    pool.tensor_tensor(diag, ident.unsqueeze(1).to_broadcast([P, KC, P]), g, ALU.mult)\
                        .then_inc(*signal("diag", (layer, kind, s)))

            for layer in range(DEPTH):
                seqs = 2 if layer == 0 else 1
                pool.wait_ge(*after("mods", layer))
                gate_diag(layer, 0, seqs)
                if layer == 1:
                    pool.wait_ge(*after("x2", (0, 1, 3)))
                    pool.dma_start(g_row[:, 1, :], w["final_g_2"].partition_broadcast(P)).then_inc(*signal("final_row_in", 0, 16))
                for i in range(2):
                    b, c = (y_lo[:, j, 0:SEQ * seqs].rearrange("p (s k) -> p s k", k=SEQ) for j in (i, 2 + i))
                    z = z_pad[:, i, 0:seqs]
                    at = 6 * layer + i
                    pool.wait_ge(*after("ab_in", (layer, 5)))
                    tmp = xT[:, i, 0:SEQ * seqs].rearrange("p (s k) -> p s k", k=SEQ)
                    link(pool.tensor_tensor(z[:, :, 1:1 + SEQ], z[:, :, 1:1 + SEQ], c, ALU.mult))
                    link(pool.tensor_scalar(c, z[:, :, 0:SEQ], col("conv_a", at), None, ALU.mult))
                    for j in (1, 2):
                        link(pool.tensor_scalar(tmp, z[:, :, j:j + SEQ], col("conv_a", at + 2 * j), None, ALU.mult))
                        link(pool.tensor_tensor(c, c, tmp, ALU.add))
                    link(pool.tensor_tensor(b, b, c, ALU.mult))
                pool.sem_inc(*signal("short", layer))
                pool.wait_ge(*after("x2", (layer, 0, 2 * seqs - 1)))
                gate_diag(layer, 1, seqs)
                pool.wait_ge(*after("logit_max", layer))
                pool.memset(moe_pick, 0.0)
                pool.memset(moe_pick_g, 0.0)
                pool.memset(acc[:, 0:4 * seqs, :], 0.0).then_inc(*signal("cleared", layer))

        @block.scalar
        def _(act):
            steps = [0]

            def link(ins):
                steps[0] += 1
                ins.then_inc(act_step, 1)
                act.wait_ge(act_step, steps[0])

            split, hold = [0], [len(split_units)]

            def split_through(n):
                while split[0] < min(n + 1, hold[0]):
                    i = split[0]
                    u = split_units[i]
                    kc, n_col = units[u][1].shape[1:]
                    slot, loaded, count = slot_of(u)
                    if i >= HI_SLOTS:
                        act.wait_ge(*last_reader[split_units[i - HI_SLOTS]])
                    act.wait_ge(loaded, count)
                    act.activation(hi_of(u)[:, 0:kc, 0:n_col], ring[:, slot, 0:kc, 0:n_col], ACT.Copy).then_inc(*signal("w_hi", u))
                    split[0] += 1

            def follow(block_key, last=True):
                h = 0
                while block_key + (h,) in unit_at:
                    more = block_key + (h + 1,) in unit_at
                    if more or last:
                        split_through(place[unit_at[block_key + (h,)]] + HI_SLOTS)
                    h += 1

            def evac(key, dst, func=ACT.Copy):
                block_key = key[:-2]
                projected = key[-2:-1] == ("out",) and unit_at[block_key + (0,)] in place
                if projected:
                    follow(block_key, last=False)
                act.wait_ge(*full(key))
                src = bank_of(key)[:, 0:int(np.prod(dst.shape[1:]))]
                if len(dst.shape) == 3:
                    src = src.rearrange("p (a b) -> p a b", a=dst.shape[1])
                link(act.activation(dst, src, func))
                act.sem_inc(*freed(key))
                if projected and key == last_out[block_key]:
                    follow(block_key)

            def done(kind, key):
                act.sem_inc(*signal(kind, key))

            def to_T(key, event, dst, t):
                for h in range(2):
                    act.wait_ge(*full(key + (h,)))
                    act.activation(dst[:, 4 * h:4 * h + 4, t * P:t * P + P], bank_of(key + (h,))[:, :].rearrange("p (a b) -> p a b", a=4),
                                   ACT.Copy).then_inc(*signal("xT_hi", event + (h,)))

            def roots(i, *blocks):
                for n, block_key in enumerate(blocks):
                    follow(block_key, last=n < len(blocks) - 1)
                for t in range(T2):
                    act.wait_ge(*after("var", (i, t)))
                    act.activation(std[:, t:t + 1], mv[:, t, 1:2], ACT.Sqrt).then_inc(*signal("rstd", (i, t)))
                if i == 0:
                    act.wait_ge(*after("zero", "scT"))
                    act.activation(scT[:, :, 0:2], col("cc", 0, 16).rearrange("p (c s) -> p c s", s=2), ACT.Silu)\
                       .then_inc(*signal("sc_silu", 0))
                follow(blocks[-1])

            def norm_T(i):
                for t in range(T2):
                    if i < 5:
                        to_T(("xT", i, t), (i, t), x_hi, t)

            def exps(u, scale_in=True):
                parts = 1 if u["keys"] == 256 else 2
                act.wait_ge(*after("nmax", u["key"]))
                if u["n"] >= 2:
                    act.wait_ge(*full(turned(u)))
                pr, m = probs_of(u), u["n"] % 2
                for t in range(2):
                    if u["bias"] is None:
                        key = ("s",) + u["key"] + (0 if parts == 1 else t,)
                        act.wait_ge(*full(key))
                        src = bank_of(key)[:, 0:512] if parts == 2 else bank_of(key)[:, 256 * t:256 * t + 256]
                        scale = u["scale"]
                    else:
                        src, scale = pr[:, t, :], 1.0
                    link(act.activation(pr[:, t, :], src, ACT.Exp, bias=small[:, m, t:t + 1], scale=scale,
                                        accum_out=small[:, m, 2 + t:3 + t]))
                    if u["bias"] is None and (parts == 2 or t == 1):
                        act.sem_inc(*freed(key))
                if u["sink"] is not None:
                    for t in range(2):
                        link(act.activation(small[:, m, 4 + t:5 + t], u["sink"], ACT.Exp, bias=small[:, m, t:t + 1]))
                done("probs_exp", u["key"])

            def evac_T(u):
                if u["n"] >= 2:
                    act.wait_ge(*full(("o", u["key"][0], u["n"] - 2)))
                for part in range(u["keys"] // 256):
                    key = ("pT",) + u["key"] + (part,)
                    evac(key, probsT_of(u)[:, 2 * part:2 * part + 2, :])
                done("probsT", u["key"])

            def attend(us, between=None):
                for i in range(len(us) + 1):
                    if i < len(us):
                        exps(us[i])
                    if i:
                        evac_T(us[i - 1])
                    if between and i == 2:
                        between()

            act.dma_start(cols[:, :], w["cols"]).then_inc(*signal("cols_in", 0, 16))
            act.dma_start(gate_b[:, :], w["gate_b"]).then_inc(*signal("gate_b_in", 0, 16))
            split_through(0)
            for t in range(T2):
                to_T(("xT", "in", t), ("in", t), x_hi, t)
            split_through(HI_SLOTS - 1)
            for b in (0, 1):
                for j in range(2):
                    c = 4 * b + 2 * j
                    evac(("even_in", b, "out", j), qk_pad[:, c:c + 2, 2:2 + SEQ])
                    done("proj", ("even_in", b, "out", j))
                if b == 0:
                    for t in range(T2):
                        to_T(("memT", t), ("mem", t), m_hi, t)
            act.wait_ge(*after("gate_abs", 0))
            act.activation(g_tmp, g_tmp, ACT.Exp, scale=-1.0).then_inc(*signal("gate_exp", 0))
            act.wait_ge(*after("gate_ln1", 0))
            act.activation(g_tmp, g_tmp, ACT.Ln).then_inc(*signal("gate_ln", 0))
            for t in range(T2):
                evac(("even_in", 2, "out", t), a_v[:, t, :])
            for j in range(2):
                evac(("even_in", 3, "out", j), a_oT[:, 2 * j:2 * j + 2, :], ACT.Sigmoid)
            done("proj", "a_o")
            act.wait_ge(*full(("gate_cols",)))
            g = bank_of(("gate_cols",))
            link(act.activation(gcols[:, 0].rearrange("p a b c -> p (a b c)"), g[:, 0:16], ACT.Copy))
            link(act.activation(gcols[:, 1].rearrange("p a b c -> p (a b c)"), g[:, 16:32], ACT.Exp))
            act.sem_inc(*freed(("gate_cols",)))
            done("gate_cols", 0)
            for c in range(8):
                act.wait_ge(*after("conv", c))
                act.activation(qkT[:, c, :], qkT[:, c, :], ACT.Silu).then_inc(*signal("silu", c))
            def mlstm_exps(h):
                act.wait_ge(*after("decay", h))
                for d in range(2):
                    for t in range(2):
                        e = decay[h % 2][:, d, t, :]
                        ins = act.activation(e, e, ACT.Exp, bias=gcols[:, 0, d, t, h:h + 1])
                ins.then_inc(*signal("decay_exp", h))

            for b in (4, 5):
                for j in range(2):
                    c = 4 * (b - 4) + 2 * j
                    evac(("even_in", b, "out", j), b_qkT[:, c:c + 2, :])
                if b == 4:
                    mlstm_exps(0)
                    mlstm_exps(1)
            evac_T(ml_units[0])
            mlstm_exps(2)
            for t in range(T2):
                evac(("even_in", 6, "out", t), b_v[:, t, :])
                done("proj", ("even_in", 6, "out", t))
            evac_T(ml_units[1])
            mlstm_exps(3)
            for u in ml_units[2:]:
                evac_T(u)
            attend(na_units)

            for layer in range(DEPTH):
                if layer == 1:
                    act.wait_ge(*after("lam_sums", 0))
                    link(act.activation(lam[:, 2:4], lam[:, 0:2], ACT.Exp))
                    done("lam_exps", 0)
                    for b in range(4):
                        for j in range(2):
                            for m in range(2):
                                c = 4 * b + 2 * j + m
                                if m == 0:
                                    follow(("odd_in", b), last=False)
                                    act.wait_ge(*full(("odd_in", b, "out", j)))
                                if c >= 2:
                                    act.wait_ge(*after("rope_out", c - 2))
                                else:
                                    act.wait_ge(*after("lam_sums", 0))
                                link(act.activation(raw[:, c % 2, :], bank_of(("odd_in", b, "out", j))[:, 256 * m:256 * m + 256], ACT.Copy))
                                done("proj", ("raw", c))
                            act.sem_inc(*freed(("odd_in", b, "out", j)))
                        follow(("odd_in", b))
                    for b in (4, 5):
                        for t in range(T2):
                            evac(("odd_in", b, "out", t), v_rows[:, t, 512 * (b - 4):512 * (b - 4) + 512])
                            done("proj", ("odd_in", b, "out", t))

                    def diff_exps(u):
                        act.wait_ge(*after("nmax", u["key"]))
                        for m in range(2):
                            for t in range(2):
                                key = ("s",) + u["key"] + (m,)
                                link(act.activation(diff_probs(u, m)[:, t, :], bank_of(key)[:, 256 * t:256 * t + 256], ACT.Exp,
                                                    bias=small[:, u["n"] % 2, 2 * m + t:2 * m + t + 1], scale=u["scale"],
                                                    accum_out=small[:, u["n"] % 2, 4 + 2 * m + t:5 + 2 * m + t]))
                            act.sem_inc(*freed(key))
                        done("probs_exp", u["key"])

                    def diff_out(u):
                        key = ("o",) + u["key"]
                        act.wait_ge(*full(key))
                        act.activation(u["y"][0][0], bank_of(key)[:, 0:SEQ], ACT.Copy)
                        if u["n"] >= 2:
                            act.wait_ge(*full(("ss", u["n"] - 2)))
                        link(act.activation(raw[:, u["n"] % 2, :], bank_of(key)[:, 0:SEQ], ACT.Square))
                        act.sem_inc(*freed(key))
                        done("ssq", u["n"])
                    for i in range(C_HEADS + 2):
                        if i < C_HEADS:
                            diff_exps(diff_units[i])
                        if 0 <= i - 2:
                            diff_out(diff_units[i - 2])
                        if 0 <= i - 1 < C_HEADS:
                            evac_T(diff_units[i - 1])
                    act.wait_ge(*after("rms", "diff"))
                    act.activation(dvar, dvar, ACT.Sqrt).then_inc(*signal("rstd", "diff"))
                    for h in range(C_HEADS):
                        act.wait_ge(*after("oT", ("diff", h)))
                        act.activation(x_hi[:, h], y1T[:, h, :], ACT.Copy).then_inc(*signal("y_hi", ("diff", h)))
                n0 = 3 * layer
                name = ("even_out", "odd_out")[layer]
                roots(n0, (name, 0), (name, 1))
                for b in range(2):
                    for j in range(2):
                        c = 4 * b + 2 * j
                        evac(("mem_kv", layer, b, "out", j), kT[:, c:c + 2, :])
                for b in range(2, 4):
                    for t in range(T2):
                        evac(("mem_kv", layer, b, "out", t), v_rows[:, t, 512 * (b - 2):512 * (b - 2) + 512])
                norm_T(n0)
                hold[0] = place[unit_at[("mem_o", layer, 0, 0)]]
                for b in range(2):
                    for j in range(2):
                        c = 4 * b + 2 * j
                        evac(("mem_q", layer, b, "out", j), qT[:, c:c + 2, :])
                        done("proj", ("mem_q", layer, b, "out", j))
                def two_units():
                    hold[0] += RAW_SLOTS - 4
                    split_through(hold[0])
                attend(mem_units(layer), two_units)
                hold[0] = len(split_units)
                if layer:
                    act.wait_ge(*full(("modsT", 0, 2)))
                follow(("mem_q", layer, 1))
                evac(("ada", layer, 0), mods_rows[0])
                done("mods_rows", (layer, 0))
                roots(n0 + 1, ("mem_o", layer, 0), ("mem_o", layer, 1))
                norm_T(n0 + 1)
                for k in range(FC // 2):
                    b, j = k // 2, k % 2
                    key = ("gate", layer, b, "out", j)
                    follow(("gate", layer, b), last=False)
                    act.wait_ge(*full(key))
                    if k >= 2:
                        act.wait_ge(*after("h_full", (layer, k - 2)))
                    link(act.activation(hsilu[:, k % 2, :], bank_of(key)[:, :], ACT.Silu))
                    act.sem_inc(*freed(key))
                    done("silu", (layer, k))
                    if key == last_out[key[:-2]]:
                        follow(("gate", layer, b))
                        follow(("up", layer, b))
                        for i in range(2 * b, k + 1):
                            act.wait_ge(*after("h_full", (layer, i)))
                            c = 2 * i
                            hi = hT_hi[0][:, c:c + 2] if c < 16 else hT_hi[1][:, c - 16:c - 14]
                            act.activation(hi, hT[:, c:c + 2, :], ACT.Copy).then_inc(*signal("h_hi", (layer, i)))
                        if b in (1, 3):
                            g = 1 + b // 2
                            if g == 2:
                                act.wait_ge(*full(("modsT", layer, 0)))
                            elif layer:
                                act.wait_ge(*full(("modsT", 0, 1)))
                            evac(("ada", layer, g), mods_rows[g % 2])
                            done("mods_rows", (layer, g))
                roots(n0 + 2, ("down", layer, 0), ("down", layer, 1))
                norm_T(n0 + 2)
            if stop:
                return

            def squares_of(layer, kind, ts):
                mine = scalar_tiles(layer, kind, ts)
                if (layer, kind) == (0, 0):
                    act.wait_ge(*after("ctx_in", 0))
                    act.wait_ge(*after("var", (5, T2 - 1)))
                for t in mine:
                    if (layer, kind, t) == (0, 0, 0):
                        act.wait_ge(*after("x_ready", (5, 0)))
                    if kind == 1:
                        act.wait_ge(*after("x2", (layer, 0, t)))
                    elif layer:
                        act.wait_ge(*after("x2", (0 if layer == 1 else DEPTH - 1, 1, t)))
                    ins = act.activation(xhat[:, t, :], x[:, t, :], ACT.Square, accum_out=mv[:, t, 0:1])
                ins.then_inc(*signal("ssq_act", (layer, kind)))

            for layer in range(DEPTH):
                seqs = 2 if layer == 0 else 1
                n_tok = SEQ * seqs
                tiles = range(2 * seqs)

                def gate_rows_of(kind):
                    for s in range(seqs):
                        for h in range(2):
                            if kind == 1 and s == 0 and h == 0:
                                for t in tiles:
                                    act.wait_ge(*after("x2", (layer, 0, t)))
                            evac(("gbc", layer, kind, s, h), g_row[:, s, 512 * h:512 * h + 512])
                    done("gates_bc", (layer, kind))

                def norm_rows(kind, ts):
                    squares_of(layer, kind, ts)
                    act.wait_ge(*after("ssq2", (layer, kind)))
                    act.activation(std[:, 0:len(ts)], mv[:, 0:len(ts), 1], ACT.Sqrt).then_inc(*signal("rstd", ("n2", layer, kind)))

                def hidden_T(kind, ns):
                    for c in range(0, KC, 2):
                        act.wait_ge(*full(("h", layer, kind, c)))
                        for s in range(ns):
                            ins = act.activation(xT[:, c, SEQ * s:SEQ * s + SEQ], bank_of(("h", layer, kind, c))[:, SEQ * s:SEQ * s + SEQ],
                                                 ACT.Identity, bias=shift(layer, kind)[:, c, s:s + 1], scale=gain[:, kind, c, s:s + 1])
                        link(ins)
                        act.sem_inc(*freed(("h", layer, kind, c)))
                        done("hT", (layer, kind, c))

                norm_rows(0, range(4))
                act.wait_ge(*after("mods", layer))
                hidden_T(0, 2)
                for i in range(2):
                    evac(("c", layer, f"bv{i}"), sig[:, i, 0:n_tok])
                    done("u_in", (layer, "v", i))
                for i in range(2):
                    key = ("c", layer, f"bg{i}")
                    act.wait_ge(*full(key))
                    link(act.activation(sq[:, i, 0:n_tok], bank_of(key)[:, 0:n_tok], ACT.Sigmoid))
                    act.sem_inc(*freed(key))
                    done("u_in", (layer, "g", i))
                gate_rows_of(0)

                def qk_evac(name):
                    n = n_tok if name[1] == "q" else 2 * SEQ
                    evac(("c", layer, name), qk[:, QK_AT[name], 0:n])
                    done("proj", ("qk", layer, name))

                def squares(names):
                    for name in names:
                        n, i = n_tok if name[1] == "q" else 2 * SEQ, int(name[2])
                        act.wait_ge(*(after("u_in2", (layer, i)) if name[1] == "q" else full(("qss", layer, f"dq{i}"))))
                        act.activation(sq[:, i, 0:n], qk[:, QK_AT[name], 0:n], ACT.Square).then_inc(*signal("sq", (layer, name)))

                def roots(names):
                    for name in names:
                        n, i = n_tok if name[1] == "q" else 2 * SEQ, int(name[2])
                        act.wait_ge(*after("ssq", ("qk", layer, name)))
                        act.activation(qvar[:, i, 0:n], qvar[:, i, 0:n], ACT.Sqrt).then_inc(*signal("rstd", ("qk", layer, name)))

                for name in ("dq0", "dq1", "dk0"):
                    qk_evac(name)
                evac(("c", layer, "dv"), v2[:, :, 1, :])
                squares(("dq0", "dq1"))
                for name in ("cq0", "cq1"):
                    qk_evac(name)
                squares(("dk0",))
                roots(("dq0", "dq1"))
                for name in ("ck0",):
                    qk_evac(name)
                evac(("c", layer, "cv"), v2[:, :, 0, :])
                done("proj", ("v2", layer, "cv"))
                roots(("dk0",))
                for j, name in enumerate(("ab0", "ab1", "ac0", "ac1")):
                    evac(("c", layer, name), y_lo[:, j, 0:n_tok])
                    done("ab_in", (layer, j))
                for i in range(2):
                    key = ("c", layer, f"ah{i}")
                    act.wait_ge(*full(key))
                    act.wait_ge(*after("zero", ("z", layer)))
                    link(act.activation(z_pad[:, i, 0:seqs, 1:1 + SEQ], bank_of(key)[:, 0:n_tok].rearrange("p (s k) -> p s k", k=SEQ), ACT.Copy))
                    act.sem_inc(*freed(key))
                    done("ab_in", (layer, 4 + i))
                act.wait_ge(*after("uvar", layer))
                act.activation(std[:, 0:len(tiles)], mv[:, 0:len(tiles), 1], ACT.Sqrt).then_inc(*signal("rstd", ("u", layer)))
                act.wait_ge(*full(("ub", layer, 1)))
                for c in range(2):
                    key = ("ub", layer, c)
                    act.wait_ge(*full(key))
                    at = 2 * layer + c
                    link(act.activation(yb[:, c, 0:n_tok], bank_of(key)[:, 0:n_tok], ACT.Silu, bias=col("cln_b", at), scale=col("cln_g", at)))
                    act.sem_inc(*freed(key))
                    done("yb", (layer, c))
                attend(block2_units(layer))
                norm_rows(1, tiles)
                hidden_T(1, seqs)
                act.wait_ge(*after("logit_max", layer))
                act.activation(aff_of(seqs), aff_of(seqs), ACT.Exp).then_inc(*signal("aff_exp", layer))
                gate_rows_of(1)

                m, G = M[layer], experts_per_group(layer)
                act.sem_inc(m["y_sb"], 2)
                with act.Fori(0, NE // G) as i:
                    act.wait_ge(m["g_full"], i + 1)
                    n = P * len(tiles)
                    act.activation(moe_g[:, 0:n], bank[6][:, 0:n], ACT.Copy).then_inc(m["g_sb"], 1)
                    for nb in range(2):
                        act.wait_ge(m["blocks"], 6 * i + 2 * nb + 1)
                        act.activation(moe_silu[:, nb, :], bank[2 * nb][:, :], ACT.Silu).then_inc(m["silu"], 1)
                    for nb in range(2):
                        act.wait_ge(m["ht_full"], 2 * i + nb + 1)
                        act.activation(moe_hT[:, 4 * nb:4 * nb + 4, :].rearrange("p a b -> p (a b)"), bank[7][:, :], ACT.Copy)\
                           .then_inc(m["ht_sb"], 1)
                    for nb in range(2):
                        act.wait_ge(m["blocks"], 6 * i + 5 + nb)
                        act.activation(moe_y[:, 512 * nb:512 * nb + 512], bank[4 + nb][:, :], ACT.Copy).then_inc(m["y_sb"], 1)
            squares_of("final", 0, range(T2))
            act.wait_ge(*after("ssq2", ("final", 0)))
            act.activation(std[:, 0:2], mv[:, 0:2, 1], ACT.Sqrt).then_inc(*signal("rstd", "final"))

        @block.vector
        def _(dve):
            steps = [0]

            def link(ins):
                steps[0] += 1
                ins.then_inc(dve_step, 1)
                dve.wait_ge(dve_step, steps[0])

            def done(kind, key):
                dve.sem_inc(*signal(kind, key))

            def drop(key):
                dve.sem_inc(*freed(key))

            def ada_T(l, g):
                key = ("modsT", l, g)
                dve.wait_ge(*full(key))
                src = bank_of(key)[:, :].rearrange("p (q j r) -> p j q r", q=4, j=4)[:, :, :, 0:2]
                at = COLS["ada_b"][0] + 48 * l + 16 * g
                bias = cols[:, at:at + 16].rearrange("p (j q) -> p j q", j=4).unsqueeze(3).to_broadcast([P, 4, 4, 2])
                dst = mods_all[:, l, 16 * g:16 * g + 16, :].rearrange("p (j q) s -> p j q s", j=4)
                link(dve.tensor_tensor(dst, src, bias, ALU.add))
                drop(key)

            def residual_norm(i, key):
                for nb in range(2):
                    for t in range(T2):
                        k = key + (nb, "out", t)
                        dve.wait_ge(*full(k))
                        xs = x[:, t, 512 * nb:512 * nb + 512]
                        link(dve.scalar_tensor_tensor(xs, xs, ALPHA, bank_of(k)[:, :], ALU.mult, ALU.add))
                        drop(k)
                        link(dve.bn_stats(stats[:, t, nb, :], xs))
                for t in range(T2):
                    link(dve.bn_aggr(mv[:, t, :], stats[:, t, :, :].rearrange("p a b -> p (a b)")))
                    dve.tensor_scalar(mv[:, t, 1:2], mv[:, t, 1:2], LN_EPS, None, ALU.add).then_inc(*signal("var", (i, t)))
                for t in range(T2):
                    dve.wait_ge(*after("rstd", (i, t)))
                    link(dve.reciprocal(rstd[:, t:t + 1], std[:, t:t + 1]))
                    link(dve.tensor_scalar(x[:, t, :], x[:, t, :], mv[:, t, 0:1], rstd[:, t:t + 1], ALU.subtract, ALU.mult))
                    dve.wait_ge(*after("ln_row_in", (i, 1)))
                    link(dve.tensor_tensor(x[:, t, :], x[:, t, :], ln_row[:, 0, :], ALU.mult))
                    dve.tensor_tensor(x[:, t, :], x[:, t, :], ln_row[:, 1, :], ALU.add).then_inc(*signal("x_ready", (i, t)))

            def rest_T(key, event, hi, lo, t):
                for h in range(2):
                    dve.wait_ge(*after("xT_hi", event + (h,)))
                    src = bank_of(key + (h,))[:, :].rearrange("p (a b) -> p a b", a=4)
                    at = (slice(None), slice(4 * h, 4 * h + 4), slice(t * P, t * P + P))
                    link(dve.tensor_tensor(lo[at], src, hi[at], ALU.subtract))
                    drop(key + (h,))
                    done("xT", event + (h,))

            def norm_T(i):
                for t in range(T2):
                    rest_T(("xT", i, t), (i, t), x_hi, x_lo, t)

            def maxima(u):
                parts = 1 if u["keys"] == 256 else 2
                m, pr = u["n"] % 2, probs_of(u)
                if u["n"] >= 2:
                    dve.wait_ge(*full(turned(u)))
                for part in range(parts):
                    key = ("s",) + u["key"] + (part,)
                    dve.wait_ge(*full(key))
                    ts = slice(0, 2) if parts == 1 else slice(part, part + 1)
                    src = bank_of(key)[:, :].rearrange("p (t k) -> p t k", k=u["keys"])
                    if u["bias"] is not None:
                        n = u["bias"].shape[2]
                        link(dve.scalar_tensor_tensor(pr[:, ts, 0:n], src[:, :, 0:n], u["scale"], u["bias"][:, ts, :], ALU.mult, ALU.add))
                        if n < u["keys"]:
                            link(dve.tensor_scalar(pr[:, ts, n:], src[:, :, n:], u["scale"], None, ALU.mult))
                        drop(key)
                        src = pr[:, ts, :]
                    link(dve.tensor_reduce(small[:, m, 6:8][:, ts], src, AX.X, ALU.max))
                scale = u["scale"] if u["bias"] is None else 1.0
                if u["sink"] is not None:
                    if scale != 1.0:
                        link(dve.tensor_scalar(small[:, m, 6:8], small[:, m, 6:8], scale, None, ALU.mult))
                        scale = 1.0
                    link(dve.tensor_scalar(small[:, m, 6:8], small[:, m, 6:8], u["sink"], None, ALU.max))
                link(dve.tensor_scalar(small[:, m, 0:2], small[:, m, 6:8], -scale, None, ALU.mult))
                done("nmax", u["key"])

            def normalise(u):
                m, pr = u["n"] % 2, probs_of(u)
                dve.wait_ge(*after("probs_exp", u["key"]))
                if u["sink"] is not None:
                    link(dve.tensor_tensor(small[:, m, 2:4], small[:, m, 2:4], small[:, m, 4:6], ALU.add))
                link(dve.reciprocal(small[:, m, 8:10], small[:, m, 2:4]))
                for t in range(2):
                    ins = dve.tensor_scalar(pr[:, t, :], pr[:, t, :], small[:, m, 8 + t:9 + t], None, ALU.mult)
                ins.then_inc(*signal("probs", u["key"]))

            def output(u, gate=None):
                key = ("o",) + u["key"]
                dve.wait_ge(*full(key))
                for i, (y, p0) in enumerate(u["y"]):
                    src = bank_of(key)[p0:p0 + y.shape[0], 256 * i:256 * i + 256]
                    if gate is not None:
                        link(dve.tensor_tensor(y, src, gate, ALU.mult))
                        src = y
                    if u["parts"] is not None:
                        hi, lo = u["parts"][i]
                        link(dve.tensor_copy(hi, src))
                        ins = dve.tensor_tensor(lo, src, hi, ALU.subtract)
                    else:
                        ins = dve.tensor_copy(y, src)
                link(ins)
                drop(key)
                done("oT", u["key"])

            def attend(us):
                for u in us[:2]:
                    maxima(u)
                for i in range(len(us) + 2):
                    if i < len(us):
                        normalise(us[i])
                    if i >= 2:
                        output(us[i - 2])
                    if i + 2 < len(us):
                        maxima(us[i + 2])

            def gates():
                dve.wait_ge(*after("gate_b_in", 0))
                dve.wait_ge(*after("xT", ("mem", T2 - 1, 1)))
                for kind, dst in ((0, g_in), (1, g_forget)):
                    dve.wait_ge(*full(("gates", kind)))
                    src = bank_of(("gates", kind))[0:4, :].rearrange("p (d k) -> p d k", d=2)
                    for d in range(2):
                        ins = dve.tensor_scalar(dst[:, d, :], src[:, d, :], gate_b[:, 2 * kind + d:2 * kind + d + 1], None, ALU.add)
                    link(ins)
                    drop(("gates", kind))
                dve.scalar_tensor_tensor(g_tmp, g_forget, -1.0, g_forget, ALU.mult, ALU.max).then_inc(*signal("gate_abs", 0))
                dve.wait_ge(*after("gate_exp", 0))
                dve.tensor_scalar(g_tmp, g_tmp, 1.0, None, ALU.add).then_inc(*signal("gate_ln1", 0))
                dve.wait_ge(*after("gate_ln", 0))
                link(dve.scalar_tensor_tensor(g_forget, g_forget, 0.0, g_tmp, ALU.min, ALU.subtract))

                def along(v, d):
                    return v[:, d, :] if d == 0 else v[:, d, ::-1]
                for d in range(2):
                    ins = dve.tensor_tensor_scan(along(g_tmp, d), g_one[:, :], along(g_forget, d), 0.0, ALU.mult, ALU.add)
                link(ins)
                link(dve.tensor_tensor(g_c, g_in, g_tmp, ALU.subtract))
                for d in range(2):
                    ins = dve.tensor_tensor_scan(along(g_in, d), along(g_c, d), along(g_c, d), NEG, ALU.max, ALU.max)
                link(ins)
                link(dve.tensor_scalar(g_max[:, 0:2, :], g_in, -1.0, None, ALU.mult))
                dve.tensor_tensor(g_max[:, 2:4, :], g_max[:, 0:2, :], g_tmp, ALU.subtract).then_inc(*signal("gate_rows", 0))

            dve.memset(qk_pad[:, :, 0:2], 0.0)
            link(dve.memset(qk_pad[:, :, SEQ + 2:SEQ + 4], 0.0))
            link(dve.memset(g_one[:, :], 1.0))
            dve.wait_ge(*after("gate_w_in", 0))
            link(dve.tensor_copy(gate_w_hi, gate_w))
            link(dve.tensor_tensor(gate_w_lo, gate_w, gate_w_hi, ALU.subtract))
            done("gate_w_hi", 0)
            for t in range(T2):
                rest_T(("xT", "in", t), ("in", t), x_hi, x_lo, t)
            for t in range(T2):
                rest_T(("memT", t), ("mem", t), m_hi, m_lo, t)
            dve.wait_ge(*after("cols_in", 0))
            for c in range(8):
                dve.wait_ge(*after("proj", ("even_in", c // 4, "out", c // 2 % 2)))
                link(dve.tensor_scalar(qkT[:, c, :], qk_pad[:, c, 0:SEQ], col("conv", c), None, ALU.mult))
                for j in range(1, A_CONV):
                    ins = dve.scalar_tensor_tensor(qkT[:, c, :], qk_pad[:, c, j:j + SEQ], col("conv", 8 * j + c), qkT[:, c, :],
                                                   ALU.mult, ALU.add)
                    if j < A_CONV - 1:
                        link(ins)
                ins.then_inc(*signal("conv", c))
                if c == 3:
                    gates()

            mlmask = con("mlmask").rearrange("p (d t k) -> p d t k", d=2, t=2)

            def decays(h):
                if h >= 2:
                    dve.wait_ge(*after("probs", ("ml", h - 2)))
                dve.wait_ge(*full(("cb", h)))
                for d in range(2):
                    cb = bank_of(("cb", h))[:, 256 * d:256 * d + 256].unsqueeze(1).to_broadcast([P, 2, SEQ])
                    ins = dve.tensor_tensor(decay[h % 2][:, d], cb, mlmask[:, d], ALU.add)
                link(ins)
                drop(("cb", h))
                done("decay", h)

            def mixes(h):
                u = ml_units[h]
                m, pr, key = h % 2, probs_of(u), ("s", "ml", h, 0)
                dve.wait_ge(*after("decay_exp", h))
                dve.wait_ge(*full(key))
                for d in range(2):
                    for t in range(2):
                        e = decay[h % 2][:, d, t, :]
                        ins = dve.scalar_tensor_tensor(e, bank_of(key)[:, 256 * t:256 * t + 256], P ** -0.5, e, ALU.mult, ALU.mult,
                                                       accum_out=small[:, m, 2 * d + t:2 * d + t + 1])
                link(ins)
                drop(key)
                dve.wait_ge(*after("gate_cols", 0))
                den, big = small[:, m, 0:4], small[:, m, 4:8]
                link(dve.scalar_tensor_tensor(big, den, -1.0, den, ALU.mult, ALU.max))
                floor = gcols[:, 1, :, :, h]
                big2 = big.rearrange("p (d t) -> p d t", d=2)
                link(dve.tensor_tensor(big2, big2, floor, ALU.max))
                link(dve.reciprocal(small[:, m, 8:12], big))
                if h >= 2:
                    dve.wait_ge(*full(("pT", "ml", h - 2, 0)))
                for t in range(2):
                    ins = dve.tensor_scalar(pr[:, t, :], decay[h % 2][:, 0, t, :], small[:, m, 8 + t:9 + t], None, ALU.mult)
                link(ins)
                for t in range(2):
                    ins = dve.scalar_tensor_tensor(pr[:, t, :], decay[h % 2][:, 1, t, :], small[:, m, 10 + t:11 + t], pr[:, t, :],
                                                   ALU.mult, ALU.add)
                ins.then_inc(*signal("probs", ("ml", h)))

            dve.wait_ge(*after("proj", "a_o"))
            dve.wait_ge(*after("const_in", 0))
            decays(0)
            for h in range(A_HEADS):
                if h + 1 < A_HEADS:
                    decays(h + 1)
                mixes(h)
                if h:
                    output(ml_units[h - 1], a_oT[:, h - 1, :])
            output(ml_units[-1], a_oT[:, A_HEADS - 1, :])
            dve.wait_ge(*after("nab_in", ROWS - 1))
            keep = con("namask").unsqueeze(1).to_broadcast([P, T2 * B_HEADS * ROWS, GRID_W])
            nab_rows = nab.rearrange("p t h (i k) -> p (t h i) k", k=GRID_W)
            link(dve.tensor_tensor(nab_rows, nab_rows, keep, ALU.add))
            attend(na_units)
            dve.memset(scT, 0.0).then_inc(*signal("zero", "scT"))
            residual_norm(0, ("even_out",))
            for layer in range(DEPTH):
                n0 = 3 * layer
                if layer == 1:
                    lp = lam_raw
                    dve.wait_ge(*after("lam_in", 0))
                    for i in range(2):
                        ins = dve.scalar_tensor_tensor(rcos[:, 0, 64 * i:64 * i + 64], lp[:, 2 * i, :], 1.0, lp[:, 2 * i + 1, :], ALU.mult,
                                                       ALU.mult, accum_out=lam[:, i:i + 1])
                    link(ins)
                    done("lam_sums", 0)
                    dve.wait_ge(*after("lam_exps", 0))
                    link(dve.tensor_tensor(lam[:, 4:5], lam[:, 3:4], lam[:, 2:3], ALU.subtract))
                    link(dve.tensor_scalar(lam[:, 5:6], lam[:, 4:5], -LAM_INIT, None, ALU.add))
                    link(dve.tensor_scalar(lam[:, 6:7], col("subln"), 1.0 - LAM_INIT, None, ALU.mult))
                    for c in range(16):
                        dst = (qT if c < 8 else kT)[:, c % 8, :]
                        dve.wait_ge(*after("proj", ("raw", c)))
                        dve.tensor_tensor(rcos[:, c % 2, :], raw[:, c % 2, :], con("cos1"), ALU.mult)
                        dve.wait_ge(*full(("rot", c)))
                        link(dve.tensor_tensor(dst, bank_of(("rot", c))[:, 0:SEQ], con("sin1"), ALU.mult))
                        drop(("rot", c))
                        dve.tensor_tensor(dst, dst, rcos[:, c % 2, :], ALU.add).then_inc(*signal("rope_out", c))

                    def diff_maxima(u):
                        m = u["n"] % 2
                        for k in range(2):
                            key = ("s",) + u["key"] + (k,)
                            dve.wait_ge(*full(key))
                            link(dve.tensor_reduce(small[:, m, 12 + 2 * k:14 + 2 * k],
                                                   bank_of(key)[:, :].rearrange("p (t k) -> p t k", t=2), AX.X, ALU.max))
                        link(dve.tensor_scalar(small[:, m, 0:4], small[:, m, 12:16], -u["scale"], None, ALU.mult))
                        done("nmax", u["key"])

                    def diff_normalise(u):
                        m = u["n"] % 2
                        dve.wait_ge(*after("probs_exp", u["key"]))
                        link(dve.reciprocal(small[:, m, 8:12], small[:, m, 4:8]))
                        link(dve.tensor_scalar(small[:, m, 10:12], small[:, m, 10:12], lam[:, 5:6], None, ALU.mult))
                        for t in range(2):
                            ins = dve.tensor_scalar(diff_probs(u, 0)[:, t, :], diff_probs(u, 0)[:, t, :], small[:, m, 8 + t:9 + t], None, ALU.mult)
                        link(ins)
                        for t in range(2):
                            ins = dve.scalar_tensor_tensor(diff_probs(u, 0)[:, t, :], diff_probs(u, 1)[:, t, :], small[:, m, 10 + t:11 + t],
                                                           diff_probs(u, 0)[:, t, :], ALU.mult, ALU.add)
                        ins.then_inc(*signal("probs", u["key"]))

                    for u in diff_units[:2]:
                        diff_maxima(u)
                    for i in range(C_HEADS + 2):
                        if i < C_HEADS:
                            diff_normalise(diff_units[i])
                        if i + 2 < C_HEADS:
                            diff_maxima(diff_units[i + 2])
                        if i >= 2:
                            dve.wait_ge(*full(("ss", i - 2)))
                            link(dve.tensor_scalar(dvar[:, i - 2, :], bank_of(("ss", i - 2))[:, 0:SEQ], 1.0 / P, LN_EPS, ALU.mult, ALU.add))
                            drop(("ss", i - 2))
                            link(dve.reciprocal(dvar[:, i - 2, :], dvar[:, i - 2, :]))
                    done("rms", "diff")
                    dve.wait_ge(*after("rstd", "diff"))
                    for h in range(C_HEADS):
                        y = y1T[:, h, :]
                        dve.scalar_tensor_tensor(y, y, lam[:, 6:7], dvar[:, h, :], ALU.mult, ALU.mult)\
                           .then_inc(*signal("oT", ("diff", h)))
                    for h in range(C_HEADS):
                        dve.wait_ge(*after("y_hi", ("diff", h)))
                        dve.tensor_tensor(y1_lo[:, h], y1T[:, h, :], x_hi[:, h], ALU.subtract).then_inc(*signal("y_lo", ("diff", h)))
                    residual_norm(n0, ("odd_out",))
                norm_T(n0)
                attend(mem_units(layer))
                residual_norm(n0 + 1, ("mem_o", layer))
                norm_T(n0 + 1)
                for k in range(FC // 2):
                    key = ("up", layer, k // 2, "out", k % 2)
                    dve.wait_ge(*after("silu", (layer, k)))
                    dve.wait_ge(*full(key))
                    link(dve.tensor_tensor(hT[:, 2 * k:2 * k + 2, :].rearrange("p a b -> p (a b)"), bank_of(key)[:, :], hsilu[:, k % 2, :], ALU.mult))
                    drop(key)
                    done("h_full", (layer, k))
                    if key == last_out[key[:-2]]:
                        for i in range(k // 2 * 2, k + 1):
                            dve.wait_ge(*after("h_hi", (layer, i)))
                            hi = hT_hi[0][:, 2 * i:2 * i + 2] if i < 8 else hT_hi[1][:, 2 * i - 16:2 * i - 14]
                            dve.tensor_tensor(hT_lo[:, 2 * i:2 * i + 2], hT[:, 2 * i:2 * i + 2, :], hi, ALU.subtract)\
                               .then_inc(*signal("hid", (layer, i)))
                        if k // 2 in (0, 2):
                            ada_T(layer, k // 4)
                ada_T(layer, 2)
                residual_norm(n0 + 2, ("down", layer))
                if layer == 0:
                    norm_T(n0 + 2)
            if stop:
                return

            def hidden_T(layer, kind, ns):
                for c in range(1, KC, 2):
                    key = ("h", layer, kind, c)
                    dve.wait_ge(*full(key))
                    for s in range(ns):
                        span = slice(SEQ * s, SEQ * s + SEQ)
                        ins = dve.tensor_scalar(xT[:, c, span], bank_of(key)[:, span], gain[:, kind, c, s:s + 1],
                                                shift(layer, kind)[:, c, s:s + 1], ALU.mult, ALU.add)
                    link(ins)
                    drop(key)
                    done("hT_odd", (layer, kind, c))

            def norm_rows(layer, kind, ts):
                for t in ts:
                    if t not in scalar_tiles(layer, kind, ts):
                        ins = dve.scalar_tensor_tensor(xhat[:, t, :], x[:, t, :], 1.0, x[:, t, :], ALU.mult, ALU.mult,
                                                       accum_out=mv[:, t, 0:1])
                link(ins)
                dve.wait_ge(*after("ssq_act", (layer, kind)))
                dve.tensor_scalar(mv[:, 0:len(ts), 1], mv[:, 0:len(ts), 0], 1.0 / D, EPS, ALU.mult, ALU.add)\
                   .then_inc(*signal("ssq2", (layer, kind)))
                dve.wait_ge(*after("rstd", ("n2", layer, kind) if layer != "final" else "final"))
                link(dve.reciprocal(rstd[:, 0:len(ts)], std[:, 0:len(ts)]))
                if layer != "final":
                    for t in ts:
                        dve.tensor_scalar(xhat[:, t, :], x[:, t, :], rstd[:, t:t + 1], None, ALU.mult)\
                           .then_inc(*signal("xhat", (layer, kind, t)))

            link(dve.memset(aff[:, :, :, NE:], 0.0))
            dve.wait_ge(*after("x_ready", (5, 1)))
            dve.wait_ge(*after("ctx_in", 0))
            dve.wait_ge(*after("sink_in", 0))
            for layer in range(DEPTH):
                seqs = 2 if layer == 0 else 1
                n_tok = SEQ * seqs
                tiles = range(2 * seqs)
                for kind, name in enumerate(("n1", "n2")):
                    sc = mods_all[:, layer, 24 * kind + 8:24 * kind + 16, :]
                    n = col(name, 8 * layer, 8).unsqueeze(2).to_broadcast([P, KC, 2])
                    ins = dve.scalar_tensor_tensor(gain[:, kind], sc, 1.0, n, ALU.add, ALU.mult)
                link(ins)
                done("mods", layer)
                norm_rows(layer, 0, range(4))
                hidden_T(layer, 0, 2)
                dve.memset(z_pad[:, :, :, 0:1], 0.0)
                dve.memset(z_pad[:, :, :, SEQ + 1:SEQ + 2], 0.0)
                dve.memset(u_pad[:, :, :, 0:PAD_B], 0.0)
                link(dve.memset(u_pad[:, :, :, SEQ + PAD_B:SEQ + 2 * PAD_B], 0.0))
                done("zero", ("z", layer))
                for i in range(2):
                    dve.wait_ge(*after("u_in", (layer, "v", i)))
                    dve.wait_ge(*after("u_in", (layer, "g", i)))
                    a, b = (v[:, i, 0:n_tok].rearrange("p (s k) -> p s k", k=SEQ) for v in (sig, sq))
                    link(dve.tensor_tensor(u_pad[:, i, 0:seqs, PAD_B:PAD_B + SEQ], a, b, ALU.mult))
                    done("u_in2", (layer, i))
                for i in range(2):
                    y = sig[:, i, 0:n_tok].rearrange("p (s k) -> p s k", k=SEQ)
                    at = 62 * layer + i
                    link(dve.tensor_scalar(y, u_pad[:, i, 0:seqs, 0:SEQ], col("conv_b", at), col("conv_bb", 2 * layer + i), ALU.mult, ALU.add))
                    for j in range(1, CONV_B):
                        link(dve.scalar_tensor_tensor(y, u_pad[:, i, 0:seqs, j:j + SEQ], col("conv_b", at + 2 * j), y, ALU.mult, ALU.add))
                    done("uconv", (layer, i))

                def rotate(names):
                    for name in names:
                        v = qk[:, QK_AT[name], 0:SEQ]
                        key = ("rot2", layer, name)
                        dve.wait_ge(*full(key))
                        dve.tensor_tensor(rtmp[:, 0, :], bank_of(key)[:, 0:SEQ], con("sin2"), ALU.mult)
                        link(dve.tensor_tensor(v, v, con("cos2"), ALU.mult))
                        drop(key)
                        link(dve.tensor_tensor(v, v, rtmp[:, 0, :], ALU.add))
                        done("rope_out", ("qk", layer, name))

                dve.wait_ge(*full(("gbc", layer, 0, seqs - 1, 1)))
                for names, others in ((("dq0", "dq1"), ("cq0", "cq1")), (("dk0",), ("ck0",))):
                    for i, name in enumerate(names):
                        n = n_tok if name[1] == "q" else 2 * SEQ
                        key = ("qss", layer, name)
                        dve.wait_ge(*full(key))
                        link(dve.tensor_scalar(qvar[:, i, 0:n], bank_of(key)[:, 0:n], 1.0 / HD, EPS, ALU.mult, ALU.add))
                        drop(key)
                        done("ssq", ("qk", layer, name))
                    for i, name in enumerate(names):
                        n = n_tok if name[1] == "q" else 2 * SEQ
                        dve.wait_ge(*after("rstd", ("qk", layer, name)))
                        link(dve.reciprocal(qvar[:, i, 0:n], qvar[:, i, 0:n]))
                        v = qk[:, QK_AT[name], 0:n]
                        link(dve.scalar_tensor_tensor(v, v, col("qn" if name[1] == "q" else "kn", layer), qvar[:, i, 0:n], ALU.mult, ALU.mult))
                        done("rms", ("qk", layer, name))
                    rotate(others)
                rotate(("dq0", "dq1", "dk0"))
                for tp in range(seqs):
                    key = ("u", layer, tp)
                    dve.wait_ge(*full(key))
                    for t in range(2):
                        link(dve.bn_stats(stats[:, 2 * tp + t, 0, :], bank_of(key)[:, 256 * t:256 * t + 256]))
                        link(dve.bn_aggr(mv[:, 2 * tp + t, :], stats[:, 2 * tp + t, 0, :]))
                dve.tensor_scalar(mv[:, 0:len(tiles), 1], mv[:, 0:len(tiles), 1], EPS, None, ALU.add).then_inc(*signal("uvar", layer))
                dve.wait_ge(*after("rstd", ("u", layer)))
                link(dve.reciprocal(rstd[:, 0:len(tiles)], std[:, 0:len(tiles)]))
                for tp in range(seqs):
                    key = ("u", layer, tp)
                    for t in range(2):
                        tt = 2 * tp + t
                        ins = dve.tensor_scalar(u_rows[:, tt, :], bank_of(key)[:, 256 * t:256 * t + 256], mv[:, tt, 0:1], rstd[:, tt:tt + 1],
                                                ALU.subtract, ALU.mult)
                    link(ins)
                    drop(key)
                    done("u_norm", (layer, tp))
                attend(block2_units(layer))
                dve.wait_ge(*after("gates_bc", (layer, 0)))
                n = 0
                for nb in range(2):
                    for t in tiles:
                        key = ("out2", layer, nb, "out", t)
                        dve.wait_ge(*full(key))
                        link(dve.tensor_tensor(btmp[:, n % 2, :], bank_of(key)[:, :], g_row[:, t // 2, 512 * nb:512 * nb + 512], ALU.mult))
                        drop(key)
                        xs = x[:, t, 512 * nb:512 * nb + 512]
                        link(dve.tensor_tensor(xs, xs, btmp[:, n % 2, :], ALU.add))
                        n += 1
                        if nb:
                            done("x2", (layer, 0, t))
                norm_rows(layer, 1, tiles)
                hidden_T(layer, 1, seqs)
                L = len(tiles)
                wide = [P, seqs, T2, NE]
                key = ("logits", layer)
                dve.wait_ge(*full(key))
                lg = bank_of(key)[:, 0:NE * L].rearrange("p (s t e) -> p s t e", s=seqs, t=T2)
                peak, total = (lmax[:, i, 0:L].rearrange("p (s t) -> p s t", s=seqs) for i in range(2))
                link(dve.tensor_reduce(peak, lg, AX.X, ALU.max))
                link(dve.tensor_tensor(aff_of(seqs), lg, peak.unsqueeze(3).to_broadcast(wide), ALU.subtract))
                drop(key)
                done("logit_max", layer)
                dve.wait_ge(*after("aff_exp", layer))
                link(dve.tensor_reduce(peak, aff_of(seqs), AX.X, ALU.add))
                link(dve.reciprocal(total, peak))
                dve.tensor_tensor(aff_of(seqs), aff_of(seqs), total.unsqueeze(3).to_broadcast(wide), ALU.mult)\
                   .then_inc(*signal("aff", layer))
                R = 32 * (seqs - 1) + NE
                key = ("affT", layer)
                dve.wait_ge(*full(key))
                link(dve.memset(ones_row[0:R, :], 1.0))
                link(dve.tensor_copy(left[0:R, :], bank_of(key)[0:R, 0:SEQ]))
                drop(key)
                for _ in range(CAP // 8):
                    link(dve.max(top8[0:R, :], left[0:R, :]))
                    link(dve.match_replace(left[0:R, :], top8[0:R, :], left[0:R, :], -1.0))
                link(dve.tensor_scalar(left[0:R, :], left[0:R, :], 0.0, None, ALU.is_lt))
                link(dve.tensor_tensor_scan(affT[0:R, :], ones_row[0:R, :], left[0:R, :], 0.0, ALU.mult, ALU.add))
                link(dve.tensor_tensor(picked[0:R, :], affT[0:R, :], left[0:R, :], ALU.mult))
                done("top", layer)
                key = ("posT", layer)
                dve.wait_ge(*full(key))
                link(dve.tensor_copy(posT[:, :, :, :].rearrange("p t s e -> p t (s e)")[:, :, 0:R],
                                     bank_of(key)[:, 0:P].rearrange("p (t r) -> p t r", t=T2)[:, :, 0:R]))
                drop(key)

                m, G = M[layer], experts_per_group(layer)
                W, n_sum = P // G, 2 * L
                dve.wait_ge(*after("cleared", layer))
                dve.sem_inc(m["hid"], 2)
                dve.sem_inc(m["sum_free"], n_sum)
                with dve.Fori(0, NE // G) as i:
                    for s in range(seqs):
                        ts = slice(2 * s, 2 * s + 2)
                        full4 = [P, 2, G, CAP]
                        pos = posT[:, :, s, bass.ds(i * G, G)].unsqueeze(3).to_broadcast(full4)
                        gts = aff[:, :, s, bass.ds(i * G, G)].unsqueeze(3).to_broadcast(full4)
                        it = con("iota").unsqueeze(1).unsqueeze(1).to_broadcast(full4)
                        one = moe_pick[:, ts, :].rearrange("p t (e s k) -> p t e s k", e=G, s=seqs)[:, :, :, s, :]
                        oneg = moe_pick_g[:, ts, :].rearrange("p t (e s k) -> p t e s k", e=G, s=seqs)[:, :, :, s, :]
                        dve.tensor_tensor(one, pos, it, ALU.is_equal).then_inc(m["one"], 1)
                        dve.wait_ge(m["one"], seqs * i + s + 1)
                        ins = dve.tensor_tensor(oneg, one, gts, ALU.mult)
                    ins.then_inc(m["pick"], 1)
                    for h in range(2):
                        dve.wait_ge(m["xg_full"], 2 * i + h + 1)
                        for s in range(seqs):
                            shape = [P, 4, G, CAP]
                            src = bank[4 + h][:, :].rearrange("p (c e s k) -> p c e s k", c=4, e=G, s=seqs)[:, :, :, s, :]
                            tmp, dst = (v[:, 4 * h:4 * h + 4, :].rearrange("p c (e s k) -> p c e s k", e=G, s=seqs)[:, :, :, s, :] for v in (moe_tmp, moe_x))
                            a = gain[:, 1, 4 * h:4 * h + 4, s:s + 1].unsqueeze(3).to_broadcast(shape)
                            b = shift(layer, 1)[:, 4 * h:4 * h + 4, s:s + 1].unsqueeze(3).to_broadcast(shape)
                            dve.tensor_tensor(tmp, src, a, ALU.mult).then_inc(m["one2"], 1)
                            dve.wait_ge(m["one2"], 2 * seqs * i + seqs * h + s + 1)
                            ins = dve.tensor_tensor(dst, tmp, b, ALU.add)
                    ins.then_inc(m["xt"], 1)
                    for nb in range(2):
                        dve.wait_ge(m["silu"], 2 * i + nb + 1)
                        dve.wait_ge(m["blocks"], 6 * i + 2 * nb + 2)
                        dve.tensor_tensor(moe_h[:, 512 * nb:512 * nb + 512], bank[2 * nb + 1][:, :], moe_silu[:, nb, :], ALU.mult)\
                           .then_inc(m["hid"], 1)
                    for n in range(n_sum):
                        dve.wait_ge(m["sum_full"], n_sum * i + n + 1)
                        dve.tensor_tensor(acc[:, n, :], acc[:, n, :], bank[6 + n % 2][:, :], ALU.add).then_inc(m["sum_free"], 1)
                dve.wait_ge(*after("gates_bc", (layer, 1)))
                dve.wait_ge(m["sum_free"], n_sum * (NE // G + 1))
                for t in tiles:
                    a = acc[:, 2 * t:2 * t + 2, :].rearrange("p a b -> p (a b)")
                    link(dve.tensor_tensor(a, a, g_row[:, t // 2, :], ALU.mult))
                    dve.tensor_tensor(x[:, t, :], x[:, t, :], a, ALU.add).then_inc(*signal("x2", (layer, 1, t)))
                dve.wait_ge(*after("x2", (layer, 1, tiles[-1])))
            norm_rows("final", 0, range(T2))
            dve.wait_ge(*after("final_row_in", 0))
            for t in range(T2):
                dve.scalar_tensor_tensor(x[:, t, :], x[:, t, :], rstd[:, t:t + 1], g_row[:, 1, :], ALU.mult, ALU.mult)\
                   .then_inc(*signal("x_ready", ("final", t)))
    return marks.seen


def consts():
    c = np.zeros((P, NCONST), np.float32)

    def put(name, v):
        at, n = CONSTS[name]
        c[:v.shape[0], at:at + n] = v.reshape(v.shape[0], n)
    p = np.arange(P)
    put("ident", np.eye(P, dtype=np.float32))
    for name, r in (("rot32", 32), ("rot16", 16)):
        m = np.zeros((P, P), np.float32)
        lo = p[(p // r) % 2 == 0]
        m[lo + r, lo] = -1.0
        m[lo, lo + r] = 1.0
        put(name, m)
    put("blk64", (p[:, None] // 64 == p[None] // 64).astype(np.float32))
    put("ones", np.ones((P, P), np.float32))
    pos = np.arange(SEQ, dtype=np.float32)
    inv = np.float32(10000.0) ** (-np.arange(0, 64, 2, dtype=np.float32) / np.float32(64))
    ang = (pos[:, None] * inv[None]).astype(np.float32)
    ang = np.concatenate([ang, ang, ang, ang], 1).T
    put("cos1", np.cos(ang))
    put("sin1", np.sin(ang))
    inv = np.float32(10000.0) ** (-np.arange(16, dtype=np.float32) / np.float32(16))
    ar = (pos // GRID_W)[:, None] * inv
    ac = (pos % GRID_W)[:, None] * inv
    ang = np.concatenate([ar, ar, ac, ac] * 2, 1).astype(np.float32).T
    put("cos2", np.cos(ang))
    put("sin2", np.sin(ang))
    q, k = np.arange(SEQ).reshape(T2, P).T[:, :, None], np.arange(SEQ)[None, None]
    put("mlmask", np.stack([np.where(k <= q, 0, NEG), np.where(k >= q, 0, NEG)], 1).astype(np.float32))
    put("winmask", np.where(abs(q - k) <= 128, 0, NEG).astype(np.float32))
    start = np.clip(p % GRID_W - NA_COLS // 2, 0, GRID_W - NA_COLS)[:, None]
    kc = np.arange(GRID_W)[None]
    put("namask", np.where((kc >= start) & (kc < start + NA_COLS), 0, NEG).astype(np.float32))
    put("iota", np.tile(np.arange(1, 33, dtype=np.float32), (P, 1)))
    put("sel4", np.repeat(np.eye(4, dtype=np.float32), P, 1))
    return c


WEIGHTS = ("x", "mem", "even_w_in", "even_w_out", "odd_w_in", "odd_lambda", "odd_w_out", "mem_wq", "mem_wkv", "mem_wo",
           "ffn_w_gu", "ffn_w_down", "ln_g", "ln_b", "ctx_2", "ada_w_2", "w_in_2", "sink_2", "w_out_2", "router_w_2",
           "w_gate_2", "w_up_2", "w_down_2", "final_g_2")


def layout(a):
    def chunks(v):
        v = np.asarray(v)
        v = v.reshape(v.shape[:-1] + (-1, P))
        return np.moveaxis(v, -1, 0).reshape(P, -1)
    parts = {
        "conv": chunks(a["even_conv_w"][0]), "subln": chunks(a["odd_subln_g"]),
        "n1": chunks(a["norm1_g_2"]), "n2": chunks(a["norm2_g_2"]),
        "cc": np.stack([chunks(a["c_2"][0]), chunks(a["c_ctx_2"])], -1).reshape(P, 16),
        "conv_a": chunks(a["conv_a_w_2"]), "conv_b": chunks(a["conv_b_w_2"]), "conv_bb": chunks(a["conv_b_b_2"]),
        "cln_g": chunks(a["conv_ln_g_2"]), "cln_b": chunks(a["conv_ln_b_2"]),
        "qn": np.tile(a["q_norm_g_2"], (1, 2)).T, "kn": np.tile(a["k_norm_g_2"], (1, 2)).T,
        "ada_b": chunks(a["ada_b_2"]),
    }
    first = NA_ROWS - ROWS
    rpb = np.pad(np.asarray(a["even_rpb"][0])[:, first:first + 2 * ROWS - 1], ((0, 0), (0, 0), (GRID_W - NA_COLS, GRID_W - NA_COLS)))
    windows = np.stack([rpb[:, :, GRID_W - 1 - q:2 * GRID_W - 1 - q] for q in range(GRID_W)])
    return {"cols": np.ascontiguousarray(np.concatenate([parts[k] for k in COLS], 1)),
            "gate_b": np.ascontiguousarray(np.asarray(a["even_gate_b"]).reshape(4, 4).T),
            "rpb_windows": windows, "consts": consts()}


def program(nc, shapes, table, stop=None):
    w = {n: nc.dram_tensor(f"in_{n}", s, F32, kind="ExternalInput").ap() for n, s in shapes.items()}
    out = nc.dram_tensor("out", (1, SEQ, D), F32, kind="ExternalOutput").ap()
    return build(nc, w, out, table, stop)


def kernel(stop=None, **inputs):
    import concourse.bacc as bacc
    from concourse.bass_utils import run_bass_kernel_spmd
    arrays = {n: np.ascontiguousarray(inputs[n]) for n in WEIGHTS}
    arrays.update(layout(inputs))
    shapes = {n: v.shape for n, v in arrays.items()}
    table = program(bacc.Bacc("TRN2", target_bir_lowering=False, num_devices=1), shapes, None, stop)
    nc = bacc.Bacc("TRN2", target_bir_lowering=False, num_devices=1)
    program(nc, shapes, table, stop)
    r = run_bass_kernel_spmd(nc, [{f"in_{n}": v for n, v in arrays.items()}], core_ids=[0])
    return r.results[0]["out"]
```
